# Optimizing a Trainium2 kernel written in Bass

```python
import jax
import jax.numpy as jnp
from jax import lax
import numpy as np

D_MODEL = 1024
BATCH = 1
SEQ = 1024
DEPTH = 2
DEC_BATCH = 8
DEC_SEQ = 1
PAST_LEN = 2048
PAGE_SIZE = 128

N_A = (DEPTH + 1) // 2
N_B = DEPTH - N_A
A_HEADS = 4
A_INNER = D_MODEL
A_HDIM = A_INNER // A_HEADS
CONV_W = 4
A_CHUNK = 128
B_GROUPS = ((128, 1), (512, 4), (2048, 16))
N_GROUPS = len(B_GROUPS)
B_HEADS = 4
B_HDIM = D_MODEL // 8
B_WIDTH = B_HEADS * B_HDIM
B_BLOCK = 128
N_MEM = 256
M_HEADS = 4
M_HDIM = D_MODEL // 8
M_WIDTH = M_HEADS * M_HDIM
ROPE_THETA = 10000.0
EPS = 1e-6
A_IN = 3 * A_INNER + 2 * M_WIDTH
B_IN = N_GROUPS * B_WIDTH + B_WIDTH + 2 * M_WIDTH
KV_B = N_GROUPS * 2 * B_WIDTH

kernel_name = 'yoco_mlstm_dilated_attn_step'

def _rmsnorm(x, g):
    xf = x.astype(jnp.float32)
    y = xf * lax.rsqrt(jnp.mean(xf * xf, axis=-1, keepdims=True) + EPS)
    return (y * g.astype(jnp.float32)).astype(x.dtype)

def _rope(x, pos):
    dh = x.shape[-1]
    half = dh // 2
    inv = ROPE_THETA ** (-jnp.arange(half, dtype=jnp.float32) / half)
    ang = pos[:, None] * inv[None, :]
    shape = (pos.shape[0],) + (1,) * (x.ndim - 3) + (half,)
    cos = jnp.cos(ang).reshape(shape)
    sin = jnp.sin(ang).reshape(shape)
    xf = x.astype(jnp.float32)
    x1, x2 = xf[..., :half], xf[..., half:]
    return jnp.concatenate([x1 * cos - x2 * sin, x1 * sin + x2 * cos], axis=-1).astype(x.dtype)

def _mem_attention(q, mk, mv):
    s = jnp.einsum('bthd,bnhd->bhtn', q, mk).astype(jnp.float32) * (q.shape[-1] ** -0.5)
    p = jax.nn.softmax(s, axis=-1).astype(mv.dtype)
    return jnp.einsum('bhtn,bnhd->bthd', p, mv)

def _masked_softmax_stats(s, mask):
    s = jnp.where(mask, s, -jnp.inf)
    mx = jnp.max(s, axis=-1, keepdims=True)
    p = jnp.exp(s - mx)
    l = jnp.sum(p, axis=-1, keepdims=True)
    return p / l, (mx + jnp.log(l))[..., 0]

def _dilated_prompt(q, k, v, d, nk):
    B, S, H, dh = q.shape
    ls = S // d
    blk = min(B_BLOCK, ls)
    nblk = -(-ls // blk)
    lp = nblk * blk
    nprev = -(-nk // blk)
    n = B * d

    def sub(a):
        a = a.reshape(B, ls, d, H, dh).transpose(0, 2, 1, 3, 4).reshape(n, ls, H, dh)
        return jnp.pad(a, ((0, 0), (0, lp - ls), (0, 0), (0, 0)))

    def band(a):
        ab = jnp.pad(a.reshape(n, nblk, blk, H, dh), ((0, 0), (nprev, 0), (0, 0), (0, 0), (0, 0)))
        return jnp.concatenate([ab[:, j:j + nblk] for j in range(nprev + 1)], axis=2)

    qb = sub(q).reshape(n, nblk, blk, H, dh)
    kw = band(sub(k))
    vw = band(sub(v))
    wk = (nprev + 1) * blk
    bi = jnp.arange(nblk)[:, None, None]
    qpos = bi * blk + jnp.arange(blk)[None, :, None]
    kpos = bi * blk - nprev * blk + jnp.arange(wk)[None, None, :]
    rel = qpos - kpos
    mask = (rel >= 0) & (rel <= nk) & (kpos >= 0)
    s = jnp.einsum('nbqhd,nbkhd->nbhqk', qb, kw).astype(jnp.float32) * (dh ** -0.5)
    pr, lse = _masked_softmax_stats(s, mask[None, :, None])
    o = jnp.einsum('nbhqk,nbkhd->nbqhd', pr.astype(v.dtype), vw)
    o = o.reshape(n, lp, H, dh)[:, :ls]
    lse = lse.transpose(0, 1, 3, 2).reshape(n, lp, H)[:, :ls]
    o = o.reshape(B, d, ls, H, dh).transpose(0, 2, 1, 3, 4).reshape(B, S, H, dh)
    lse = lse.reshape(B, d, ls, H).transpose(0, 2, 1, 3).reshape(B, S, H)
    return o, lse

def _dilated_decode(q, kbuf, vbuf, kn, vn, d, nk):
    wb = kbuf.shape[1]
    T = q.shape[1]
    kall = jnp.concatenate([kbuf.astype(kn.dtype), kn], axis=1)
    vall = jnp.concatenate([vbuf.astype(vn.dtype), vn], axis=1)
    idx = wb + jnp.arange(T)[:, None] - d * jnp.arange(nk + 1)[None, :]
    valid = idx >= 0
    idx = jnp.maximum(idx, 0)
    kg = kall[:, idx]
    vg = vall[:, idx]
    s = jnp.einsum('bthd,btmhd->bhtm', q, kg).astype(jnp.float32) * (q.shape[-1] ** -0.5)
    pr, lse = _masked_softmax_stats(s, valid[None, None])
    o = jnp.einsum('bhtm,btmhd->bthd', pr.astype(vg.dtype), vg)
    return o, lse.transpose(0, 2, 1)

def _mlstm_chunk_step(carry, inp):
    C, n, m = carry
    q, k, v, li, lf = inp
    L = q.shape[2]
    b = jnp.cumsum(lf, axis=-1)
    causal = jnp.tril(jnp.ones((L, L), dtype=bool))
    dmat = jnp.where(causal, b[..., :, None] - b[..., None, :] + li[..., None, :], -jnp.inf)
    inter = b + m[..., None]
    m_row = jnp.maximum(inter, jnp.max(dmat, axis=-1))
    sc = jnp.einsum('bhtd,bhsd->bhts', q, k) * jnp.exp(dmat - m_row[..., None])
    dec = jnp.exp(inter - m_row)
    num = jnp.einsum('bhts,bhsv->bhtv', sc, v) + dec[..., None] * jnp.einsum('bhvk,bhtk->bhtv', C, q)
    den = jnp.sum(sc, axis=-1) + dec * jnp.einsum('bhk,bhtk->bht', n, q)
    h = num / jnp.maximum(jnp.abs(den), jnp.exp(-m_row))[..., None]
    b_last = b[..., -1]
    g = b_last[..., None] - b + li
    m_new = jnp.maximum(b_last + m, jnp.max(g, axis=-1))
    ws = jnp.exp(g - m_new[..., None])
    dc = jnp.exp(b_last + m - m_new)
    C_new = dc[..., None, None] * C + jnp.einsum('bhs,bhsv,bhsk->bhvk', ws, v, k)
    n_new = dc[..., None] * n + jnp.einsum('bhs,bhsk->bhk', ws, k)
    return (C_new, n_new, m_new), h

def _mlstm_branch(u, o_pre, conv_state, C0, n0, m0, conv_w, conv_b, w_q, w_k, w_v, w_if, b_if, g_hn, skip, chunk):
    B, T, _ = u.shape
    xpad = jnp.concatenate([conv_state.astype(u.dtype), u], axis=1)
    xc = conv_b.astype(u.dtype) + xpad[:, 0:T] * conv_w[0]
    for j in range(1, CONV_W):
        xc = xc + xpad[:, j:j + T] * conv_w[j]
    xc = jax.nn.silu(xc)
    new_conv = xpad[:, T:]
    xh = xc.reshape(B, T, A_HEADS, A_HDIM)
    uh = u.reshape(B, T, A_HEADS, A_HDIM)
    q = jnp.einsum('bthd,hde->bthe', xh, w_q)
    k = jnp.einsum('bthd,hde->bthe', xh, w_k) * (A_HDIM ** -0.5)
    v = jnp.einsum('bthd,hde->bthe', uh, w_v)
    gates = (jnp.concatenate([q, k, v], axis=-1).reshape(B, T, 3 * A_INNER) @ w_if + b_if).astype(jnp.float32)
    li = gates[..., :A_HEADS]
    lf = jax.nn.log_sigmoid(gates[..., A_HEADS:])
    nc = T // chunk

    def to_chunks(a):
        return a.astype(jnp.float32).reshape(B, nc, chunk, A_HEADS, A_HDIM).transpose(1, 0, 3, 2, 4)

    def gate_chunks(a):
        return a.reshape(B, nc, chunk, A_HEADS).transpose(1, 0, 3, 2)

    carry0 = (C0.astype(jnp.float32), n0.astype(jnp.float32), m0.astype(jnp.float32))
    (C1, n1, m1), hs = lax.scan(_mlstm_chunk_step, carry0,
                                (to_chunks(q), to_chunks(k), to_chunks(v), gate_chunks(li), gate_chunks(lf)))
    hs = hs.transpose(1, 0, 3, 2, 4).reshape(B, T, A_HEADS, A_HDIM)
    h = jax.nn.sigmoid(o_pre.astype(jnp.float32)).reshape(B, T, A_HEADS, A_HDIM) * hs
    mu = jnp.mean(h, axis=-1, keepdims=True)
    var = jnp.mean(jnp.square(h - mu), axis=-1, keepdims=True)
    hn = ((h - mu) * lax.rsqrt(var + EPS)).reshape(B, T, A_INNER) * g_hn.astype(jnp.float32)
    y = (hn + skip.astype(jnp.float32) * xc.astype(jnp.float32)).astype(u.dtype)
    return y, new_conv, C1, n1, m1

def _run_stack(x, pos, mem_kv, a_state, wins, chunk, p):
    B, T, _ = x.shape
    conv_l, C_l, n_l, m_l = [], [], [], []
    k_all = None
    v_all = None
    for l in range(DEPTH):
        h = _rmsnorm(x, p['g_pre'][l])
        if l < N_A:
            z = h @ p['w_in_a'][l]
            u, o_pre, zg, qm, zm = jnp.split(
                z, [A_INNER, 2 * A_INNER, 3 * A_INNER, 3 * A_INNER + M_WIDTH], axis=-1)
            ya, cs, C1, n1, m1 = _mlstm_branch(
                u, o_pre, a_state[0][l], a_state[1][l], a_state[2][l], a_state[3][l],
                p['conv_w_a'][l], p['conv_b_a'][l], p['w_q_a'][l], p['w_k_a'][l], p['w_v_a'][l],
                p['w_if_a'][l], p['b_if_a'][l], p['g_hn_a'][l], p['skip_a'][l], chunk)
            conv_l.append(cs)
            C_l.append(C1)
            n_l.append(n1)
            m_l.append(m1)
            y_mix = ya * jax.nn.silu(zg)
            w_out = p['w_out_a'][l]
        else:
            if k_all is None:
                kv = (_rmsnorm(x, p['g_kv']) @ p['w_kv_b']).reshape(B, T, N_GROUPS, 2, B_HEADS, B_HDIM)
                k_all = _rope(kv[:, :, :, 0], pos)
                v_all = kv[:, :, :, 1]
            ib = l - N_A
            z = h @ p['w_in_b'][ib]
            qd, zg, qm, zm = jnp.split(
                z, [N_GROUPS * B_WIDTH, N_GROUPS * B_WIDTH + B_WIDTH,
                    N_GROUPS * B_WIDTH + B_WIDTH + M_WIDTH], axis=-1)
            qd = _rope(qd.reshape(B, T, N_GROUPS, B_HEADS, B_HDIM), pos)
            outs, lses = [], []
            for g, (w, d) in enumerate(B_GROUPS):
                if wins is None:
                    o, lse = _dilated_prompt(qd[:, :, g], k_all[:, :, g], v_all[:, :, g], d, w // d)
                else:
                    o, lse = _dilated_decode(qd[:, :, g], wins[g][0], wins[g][1],
                                             k_all[:, :, g], v_all[:, :, g], d, w // d)
                outs.append(o)
                lses.append(lse)
            wts = jax.nn.softmax(jnp.stack(lses, axis=0), axis=0)
            ydil = jnp.einsum('gbth,gbthd->bthd', wts, jnp.stack(outs, axis=0).astype(jnp.float32))
            y_mix = ydil.reshape(B, T, B_WIDTH).astype(x.dtype) * jax.nn.silu(zg)
            w_out = p['w_out_b'][ib]
        mk = mem_kv[l, :, :, 0].astype(x.dtype)
        mv = mem_kv[l, :, :, 1].astype(x.dtype)
        ym = _mem_attention(qm.reshape(B, T, M_HEADS, M_HDIM), mk, mv).reshape(B, T, M_WIDTH) * jax.nn.silu(zm)
        out = jnp.concatenate([y_mix, ym], axis=-1) @ w_out
        x = x + _rmsnorm(out, p['g_post'][l])
    return x, (jnp.stack(conv_l), jnp.stack(C_l), jnp.stack(n_l), jnp.stack(m_l)), (k_all, v_all)

def _window_rows(k_all, v_all, g, n_rows):
    T = k_all.shape[1]
    return jnp.stack([k_all[:, T - n_rows:, g], v_all[:, T - n_rows:, g]], axis=2)

def setup_inputs(seed: int = 0) -> dict:
    key = jax.random.key(seed)
    ks = iter(list(jax.random.split(key, 40)))

    def nrm(shape, scale):
        return jax.random.normal(next(ks), shape, jnp.float32) * scale

    b_if_a = jnp.concatenate(
        [nrm((N_A, A_HEADS), 0.1),
         jnp.linspace(3.0, 6.0, A_HEADS, dtype=jnp.float32)[None, :] + nrm((N_A, A_HEADS), 0.01)], axis=-1)
    return {
        'x_prompt': nrm((BATCH, SEQ, D_MODEL), 1.0),
        'x_sample': nrm((DEC_BATCH, DEC_SEQ, D_MODEL), 1.0),
        'mem_prompt': nrm((BATCH, N_MEM, D_MODEL), 1.0),
        'state_conv': nrm((N_A, DEC_BATCH, CONV_W - 1, A_INNER), 1.0),
        'state_C': nrm((N_A, DEC_BATCH, A_HEADS, A_HDIM, A_HDIM), 0.1),
        'state_n': nrm((N_A, DEC_BATCH, A_HEADS, A_HDIM), 0.5),
        'state_m': nrm((N_A, DEC_BATCH, A_HEADS), 0.5),
        'cache_win0': nrm((DEC_BATCH, min(B_GROUPS[0][0], PAST_LEN), 2, B_HEADS, B_HDIM), 1.0),
        'cache_win1': nrm((DEC_BATCH, min(B_GROUPS[1][0], PAST_LEN), 2, B_HEADS, B_HDIM), 1.0),
        'cache_win2': nrm((DEC_BATCH, min(B_GROUPS[2][0], PAST_LEN), 2, B_HEADS, B_HDIM), 1.0),
        'cache_mem_kv': nrm((DEPTH, DEC_BATCH, N_MEM, 2, M_HEADS, M_HDIM), 1.0),
        'g_pre': 1.0 + nrm((DEPTH, D_MODEL), 0.01),
        'g_post': 1.0 + nrm((DEPTH, D_MODEL), 0.01),
        'w_in_a': nrm((N_A, D_MODEL, A_IN), D_MODEL ** -0.5),
        'conv_w_a': nrm((N_A, CONV_W, A_INNER), CONV_W ** -0.5),
        'conv_b_a': nrm((N_A, A_INNER), 0.01),
        'w_q_a': nrm((N_A, A_HEADS, A_HDIM, A_HDIM), A_HDIM ** -0.5),
        'w_k_a': nrm((N_A, A_HEADS, A_HDIM, A_HDIM), A_HDIM ** -0.5),
        'w_v_a': nrm((N_A, A_HEADS, A_HDIM, A_HDIM), A_HDIM ** -0.5),
        'w_if_a': nrm((N_A, 3 * A_INNER, 2 * A_HEADS), (3 * A_INNER) ** -0.5),
        'b_if_a': b_if_a,
        'g_hn_a': 1.0 + nrm((N_A, A_INNER), 0.01),
        'skip_a': 1.0 + nrm((N_A, A_INNER), 0.01),
        'w_out_a': nrm((N_A, A_INNER + M_WIDTH, D_MODEL), (A_INNER + M_WIDTH) ** -0.5),
        'g_kv': 1.0 + nrm((D_MODEL,), 0.01),
        'w_kv_b': nrm((D_MODEL, KV_B), D_MODEL ** -0.5),
        'w_in_b': nrm((N_B, D_MODEL, B_IN), D_MODEL ** -0.5),
        'w_out_b': nrm((N_B, B_WIDTH + M_WIDTH, D_MODEL), (B_WIDTH + M_WIDTH) ** -0.5),
        'w_mkv': nrm((DEPTH, D_MODEL, 2 * M_WIDTH), D_MODEL ** -0.5),
    }

def reference(x_prompt, x_sample, mem_prompt, state_conv, state_C, state_n, state_m,
              cache_win0, cache_win1, cache_win2, cache_mem_kv,
              g_pre, g_post, w_in_a, conv_w_a, conv_b_a, w_q_a, w_k_a, w_v_a, w_if_a, b_if_a,
              g_hn_a, skip_a, w_out_a, g_kv, w_kv_b, w_in_b, w_out_b, w_mkv):
    p = {'g_pre': g_pre, 'g_post': g_post, 'w_in_a': w_in_a, 'conv_w_a': conv_w_a, 'conv_b_a': conv_b_a,
         'w_q_a': w_q_a, 'w_k_a': w_k_a, 'w_v_a': w_v_a, 'w_if_a': w_if_a, 'b_if_a': b_if_a,
         'g_hn_a': g_hn_a, 'skip_a': skip_a, 'w_out_a': w_out_a, 'g_kv': g_kv, 'w_kv_b': w_kv_b,
         'w_in_b': w_in_b, 'w_out_b': w_out_b}
    bp, tp = x_prompt.shape[0], x_prompt.shape[1]
    ts = x_sample.shape[1]

    memkv_p = jnp.einsum('bnd,lde->lbne', mem_prompt, w_mkv).reshape(DEPTH, bp, N_MEM, 2, M_HEADS, M_HDIM)
    pos_p = jnp.arange(tp, dtype=jnp.float32)
    a0 = (jnp.zeros((N_A, bp, CONV_W - 1, A_INNER), x_prompt.dtype),
          jnp.zeros((N_A, bp, A_HEADS, A_HDIM, A_HDIM), jnp.float32),
          jnp.zeros((N_A, bp, A_HEADS, A_HDIM), jnp.float32),
          jnp.zeros((N_A, bp, A_HEADS), jnp.float32))
    y_prompt, (conv_p, C_p, n_p, m_p), (k_p, v_p) = _run_stack(
        x_prompt, pos_p, memkv_p, a0, None, min(A_CHUNK, tp), p)
    win0_p = _window_rows(k_p, v_p, 0, min(B_GROUPS[0][0], tp))
    win1_p = _window_rows(k_p, v_p, 1, min(B_GROUPS[1][0], tp))
    win2_p = _window_rows(k_p, v_p, 2, min(B_GROUPS[2][0], tp))

    pos_s = PAST_LEN + jnp.arange(ts, dtype=jnp.float32)
    wins = ((cache_win0[:, :, 0], cache_win0[:, :, 1]),
            (cache_win1[:, :, 0], cache_win1[:, :, 1]),
            (cache_win2[:, :, 0], cache_win2[:, :, 1]))
    y_sample, (conv_s, C_s, n_s, m_s), (k_s, v_s) = _run_stack(
        x_sample, pos_s, cache_mem_kv, (state_conv, state_C, state_n, state_m), wins, ts, p)
    conv_s = conv_s.astype(state_conv.dtype)
    C_s = C_s.astype(state_C.dtype)
    n_s = n_s.astype(state_n.dtype)
    m_s = m_s.astype(state_m.dtype)
    win0_s = _window_rows(k_s, v_s, 0, ts)
    win1_s = _window_rows(k_s, v_s, 1, ts)
    win2_s = _window_rows(k_s, v_s, 2, ts)
    return (y_prompt, y_sample, conv_p, C_p, n_p, m_p, win0_p, win1_p, win2_p, memkv_p,
            conv_s, C_s, n_s, m_s, win0_s, win1_s, win2_s)


_drawn_inputs = setup_inputs


def setup_inputs(seed=0):
    import zlib

    import numpy as np

    out = dict(_drawn_inputs(seed))
    spreads = {}
    factors = {'g_pre': 2.769,
     'g_post': 5.153,
     'g_hn_a': 23.375,
     'skip_a': 8.0,
     'g_kv': 5.431,
     'cache_win0': 2.95,
     'cache_win1': 8.0,
     'cache_win2': 8.0}
    for name, (base, spread) in spreads.items():
        noise = np.random.default_rng([zlib.crc32(name.encode()), seed]).standard_normal(out[name].shape)
        drawn = base * np.exp(spread * noise) if base else spread * noise
        out[name] = jnp.asarray(drawn.astype(out[name].dtype))
    for name, factor in factors.items():
        out[name] = (out[name] * factor).astype(out[name].dtype)
    return out
```

```python
from contextlib import ExitStack

import concourse.bass as bass
from concourse import mybir

F32 = mybir.dt.float32
BF16 = mybir.dt.bfloat16
ALU = mybir.AluOpType
ACT = mybir.ActivationFunctionType
AX = mybir.AxisListType

P = 128
T = 1024
NS = 8
W = T + NS
SEG = W // 3
D = 1024
KT = D // P
H = 4
HP = H * NS
CH = 128
NCH = T // CH
NMEM = 256
EPS = 1e-6
SCALE = 128 ** -0.5
STRIDES = (1, 4, 16)
NEG = -1e30

ROW_STATE, ROW_CW, ROW_CB, ROW_GPRE, ROW_GPOST, ROW_GHN, ROW_SKIP, ROW_GKV, NROW = 0, 24, 28, 29, 31, 33, 34, 35, 36

C_ID, C_ONE, C_AVG_D, C_AVG_H, C_CAUSAL, C_SEL = 0, 128, 256, 384, 512, 640
C_END = C_SEL + H * P
M_ID, M_BAND, M_PAIR, M_END = 0, 128, 640, 896


class Signal:

    def __init__(self, sem):
        self.sem, self.n = sem, 0

    def up(self, by=1):
        self.n += by
        return self.sem


def build(nc, a, o):
    with ExitStack() as ctx:
        def sb(name, shape, dt=F32):
            return ctx.enter_context(nc.sbuf_tensor(name, shape, dt))

        signals = {}

        def sig(name):
            if name not in signals:
                signals[name] = Signal(ctx.enter_context(nc.semaphore(name)))
            return signals[name]

        HT = sb("HT", [P, KT * W])
        BIG = sb("BIG", [P, 24 * W])
        WT = 1040
        WK = sb("WK", [P, 8 * WT])
        SLOT = 1536
        NSLOT = 3
        RING = sb("RING", [P, NSLOT * SLOT])
        TRIG = sb("TRIG", [P, 2 * W])
        CST = sb("CST", [P, C_END])
        VEC = sb("VEC", [P, KT, NROW])
        XTRA = sb("XTRA", [P, NCH * 3 * CH])
        RR = XTRA[0:H, :].rearrange("h (c x t) -> h c x t", c=NCH, x=3)
        MASKF = XTRA[:, 0:M_END]
        BFC = XTRA[:, M_END:M_END + M_END // 2].bitcast(BF16)
        KVS = XTRA[:, 1408:1600].rearrange("p (g x n) -> p g x n", g=3, x=2)
        SM = sb("SM", [P, 360])
        PS = ctx.enter_context(nc.psum_tensor("PS", [P, 8, 512], F32))

        def dram(name, shape):
            return nc.dram_tensor(name, shape, F32, kind="Internal").ap()

        xt_d = dram("xt_scratch", [KT, P, W])
        xc_d = dram("xc_scratch", [KT, P, W])
        sg_d = dram("sample_gates", [2, H, NS])
        qw_d = dram("sample_q_and_weighted_k", [HP, 512])
        cf_d = dram("sample_coef", [HP, 3])
        qs_d = dram("sample_query", [5, HP, P])
        ls_d = dram("window_lse", [3, 8, H, P])

        ident = CST[:, C_ID:C_ID + P]
        ones = CST[:, C_ONE:C_ONE + P]
        avg_d = CST[:, C_AVG_D:C_AVG_D + P]
        avg_h = CST[:, C_AVG_H:C_AVG_H + P]
        causal = CST[:, C_CAUSAL:C_CAUSAL + P]

        def big(i, lo=0, hi=W):
            return BIG[:, i * W + lo:i * W + hi]

        def ht(i, lo=0, hi=W):
            return HT[:, i * W + lo:i * W + hi]

        def wk(i, lo=0, hi=W):
            return WK[:, i * WT + lo:i * WT + hi]

        def seg3(ap):
            return ap.rearrange("p (b n) -> p b n", b=3)

        def vec(row, kt):
            return VEC[:, kt, row:row + 1]

        QKVN = XTRA[64:96, 0:768]
        SN, TMP32, WK32, NN32 = (XTRA[64:96, at:at + 256] for at in (768, 1024, 1280, 1536))
        SC32 = XTRA[64:96, 1792:1824]

        SQC = WK[:, 7 * WT:7 * WT + 6 * HP].rearrange("p (i h b) -> p i h b", i=6, h=H)

        ACOL = SM[:, 0:32].rearrange("p (c h) -> p c h", h=H)
        UT = SM[:, 32:120].rearrange("p (j n) -> p j n", n=11)
        MPV = SM[0:H, 120:129]
        BIAS = SM[0:H, 129:131]
        EPSC = SM[:, 131:132]
        COEF = SM[:, 132:132 + 96].rearrange("p (i k) -> p i k", k=3)
        CQ = SM[:, 228:292].rearrange("p (v i) -> p v i", v=2)
        HSS = SM[:, 312:344]

        jobs, items = [], []

        def job(name, reader="act"):
            jobs.append((name, reader))

        def item(name, loads, scale_row=None, release=None, kts=KT):
            items.append(dict(name=name, loads=loads, scale=scale_row, release=release, kts=kts))

        def tile_of(w, n0, kts=KT):
            return w[:, n0:n0 + P].rearrange("(k p) n -> p k n", p=P), kts * P

        def proj(name, w, n0, scale_row=None, reader="act", kts=KT):
            job(name, reader)
            item(name, [tile_of(w, n0, kts)], scale_row, ("job", name), kts)

        w_in_a, w_in_b, w_kv = a["w_in_a"][0], a["w_in_b"][0], a["w_kv_b"]
        for ft in range(KT):
            job(f"xt{ft}")
        for l in range(2):
            for kt in range(KT):
                item(f"mkv{l}_{kt}", [(a["w_mkv"][l][kt * P:(kt + 1) * P, :], D)], None, ("mkv", l * KT + kt + 1))
        job("norm0")

        def qkv_jobs(h):
            item(f"qkv{h}", [(a[w][0, h].rearrange("(k p) n -> p k n", p=P), 512) for w in ("w_q_a", "w_k_a", "w_v_a")],
                 None, ("job", f"v{h}_1"))
            for x in "qkv":
                for e in range(2):
                    job(f"{x}{h}_{e}")

        def u_jobs(h):
            for e in range(2):
                proj(f"u{2 * h + e}", w_in_a, (2 * h + e) * P, ROW_GPRE)

        u_jobs(0)
        for h in range(H):
            if h + 1 < H:
                u_jobs(h + 1)
            qkv_jobs(h)
        job("gates")
        job("acol")
        job("rows_u")
        job("rows_s")

        def oz_jobs(h, first, part):
            for e in range(2):
                proj(f"{part}{h}_{e}", w_in_a, first + (2 * h + e) * P, ROW_GPRE)

        for h in range(H):
            oz_jobs(h, D, "o")
            if h > 0:
                job(f"var{h - 1}")
            oz_jobs(h, 2 * D, "zg")
            job(f"mean{h}", "dve")
        job("var3")
        for h in range(H):
            proj(f"qmA{h}", w_in_a, 3 * D + h * P, ROW_GPRE)
        for h in range(H):
            proj(f"zmA{h}", w_in_a, 3 * D + (H + h) * P, ROW_GPRE)
        job("qsA")
        job("mkA")
        job("ssA"), job("spA"), job("soA", "dve")
        for n in range(KT):
            proj(f"outA{n}", a["w_out_a"][0], n * P, kts=12)
        job("postA")
        job("normB")
        for g in range(3):
            for h in range(H):
                proj(f"k{g}{h}", w_kv, (2 * g * H + h) * P, ROW_GKV, "dve")
            for h in range(H):
                proj(f"v{g}{h}", w_kv, ((2 * g + 1) * H + h) * P, ROW_GKV)
            for h in range(H):
                proj(f"q{g}{h}", w_in_b, (g * H + h) * P, ROW_GPRE + 1, "dve")
            job(f"lse{g}")
        job("qsD")
        for h in range(H):
            proj(f"zgB{h}", w_in_b, (3 * H + h) * P, ROW_GPRE + 1)
        for h in range(H):
            job(f"wb{h}_0", "dve")
            job(f"wb{h}_1", "dve")
            job(f"wb{h}_2", "dve")
        job("ssD"), job("spD"), job("soD", "dve")
        for h in range(H):
            proj(f"qmB{h}", w_in_b, (4 * H + h) * P, ROW_GPRE + 1)
        for h in range(H):
            proj(f"zmB{h}", w_in_b, (5 * H + h) * P, ROW_GPRE + 1)
        job("qsB")
        job("mkB")
        job("ssB"), job("spB"), job("soB", "dve")
        for n in range(KT):
            proj(f"outB{n}", a["w_out_b"][0], n * P)
        job("postB")
        for t in range(9):
            job(f"yt{t}")

        JOB = {name: g for g, (name, _) in enumerate(jobs)}
        ITEM = {it["name"]: n for n, it in enumerate(items)}
        job_done = sig("job_done")
        job_read = {"act": sig("job_read_by_act"), "dve": sig("job_read_by_dve")}

        def slot_of(name):
            return 3 * (JOB[name] % 2)

        def slot3(name):
            s = slot_of(name)
            return PS[:, s:s + 3, 0:SEG]

        def read_count(g):
            r = jobs[g][1]
            return r, sum(1 for _, x in jobs[:g + 1] if x == r)

        def read_of(name):
            r, n = read_count(JOB[name])
            return job_read[r].sem, n

        def slot_free(name):
            r, n = read_count(JOB[name] - 2)
            return job_read[r].sem, n

        def done(name):
            return JOB[name] + 1

        slot_loaded = [sig(f"ring{s}_loaded") for s in range(NSLOT)]
        scaled = sig("weights_scaled")
        loaded_at, n_loaded = [], [0] * NSLOT
        for n, it in enumerate(items):
            n_loaded[n % NSLOT] += 16 * len(it["loads"])
            loaded_at.append(n_loaded[n % NSLOT])
        scaled_at = [sum(1 for x in items[:n + 1] if x["scale"] is not None) for n in range(len(items))]

        def released(n):
            kind, v = items[n]["release"]
            return (job_done.sem, done(v)) if kind == "job" else (sig("memkv_steps").sem, v)

        def load_item(sp, name):
            n = ITEM[name]
            it = items[n]
            if n >= NSLOT:
                sp.wait_ge(*released(n - NSLOT))
            at = (n % NSLOT) * SLOT
            for src, size in it["loads"]:
                dst = RING[:, at:at + size]
                if len(src.shape) == 3:
                    dst = dst.rearrange("p (k n) -> p k n", k=src.shape[1])
                sp.dma_start(dst, src).then_inc(slot_loaded[n % NSLOT].sem, 16)
                at += size

        def scale_item(pool, name):
            n = ITEM[name]
            it = items[n]
            pool.wait_ge(slot_loaded[n % NSLOT].sem, loaded_at[n])
            at = (n % NSLOT) * SLOT
            w = RING[:, at:at + D].rearrange("p (k n) -> p k n", k=KT)
            g = VEC[:, :, it["scale"]:it["scale"] + 1].to_broadcast([P, KT, P])
            nc.gpsimd.tensor_tensor(w, w, g, ALU.mult).then_inc(scaled.up(), 1)

        def ring(name):
            at = (ITEM[name] % NSLOT) * SLOT
            return RING[:, at:at + SLOT]

        def weights_of(name):
            n = ITEM[name]
            if items[n]["scale"] is None:
                return slot_loaded[n % NSLOT].sem, loaded_at[n]
            return scaled.sem, scaled_at[n]

        def pe_proj(pe, name, rhs, kts=KT, before=None):
            pe.wait_ge(*slot_free(name))
            pe.wait_ge(*weights_of(name))
            w = ring(name)
            s = slot_of(name)
            for kt in range(kts):
                if before:
                    before(kt)
                for b in range(3):
                    last = nc.tensor.matmul(PS[:, s + b, 0:SEG], w[:, kt * P:(kt + 1) * P],
                                            rhs(kt, b * SEG, (b + 1) * SEG), start=(kt == 0), stop=(kt == kts - 1))
            last.then_inc(job_done.up(), 1)

        XN = BIG[:, 0:8 * D].rearrange("p (t d) -> p t d", t=8)
        MEMN = BIG[:, 8 * D:10 * D].rearrange("p (t d) -> p t d", t=2)
        XS = BIG[0:NS, 10 * D:11 * D]
        PAR = BIG[0:NROW, 11 * D:12 * D]
        MEMT = HT[:, 0:8 * NMEM].rearrange("p (k n) -> p k n", k=KT)

        def xt0(kt, lo=0, hi=W):
            return big(12 + kt, lo, hi)

        WIF = TRIG[:, 0:24 * 36].rearrange("p (i n) -> p i n", i=24)
        s_const, s_x, s_gate_w = sig("constants_loaded"), sig("inputs_loaded"), sig("gate_weights_loaded")
        s_zero = sig("pads_zeroed")
        N_X = 8 + 2 + 1 + 8

        def stage0_sp(sp):
            sp.dma_start(CST[:, :], a["c_block"]).then_inc(s_const.sem, 16)
            for t in range(8):
                sp.dma_start(XN[:, t, :], a["x_prompt"][0, t * P:(t + 1) * P, :]).then_inc(s_x.sem, 16)
            sp.dma_start(MEMN, a["mem_prompt"][0].rearrange("(t p) d -> p t d", p=P)).then_inc(s_x.sem, 16)
            sp.dma_start(XS, a["x_sample"].rearrange("b t d -> (b t) d")).then_inc(s_x.sem, 16)
            sp.dma_start(PAR[ROW_STATE:24, :], a["state_conv"].rearrange("a b r d -> (a b r) d")).then_inc(s_x.sem, 16)
            for row, n, name in ((ROW_CW, 4, "conv_w_a"), (ROW_CB, 1, "conv_b_a"), (ROW_GPRE, 2, "g_pre"),
                                 (ROW_GPOST, 2, "g_post"), (ROW_GHN, 1, "g_hn_a"), (ROW_SKIP, 1, "skip_a")):
                src = a[name]
                if len(src.shape) == 3:
                    src = src[0]
                sp.dma_start(PAR[row:row + n, :], src).then_inc(s_x.sem, 16)
            sp.dma_start(PAR[ROW_GKV:NROW, :], a["g_kv"].rearrange("(a d) -> a d", a=1)).then_inc(s_x.sem, 16)
            for i in range(2):
                sp.dma_start(BIAS[:, i:i + 1], a["b_if_a"][0, i * H:(i + 1) * H].rearrange("(h a) -> h a", a=1))\
                    .then_inc(s_x.sem, 16)
            for l in range(2):
                for kt in range(KT):
                    load_item(sp, f"mkv{l}_{kt}")
                    if l == 0 and kt == 3:
                        sp.wait_ge(s_zero.sem, 1)
                        src = a["w_if_a"][0].rearrange("(i p) n -> p i n", p=P)
                        sp.dma_start(WIF[:, :, 0:H], src[:, :, 0:H]).then_inc(s_gate_w.sem, 16)
                        sp.dma_start(WIF[:, :, 32:36], src[:, :, H:2 * H]).then_inc(s_gate_w.sem, 16)

        INPUTS = 16 * (8 + 1 + 1 + 1 + 6 + 1 + 2)

        def stage0_pool(pool):
            nc.gpsimd.memset(TRIG[:, 0:24 * 36], 0.0).then_inc(s_zero.up(), 1)
            for ub in range(4):
                nc.gpsimd.memset(wk(ub, 0, 3), 0.0).then_inc(s_zero.up(), 1)
            nc.gpsimd.memset(EPSC, EPS).then_inc(s_zero.up(), 1)

        def stage0_pe(pe):
            pe.wait_ge(s_const.sem, 16)
            pe.wait_ge(s_x.sem, INPUTS)
            for ft in range(KT):
                if ft >= 2:
                    pe.wait_ge(*slot_free(f"xt{ft}"))
                s = slot_of(f"xt{ft}")
                c = slice(ft * P, (ft + 1) * P)
                for t in range(8):
                    nc.tensor.transpose(PS[:, s + t // 4, (t % 4) * P:(t % 4 + 1) * P], XN[:, t, c], ident)
                for t in range(2):
                    nc.tensor.transpose(PS[:, s + 2, t * P:(t + 1) * P], MEMN[:, t, c], ident)
                nc.tensor.transpose(PS[:, s + 2, 256:256 + NS], XS[:, c], ident[0:NS, 0:NS])
                last = nc.tensor.transpose(PS[:, s + 2, 264:264 + NROW], PAR[:, c], ident[0:NROW, 0:NROW])
                last.then_inc(job_done.up(), 1)
            pe.wait_ge(*read_of("xt7"))
            for l in range(2):
                for kt in range(KT):
                    pe.wait_ge(*weights_of(f"mkv{l}_{kt}"))
                    w = ring(f"mkv{l}_{kt}")
                    for nt in range(2):
                        for half in range(2):
                            last = nc.tensor.matmul(PS[:, 4 * l + 2 * nt + half, :], MEMT[:, kt, nt * P:(nt + 1) * P],
                                                    w[:, half * 512:(half + 1) * 512],
                                                    start=(kt == 0), stop=(kt == KT - 1))
                    last.then_inc(sig("memkv_steps").up(), 1)
            pe.wait_ge(sig("memkv_read").sem, 4)
            norm_pe(pe, "norm0")

        def stage0_act(act):
            own = sig("xt_copied")
            for ft in range(KT):
                act.wait_ge(job_done.sem, done(f"xt{ft}"))
                s = slot_of(f"xt{ft}")
                if ft == 0:
                    act.wait_ge(s_zero.sem, 6)
                nc.scalar.activation(xt0(ft, 0, T).rearrange("p (b n) -> p b n", b=2), PS[:, s:s + 2, :], ACT.Copy)
                nc.scalar.activation(xt0(ft, T, W), PS[:, s + 2, 256:256 + NS], ACT.Copy).then_inc(own.up(), 1)
                nc.scalar.activation(MEMT[:, ft, :], PS[:, s + 2, 0:256], ACT.Copy)
                nc.scalar.activation(VEC[:, ft, :], PS[:, s + 2, 264:264 + NROW], ACT.Copy).then_inc(job_read["act"].up(), 1)
                act.wait_ge(own.sem, own.n)
                act.dma_start(xt_d[ft], xt0(ft)).then_inc(sig("xt_saved").sem, 16)
            own2 = sig("memkv_read")
            for l in range(2):
                act.wait_ge(sig("memkv_steps").sem, KT * (l + 1))
                for nt in range(2):
                    i = 2 * l + nt
                    dst = BIG[:, i * D:(i + 1) * D]
                    nc.scalar.activation(dst.rearrange("p (b n) -> p b n", b=2),
                                         PS[:, 4 * l + 2 * nt:4 * l + 2 * nt + 2, :], ACT.Copy).then_inc(own2.up(), 1)
                    act.wait_ge(own2.sem, own2.n)
                    act.dma_start(o["memkv_p"][l, 0, nt * P:(nt + 1) * P].rearrange("n a h d -> n (a h d)"), dst)\
                        .then_inc(sig("memkv_saved").sem, 16)
            norm_act(act, "norm0", xt0)

        def norm_act(act, name, src, src_ready=None):
            ready = sig(f"sq_{name}")
            for kt in range(KT):
                if kt >= 2:
                    act.wait_ge(sig(f"sq_used_{name}").sem, kt - 1)
                if src_ready:
                    src_ready(kt)
                nc.scalar.activation(wk(5 + kt % 2), src(kt), ACT.Square).then_inc(ready.up(), 1)
            act.wait_ge(job_done.sem, done(name))
            nc.scalar.activation(seg3(wk(7)), slot3(name), ACT.Sqrt, bias=EPSC).then_inc(job_read["act"].up(), 1)

        def norm_pe(pe, name):
            pe.wait_ge(*slot_free(name))
            s = slot_of(name)
            for kt in range(KT):
                pe.wait_ge(sig(f"sq_{name}").sem, kt + 1)
                for b in range(3):
                    last = nc.tensor.matmul(PS[:, s + b, 0:SEG], avg_d, wk(5 + kt % 2, b * SEG, (b + 1) * SEG),
                                            start=(kt == 0), stop=(kt == KT - 1))
                last.then_inc((sig(f"sq_used_{name}") if kt < KT - 1 else job_done).up(), 1)

        def norm_dve(dve, name):
            dve.wait_ge(*read_of(name))
            nc.vector.reciprocal(wk(7), wk(7)).then_inc(step.up(), 1)
            dve.wait_ge(step.sem, step.n)

        step = sig("vector_steps")

        def stage0_dve(dve):
            norm_dve(dve, "norm0")
            for kt in range(KT):
                nc.vector.tensor_tensor(ht(kt), xt0(kt), wk(7), ALU.mult).then_inc(sig("h_ready").up(), 1)

        def ub_of(j):
            return (j // 2 % 2) * 2 + j % 2

        def stage1_sp(sp):
            for h in range(H):
                if h == 0:
                    load_item(sp, "u0"), load_item(sp, "u1")
                if h + 1 < H:
                    load_item(sp, f"u{2 * h + 2}"), load_item(sp, f"u{2 * h + 3}")
                load_item(sp, f"qkv{h}")
            sp.dma_start(o["conv_s"][0, :, 0:2, :], a["state_conv"][0, :, 1:3, :]).then_inc(s_out.sem, 16)

        def stage1_pool(pool):
            pool.wait_ge(*read_of("xt7"))
            for j in range(8):
                scale_item(pool, f"u{j}")

        def stage1_pe(pe):
            pe.wait_ge(sig("h_ready").sem, 1)

            def u(j):
                pe_proj(pe, f"u{j}", ht, before=(lambda kt: pe.wait_ge(sig("h_ready").sem, kt + 1)) if j == 0 else None)

            u(0), u(1)
            for h in range(H):
                if h + 1 < H:
                    u(2 * h + 2), u(2 * h + 3)
                pe.wait_ge(*weights_of(f"qkv{h}"))
                w = ring(f"qkv{h}")
                for x in range(3):
                    for e in range(2):
                        name = f"{'qkv'[x]}{h}_{e}"
                        pe.wait_ge(*slot_free(name))
                        if x < 2:
                            pe.wait_ge(sig("xc_ready").sem, 2 * h + 2)
                        s = slot_of(name)
                        for kt in range(2):
                            ub = ub_of(2 * h + kt)
                            for b in range(3):
                                rhs = wk(4 + ub, b * SEG, (b + 1) * SEG) if x < 2 else \
                                    wk(ub, 3 + b * SEG, 3 + (b + 1) * SEG)
                                c = (x * 2 + kt) * 256 + e * P
                                last = nc.tensor.matmul(PS[:, s + b, 0:SEG], w[:, c:c + P], rhs,
                                                        start=(kt == 0), stop=(kt == 1))
                        last.then_inc(job_done.up(), 1)
            pe.wait_ge(*slot_free("gates"))
            pe.wait_ge(*read_of("v3_1"))
            pe.wait_ge(s_gate_w.sem, 32)
            s = slot_of("gates")
            for i in range(24):
                for b in range(3):
                    last = nc.tensor.matmul(PS[0:36, s + b, 0:SEG], WIF[:, i, :], big(i, b * SEG, (b + 1) * SEG),
                                            start=(i == 0), stop=(i == 23))
            last.then_inc(job_done.up(), 1)
            pe.wait_ge(*slot_free("acol"))
            s = slot_of("acol")
            pe.wait_ge(sig("a_rows_ready").sem, 1)
            for c in range(NCH):
                last = nc.tensor.transpose(PS[:, s, c * H:(c + 1) * H], WK[0:H, 4 * WT + c * CH:4 * WT + (c + 1) * CH],
                                           ident[0:H, 0:H])
            last.then_inc(job_done.up(), 1)

            pe.wait_ge(*slot_free("rows_u"))
            s = slot_of("rows_u")
            for j in range(8):
                last = nc.tensor.transpose(PS[0:11, s + j // 4, (j % 4) * P:(j % 4 + 1) * P], UT[:, j, :], ident)
            last.then_inc(job_done.up(), 1)
            pe.wait_ge(*slot_free("rows_s"))
            s = slot_of("rows_s")
            pe.wait_ge(sig("sample_cols").sem, 1)
            for i in range(6):
                last = nc.tensor.transpose(PS[0:HP, s + i // 4, (i % 4) * P:(i % 4 + 1) * P], SQC[:, i, :, :]
                                           .rearrange("p h b -> p (h b)"), ident)
            last.then_inc(job_done.up(), 1)

        def stage1_act(act):
            def evac_u(j):
                act.wait_ge(job_done.sem, done(f"u{j}"))
                ub = ub_of(j)
                if j == 0:
                    act.wait_ge(job_done.sem, done("norm0"))
                if j >= 4:
                    act.wait_ge(job_done.sem, done(f"v{j // 2 - 2}_1"))
                s = slot_of(f"u{j}")
                nc.scalar.activation(UT[:, j, :], PS[:, s + 2, SEG - 11:SEG], ACT.Copy)
                nc.scalar.activation(seg3(wk(ub, 3, 3 + W)), slot3(f"u{j}"), ACT.Copy).then_inc(job_read["act"].up(), 1)

            def silu(j):
                act.wait_ge(sig("conv_done").sem, j + 1)
                ub = ub_of(j)
                nc.scalar.activation(wk(4 + ub), wk(4 + ub), ACT.Silu).then_inc(sig("xc_ready").up(), 1)
                act.wait_ge(sig("xc_ready").sem, j + 1)
                act.dma_start(xc_d[j], wk(4 + ub)).then_inc(sig(f"xc{ub}_saved").sem, 16)

            evac_u(0), evac_u(1)
            act.wait_ge(sig("memkv_saved").sem, 64)
            act.wait_ge(sig("xt_saved").sem, 16 * KT)
            for h in range(H):
                if h + 1 < H:
                    evac_u(2 * h + 2)
                silu(2 * h)
                if h + 1 < H:
                    evac_u(2 * h + 3)
                silu(2 * h + 1)
                for x in range(3):
                    for e in range(2):
                        name = f"{'qkv'[x]}{h}_{e}"
                        act.wait_ge(job_done.sem, done(name))
                        nc.scalar.activation(
                            seg3(big(h * 6 + 2 * x + e)), slot3(name), ACT.Copy, scale=1.0 / 16 if x == 1 else 1.0).then_inc(job_read["act"].up(), 1)
            tiles = BIG[:, :].rearrange("p (h i w) -> p i h w", h=H, i=6)
            act.wait_ge(*read_of("v3_1"))
            for ub in range(4):
                act.wait_ge(sig(f"xc{ub}_saved").sem, 32)
            nc.scalar.activation(SQC, tiles[:, :, :, T:W], ACT.Copy).then_inc(sig("sample_cols").up(), 1)
            act.wait_ge(job_done.sem, done("gates"))
            s = slot_of("gates")
            nc.scalar.activation(seg3(WK[0:H, 0:W]), PS[0:H, s:s + 3, 0:SEG], ACT.Identity, bias=BIAS[:, 0:1])
            nc.scalar.activation(seg3(WK[0:H, WT:WT + W]), PS[32:32 + H, s:s + 3, 0:SEG],
                                 ACT.Identity, bias=BIAS[:, 1:2]).then_inc(job_read["act"].up(), 1)
            g = sig("gate_act")
            act.wait_ge(*read_of("gates"))
            nc.scalar.activation(WK[0:H, 2 * WT:2 * WT + W], WK[0:H, WT:WT + W], ACT.Abs).then_inc(g.up(), 1)
            act.wait_ge(g.sem, g.n)
            nc.scalar.activation(WK[0:H, 2 * WT:2 * WT + W], WK[0:H, 2 * WT:2 * WT + W], ACT.Exp, scale=-1.0).then_inc(g.up(), 1)
            act.wait_ge(g.sem, g.n)
            nc.scalar.activation(WK[0:H, 2 * WT:2 * WT + W], WK[0:H, 2 * WT:2 * WT + W], ACT.Ln, bias=1.0).then_inc(g.up(), 1)
            act.wait_ge(job_done.sem, done("acol"))
            nc.scalar.activation(SM[:, 0:32], PS[:, slot_of("acol"), 0:32], ACT.Copy).then_inc(job_read["act"].up(), 1)
            act.wait_ge(job_done.sem, done("rows_u"))
            s = slot_of("rows_u")
            UR = WK[32:43, 0:D]
            nc.scalar.activation(UR.rearrange("p (b n) -> p b n", b=2), PS[0:11, s:s + 2, :],
                                 ACT.Copy).then_inc(job_read["act"].up(), 1)
            act.wait_ge(*read_of("rows_u"))
            act.dma_start(o["conv_p"][0, 0], UR[0:3, :]).then_inc(sig("conv_saved").sem, 16)
            act.dma_start(o["conv_s"][0, :, 2, :], UR[3:11, :]).then_inc(sig("conv_saved").sem, 16)
            act.wait_ge(job_done.sem, done("rows_s"))
            s = slot_of("rows_s")
            nc.scalar.activation(QKVN[:, 0:512], PS[0:HP, s, :], ACT.Copy)
            nc.scalar.activation(QKVN[:, 512:768], PS[0:HP, s + 1, 0:256], ACT.Copy).then_inc(job_read["act"].up(), 1)
            act.wait_ge(sig("rows_ready").sem, 1)
            nc.scalar.activation(RR[:, :, 1:3, :], RR[:, :, 1:3, :], ACT.Exp).then_inc(sig("rows_exp").up(), 1)

        def stage1_dve(dve):
            for j in range(8):
                dve.wait_ge(*read_of(f"u{j}"))
                ub = ub_of(j)
                if j == 0:
                    dve.wait_ge(s_zero.sem, 6)
                if j >= 4:
                    dve.wait_ge(job_done.sem, done(f"k{j // 2 - 2}_1"))
                    dve.wait_ge(sig(f"xc{ub}_saved").sem, 16)
                x = wk(4 + ub)
                new = wk(ub, 3 + T, 3 + W)
                old = VEC[:, j, 0:24].rearrange("p (b r) -> p b r", r=3)
                cw = [vec(ROW_CW + i, j) for i in range(4)]
                nc.vector.tensor_scalar(x[:, 0:T], wk(ub, 3, 3 + T), cw[3], vec(ROW_CB, j), ALU.mult, ALU.add)
                nc.vector.tensor_scalar(x[:, T:W], new, cw[3], vec(ROW_CB, j), ALU.mult, ALU.add).then_inc(step.up(), 1)
                for i in range(3):
                    dve.wait_ge(step.sem, step.n)
                    nc.vector.scalar_tensor_tensor(out=x[:, 0:T], in0=wk(ub, i, i + T), scalar=cw[i], in1=x[:, 0:T],
                                                   op0=ALU.mult, op1=ALU.add)
                    last = nc.vector.scalar_tensor_tensor(out=x[:, T:W], in0=old[:, :, i], scalar=cw[i],
                                                          in1=x[:, T:W], op0=ALU.mult, op1=ALU.add)
                    if i < 2:
                        last.then_inc(step.up(), 1)
                last.then_inc(sig("conv_done").up(), 1)

            def row(i, lo=0, hi=W):
                return WK[0:H, i * WT + lo:i * WT + hi]

            dve.wait_ge(*read_of("gates"))
            dve.wait_ge(sig("gate_act").sem, 3)
            nc.vector.memset(MPV[:, 0:1], 0.0)
            nc.vector.scalar_tensor_tensor(out=row(1), in0=row(1), scalar=0.0, in1=row(2), op0=ALU.min,
                                           op1=ALU.subtract).then_inc(step.up(), 1)
            dve.wait_ge(step.sem, step.n)
            nc.vector.tensor_copy(SM[0:H, 344:352], row(1, T, W)).then_inc(sig("sample_gates_ready").up(), 1)
            nc.vector.tensor_copy(SM[0:H, 352:360], row(0, T, W)).then_inc(sig("sample_gates_ready").up(), 1)
            for ub in range(4):
                dve.wait_ge(sig(f"xc{ub}_saved").sem, 32)
            for c in range(NCH):
                last = nc.vector.tensor_tensor_scan(row(3, c * CH, (c + 1) * CH), ones[0:H, :],
                                                    row(1, c * CH, (c + 1) * CH), 0.0, ALU.mult, ALU.add)
            last.then_inc(step.up(), 1)
            dve.wait_ge(step.sem, step.n)
            nc.vector.tensor_tensor(row(4, 0, T), row(0, 0, T), row(3, 0, T), ALU.subtract).then_inc(sig("a_rows_ready").up(), 1)
            dve.wait_ge(sig("a_rows_ready").sem, sig("a_rows_ready").n)
            for c in range(NCH):
                end = (c + 1) * CH
                nc.vector.tensor_tensor_scan(row(5, c * CH, end), ones[0:H, :], row(4, c * CH, end),
                                             MPV[:, c:c + 1], ALU.mult, ALU.max).then_inc(step.up(), 1)
                dve.wait_ge(step.sem, step.n)
                nc.vector.tensor_tensor(MPV[:, c + 1:c + 2], row(5, end - 1, end), row(3, end - 1, end),
                                        ALU.add).then_inc(step.up(), 1)
                dve.wait_ge(step.sem, step.n)
            m = row(5, 0, T).rearrange("h (c t) -> h c t", c=NCH)
            nc.vector.tensor_scalar(RR[:, :, 0, :], m, -1.0, None, ALU.mult).then_inc(step.up(), 1)
            dve.wait_ge(step.sem, step.n)
            mp = MPV[:, 0:NCH].unsqueeze(2).to_broadcast([H, NCH, CH])
            nc.vector.tensor_tensor(RR[:, :, 1, :], RR[:, :, 0, :], mp, ALU.add)
            nc.vector.tensor_tensor(
                RR[:, :, 2, :], RR[:, :, 0, :], row(3, 0, T).rearrange("h (c t) -> h c t", c=NCH), ALU.subtract).then_inc(sig("rows_ready").up(), 1)

        s_out = sig("outputs_stored")

        CT = WK[:, 0:3072].rearrange("p (h k n) -> p h k n", h=H, k=2)
        VA = WK[:, 3072:3840].rearrange("p (b n) -> p b n", b=2)
        KW = WK[:, 3840:4352].rearrange("p (b n) -> p b n", b=2)
        BS = WK[:, 4352:5376].rearrange("p (b n) -> p b n", b=2)
        DD = WK[:, 5376:5632].rearrange("p (b n) -> p b n", b=2)
        SCT = WK[:, 5632:5888].rearrange("p (b n) -> p b n", b=2)
        QD = WK[:, 5888:6400].rearrange("p (b k n) -> p b k n", b=2, k=2)
        DM = WK[:, 6400:6528]
        DN = WK[:, 6528:6656]
        NU = NCH * H

        def qk_view(h, x, c):
            at = (h * 6 + 2 * x) * W
            return BIG[:, at:at + 2 * W].rearrange("p (k n) -> p k n", k=2)[:, :, c * CH:(c + 1) * CH]

        def stage2_pe(pe):
            pe.wait_ge(*read_of("rows_s"))
            pe.wait_ge(sig("rows_exp").sem, 1)
            for n in range(NU + 1):
                if n < NU:
                    c, h = n // H, n % H
                    if n >= 2:
                        pe.wait_ge(sig("bs_ready").sem, n - 1)
                    nc.tensor.matmul(PS[:, n % 2, 0:384], CST[0:H, C_SEL + h * P:C_SEL + (h + 1) * P],
                                     RR[:, c].rearrange("h x t -> h (x t)"), start=True, stop=True)
                    q, k, v = (qk_view(h, x, c) for x in range(3))
                    for kt in range(2):
                        last = nc.tensor.matmul(PS[:, n % 2, 384:512], k[:, kt, :], q[:, kt, :],
                                                start=(kt == 0), stop=(kt == 1))
                    last.then_inc(sig("scores_done").up(), 1)
                    if n >= 2:
                        pe.wait_ge(sig("kw_ready").sem, n - 1)
                    for kt in range(2):
                        nc.tensor.transpose(PS[:, 2 + n % 2, kt * P:(kt + 1) * P], k[:, kt, :], ident)
                    for kt in range(2):
                        last = nc.tensor.transpose(PS[:, 2 + n % 2, 256 + kt * P:256 + (kt + 1) * P], v[:, kt, :],
                                                   ident)
                    last.then_inc(sig("kv_turned").up(), 1)
                if n >= 1:
                    u = n - 1
                    c, h, b = u // H, u % H, u % 2
                    pe.wait_ge(sig("sc_ready").sem, u + 1)
                    pe.wait_ge(sig("va_ready").sem, u + 1)
                    if u >= 2:
                        pe.wait_ge(sig("hs_done").sem, u - 1)
                    if c > 0:
                        pe.wait_ge(sig("ct_done").sem, u - 3)
                    for m in range(3):
                        out = PS[:, 4 + b, m * P:(m + 1) * P]
                        last = nc.tensor.matmul(out, VA[:, b, m * P:(m + 1) * P], SCT[:, b, :],
                                                start=True, stop=(c == 0))
                        if c > 0:
                            for kt in range(2):
                                last = nc.tensor.matmul(out, CT[:, h, kt, m * P:(m + 1) * P], QD[:, b, kt, :],
                                                        start=False, stop=(kt == 1))
                    last.then_inc(sig("num_done").up(), 1)
                    pe.wait_ge(sig("kw_ready").sem, u + 1)
                    if u >= 1:
                        pe.wait_ge(sig("ct_done").sem, u)
                    for kt in range(2):
                        last = nc.tensor.matmul(PS[:, 6 + kt, 0:384], KW[:, b, kt * P:(kt + 1) * P], VA[:, b, :],
                                                start=True, stop=True)
                    last.then_inc(sig("update_done").up(), 1)

        def stage2_act(act):
            for n in range(NU):
                b = n % 2
                act.wait_ge(sig("scores_done").sem, n + 1)
                if n >= 2:
                    act.wait_ge(sig("ct_done").sem, n - 1)
                if n == 0:
                    act.wait_ge(sig("conv_saved").sem, 32)
                nc.scalar.activation(BS[:, b, :], PS[:, b, :], ACT.Copy).then_inc(sig("bs_ready").up(), 1)
                act.wait_ge(sig("kv_turned").sem, n + 1)
                if n >= 2:
                    act.wait_ge(sig("update_done").sem, n - 1)
                nc.scalar.activation(VA[:, b, 0:256], PS[:, 2 + b, 256:512], ACT.Copy).then_inc(sig("va_ready").up(), 1)
                act.wait_ge(sig("d_args").sem, n + 1)
                nc.scalar.activation(DD[:, b, :], DD[:, b, :], ACT.Exp).then_inc(sig("d_ready").up(), 1)
                act.wait_ge(sig("d_ready").sem, sig("d_ready").n)
                nc.scalar.activation(KW[:, b, :], PS[:, 2 + b, 0:256], ACT.Copy,
                                     scale=DD[:, b, P - 1:P]).then_inc(sig("kw_ready").up(), 1)

        def stage2_dve(dve):
            dve.wait_ge(sig("rows_exp").sem, 1)
            for b in range(2):
                nc.vector.memset(VA[:, b, 256:384], 1.0).then_inc(step.up(), 1)
            dve.wait_ge(step.sem, step.n)
            for n in range(NU + 1):
                if n < NU:
                    c, h, b = n // H, n % H, n % 2
                    dve.wait_ge(sig("bs_ready").sem, n + 1)
                    if n >= 2:
                        dve.wait_ge(sig("kw_ready").sem, n - 1)
                    nc.vector.tensor_scalar(DD[:, b, :], BS[:, b, 0:CH], ACOL[:, c, h:h + 1], 0.0,
                                            ALU.add, ALU.min).then_inc(sig("d_args").up(), 1)
                    if n >= 2:
                        dve.wait_ge(sig("num_done").sem, n - 1)
                    nc.vector.tensor_tensor(QD[:, b], qk_view(h, 0, c),
                                            BS[:, b, CH:2 * CH].unsqueeze(1).to_broadcast([P, 2, CH]), ALU.mult)
                    dve.wait_ge(sig("d_ready").sem, n + 1)
                    nc.vector.tensor_tensor(DM, DD[:, b, :], causal, ALU.mult).then_inc(step.up(), 1)
                    dve.wait_ge(step.sem, step.n)
                    nc.vector.tensor_tensor(SCT[:, b, :], BS[:, b, 384:512], DM, ALU.mult).then_inc(sig("sc_ready").up(), 1)
                if n >= 1:
                    u = n - 1
                    c, h, b = u // H, u % H, u % 2
                    dve.wait_ge(sig("num_done").sem, u + 1)
                    dve.wait_ge(sig("hs_done").sem, sig("hs_done").n)
                    nc.vector.scalar_tensor_tensor(out=DN, in0=PS[:, 4 + b, 256:384], scalar=-1.0,
                                                   in1=BS[:, b, 256:384], op0=ALU.mult, op1=ALU.max).then_inc(step.up(), 1)
                    dve.wait_ge(step.sem, step.n)
                    nc.vector.tensor_tensor(DN, PS[:, 4 + b, 256:384], DN, ALU.max).then_inc(step.up(), 1)
                    dve.wait_ge(step.sem, step.n)
                    nc.vector.reciprocal(DN, DN).then_inc(step.up(), 1)
                    dve.wait_ge(step.sem, step.n)
                    nc.vector.tensor_tensor(
                        qk_view(h, 0, c), PS[:, 4 + b, 0:256].rearrange("p (k n) -> p k n", k=2),
                        DN.unsqueeze(1).to_broadcast([P, 2, CH]), ALU.mult).then_inc(sig("hs_done").up(), 1)
                    dve.wait_ge(sig("update_done").sem, u + 1)
                    for kt in range(2):
                        new = PS[:, 6 + kt, 0:384]
                        if c == 0:
                            last = nc.vector.tensor_copy(CT[:, h, kt, :], new)
                        else:
                            last = nc.vector.scalar_tensor_tensor(out=CT[:, h, kt, :], in0=CT[:, h, kt, :],
                                                                  scalar=BS[:, b, 255:256], in1=new,
                                                                  op0=ALU.mult, op1=ALU.add)
                    last.then_inc(sig("ct_done").up(), 1)

        CO = WK[:, 3072:4096 + 1024].rearrange("p (b n) -> p b n", b=2)

        def stage2_end_pe(pe):
            pe.wait_ge(sig("ct_done").sem, NU)
            for h in range(H):
                if h >= 2:
                    pe.wait_ge(sig("c_copied").sem, h - 1)
                for vt in range(2):
                    for kt in range(2):
                        last = nc.tensor.transpose(PS[:, 2 * (h % 2), vt * 256 + kt * P:vt * 256 + (kt + 1) * P],
                                                   CT[:, h, kt, vt * P:(vt + 1) * P], ident)
                last.then_inc(sig("c_turned").up(), 1)
            pe.wait_ge(sig("c_copied").sem, H)

        def stage2_end_act(act):
            own = sig("c_copied")
            for h in range(H):
                act.wait_ge(sig("c_turned").sem, h + 1)
                if h >= 2:
                    act.wait_ge(sig(f"c{h % 2}_saved").sem, 16)
                nc.scalar.activation(CO[:, h % 2, 0:512], PS[:, 2 * (h % 2), :], ACT.Copy).then_inc(own.up(), 1)
                act.wait_ge(own.sem, own.n)
                act.dma_start(o["C_p"][0, 0, h].rearrange("(v p) k -> p v k", p=P),
                              CO[:, h % 2, 0:512].rearrange("p (v k) -> p v k", v=2))\
                    .then_inc(sig(f"c{h % 2}_saved").sem, 16)

        def stage2_end_sp(sp):
            sp.wait_ge(sig("ct_done").sem, NU)
            for h in range(H):
                for kt in range(2):
                    sp.dma_start(o["n_p"][0, 0, h, kt * P:(kt + 1) * P].rearrange("(p a) -> p a", a=1),
                                 CT[:, h, kt, 256:257]).then_inc(sig("n_saved").sem, 16)
            sp.dma_start(o["m_p"].rearrange("a b h -> h (a b)"), MPV[:, NCH:NCH + 1]).then_inc(sig("n_saved").sem, 16)

        CTP, QWP, PRP = (WK[:, 4 * WT + at:4 * WT + at + 1024].rearrange("p (b n) -> p b n", b=2)
                         for at in (0, 1024, 2048))

        def hq(h):
            return BIG[:, h * 6 * W:(h * 6 + 2) * W]

        def gates_sp(sp):
            for name in ("o0_0", "o0_1", "zg0_0"):
                load_item(sp, name)
            sp.wait_ge(sig("sample_gates_ready").sem, 2)
            sp.dma_start(sg_d.rearrange("x h b -> h x b"), SM[0:H, 344:360].rearrange("h (x b) -> h x b", x=2))\
                .then_inc(sig("gates_saved").sem, 16)
            sp.wait_ge(sig("gates_saved").sem, 16)
            for x in range(2):
                sp.dma_start(SC32[:, 1 + x:2 + x], sg_d[x].rearrange("h (b a) -> (h b) a", a=1))\
                    .then_inc(sig("pair_inputs").sem, 16)
            for h in range(H):
                rows = slice(64 + h * NS, 64 + (h + 1) * NS)
                sp.dma_start(XTRA[rows, 768:1024], a["state_n"][0, :, h, :]).then_inc(sig("pair_inputs").sem, 16)
                sp.dma_start(XTRA[rows, 1792:1793], a["state_m"][0, :, h:h + 1],
                             allow_slow_non_contiguous=True).then_inc(sig("pair_inputs").sem, 16)

        def pair_scalars_dve(dve):
            def col(i, n=1):
                return SC32[:, i:i + n]

            def do(ins):
                ins.then_inc(step.up(), 1)
                dve.wait_ge(step.sem, step.n)

            dve.wait_ge(*read_of("rows_s"))
            dve.wait_ge(sig("pair_inputs").sem, 16 * 10)
            q, k = QKVN[:, 0:256], QKVN[:, 256:512]
            do(nc.vector.tensor_tensor(col(3), col(1), col(0), ALU.add))
            do(nc.vector.tensor_tensor(col(4), col(3), col(2), ALU.max))
            nc.vector.tensor_tensor(col(5), col(3), col(4), ALU.subtract)
            nc.vector.tensor_tensor(col(6), col(2), col(4), ALU.subtract)
            nc.vector.tensor_scalar(col(7), col(4), -1.0, None, ALU.mult).then_inc(sig("pair_exp_args").up(), 1)
            nc.vector.tensor_tensor_reduce(TMP32, q, k, 1.0, 0.0, ALU.mult, ALU.add, col(8))
            do(nc.vector.tensor_tensor_reduce(NN32, q, SN, 1.0, 0.0, ALU.mult, ALU.add, col(9)))
            dve.wait_ge(sig("pair_exp").sem, 1)
            do(nc.vector.tensor_tensor(col(10), col(8), col(6), ALU.mult))
            do(nc.vector.scalar_tensor_tensor(out=col(11), in0=col(9), scalar=col(5), in1=col(10), op0=ALU.mult,
                                              op1=ALU.add))
            do(nc.vector.scalar_tensor_tensor(out=col(12), in0=col(11), scalar=-1.0, in1=col(7), op0=ALU.mult,
                                              op1=ALU.max))
            do(nc.vector.tensor_tensor(col(12), col(11), col(12), ALU.max))
            do(nc.vector.reciprocal(col(12), col(12)))
            nc.vector.tensor_tensor(col(13), col(5), col(12), ALU.mult)
            nc.vector.tensor_tensor(col(14), col(10), col(12), ALU.mult)
            nc.vector.tensor_copy(col(15), col(5))
            do(nc.vector.tensor_scalar(WK32, k, col(6), None, ALU.mult))
            nc.vector.scalar_tensor_tensor(out=NN32, in0=SN, scalar=col(5), in1=WK32,
                                           op0=ALU.mult, op1=ALU.add).then_inc(sig("pair_scalars").up(), 1)

        def pair_scalars_act(act):
            act.wait_ge(sig("pair_exp_args").sem, 1)
            nc.scalar.activation(SC32[:, 5:8], SC32[:, 5:8], ACT.Exp).then_inc(sig("pair_exp").up(), 1)

        def pair_scalars_sp(sp):
            sp.wait_ge(sig("pair_scalars").sem, 1)
            back = sig("pair_saved").sem
            sp.dma_start(qw_d[:, 0:256], QKVN[:, 0:256]).then_inc(back, 16)
            sp.dma_start(qw_d[:, 256:512], WK32).then_inc(back, 16)
            sp.dma_start(cf_d, SC32[:, 13:16]).then_inc(back, 16)
            for h in range(H):
                rows = slice(64 + h * NS, 64 + (h + 1) * NS)
                sp.dma_start(o["n_s"][0, :, h, :], XTRA[rows, 1536:1792]).then_inc(sig("nm_saved").sem, 16)
                sp.dma_start(o["m_s"][0, :, h:h + 1], XTRA[rows, 1796:1797],
                             allow_slow_non_contiguous=True).then_inc(sig("nm_saved").sem, 16)
            sp.wait_ge(sig("pair_saved").sem, 48)
            sp.dma_start(COEF, cf_d.rearrange("i k -> (i k)").partition_broadcast(P)
                         .rearrange("p (i k) -> p i k", k=3)).then_inc(sig("coef_loaded").sem, 16)

        def pair_load(sp, i):
            h, b, buf = i // NS, i % NS, i % 2
            if i >= 2:
                sp.wait_ge(sig(f"cs{buf}_saved").sem, 16 * (i // 2))
            s = sig(f"pair{buf}_loaded").sem
            sp.dma_start(CTP[:, buf, :].rearrange("p (v k) -> p v k", v=2),
                         a["state_C"][0, b, h].rearrange("(v p) k -> p v k", p=P)).then_inc(s, 16)
            sp.dma_start(QWP[:, buf, :], qw_d[i].partition_broadcast(P)).then_inc(s, 16)

        def pair_store(sp, i):
            h, b, buf = i // NS, i % NS, i % 2
            sp.wait_ge(sig("pair_done").sem, i + 1)
            sp.dma_start(o["C_s"][0, b, h].rearrange("(v p) k -> p v k", p=P),
                         CTP[:, buf, :].rearrange("p (v k) -> p v k", v=2)).then_inc(sig(f"cs{buf}_saved").sem, 16)

        def pair_pool(pool, i):
            buf = i % 2
            pool.wait_ge(sig(f"pair{buf}_loaded").sem, 32 * (i // 2 + 1))
            if i >= 2:
                pool.wait_ge(sig("cq_done").sem, i - 1)
            v2 = lambda x: x[:, buf, :].rearrange("p (v k) -> p v k", v=2)
            nc.gpsimd.tensor_tensor(
                v2(PRP), v2(CTP), QWP[:, buf, 0:256].unsqueeze(1).to_broadcast([P, 2, 256]), ALU.mult).then_inc(sig("prod_done").up(), 1)

        def pair_act(act, i):
            act.wait_ge(sig("prod_done").sem, i + 1)
            nc.scalar.activation(CTP[:, i % 2, :], CTP[:, i % 2, :], ACT.Copy,
                                 scale=COEF[:, i, 2:3]).then_inc(sig("c_decayed").up(), 1)

        def pair_dve(dve, i):
            h, b, buf = i // NS, i % NS, i % 2
            dve.wait_ge(sig("prod_done").sem, i + 1)
            nc.vector.tensor_reduce(CQ[:, :, i:i + 1], PRP[:, buf, :].rearrange(
                "p (v k) -> p v k", v=2), AX.X, ALU.add).then_inc(sig("cq_done").up(), 1)
            dve.wait_ge(sig("c_decayed").sem, i + 1)
            for vt in range(2):
                c = CTP[:, buf, vt * 256:(vt + 1) * 256]
                at = (h * 6 + 4 + vt) * W + T + b
                last = nc.vector.scalar_tensor_tensor(out=c, in0=QWP[:, buf, 256:512], scalar=BIG[:, at:at + 1],
                                                      in1=c, op0=ALU.mult, op1=ALU.add)
            last.then_inc(sig("pair_done").up(), 1)

        def stage3_sp(sp):
            pair_scalars_sp(sp)
            for h in range(H):
                if h > 0:
                    load_item(sp, f"o{h}_0"), load_item(sp, f"o{h}_1"), load_item(sp, f"zg{h}_0")
                load_item(sp, f"zg{h}_1")
                if h >= 2:
                    sp.wait_ge(sig("y_ready").sem, h - 1)
                if h == 0:
                    sp.wait_ge(sig("n_saved").sem, 16 * 9)
                    sp.wait_ge(sig("c0_saved").sem, 32)
                    sp.wait_ge(sig("c1_saved").sem, 32)
                for e in range(2):
                    sp.dma_start(wk(2 * (h % 2) + e), xc_d[2 * h + e]).then_inc(sig(f"xc_pair{h % 2}").sem, 16)
                for i in range(h * NS, (h + 1) * NS):
                    if i >= 2:
                        pair_store(sp, i - 2)
                    pair_load(sp, i)
            for i in (30, 31):
                pair_store(sp, i)

        def stage3_pool(pool):
            for h in range(H):
                scale_item(pool, f"o{h}_0"), scale_item(pool, f"o{h}_1")
                scale_item(pool, f"zg{h}_0"), scale_item(pool, f"zg{h}_1")
                for i in range(h * NS, (h + 1) * NS):
                    pair_pool(pool, i)

        def stage3_pe(pe):
            def mean(h):
                name = f"mean{h}"
                pe.wait_ge(*slot_free(name))
                pe.wait_ge(sig("gated").sem, h + 1)
                s = slot_of(name)
                for e in range(2):
                    for b in range(3):
                        last = nc.tensor.matmul(PS[:, s + b, 0:SEG], avg_h, big(h * 6 + e, b * SEG, (b + 1) * SEG),
                                                start=(e == 0), stop=(e == 1))
                last.then_inc(job_done.up(), 1)

            def var(h):
                name = f"var{h}"
                pe.wait_ge(*slot_free(name))
                pe.wait_ge(sig("squares").sem, h + 1)
                s = slot_of(name)
                for e in range(2):
                    for b in range(3):
                        last = nc.tensor.matmul(PS[:, s + b, 0:SEG], avg_h,
                                                big(h * 6 + 2 + e, b * SEG, (b + 1) * SEG),
                                                start=(e == 0), stop=(e == 1))
                last.then_inc(job_done.up(), 1)

            for h in range(H):
                for e in range(2):
                    pe_proj(pe, f"o{h}_{e}", ht)
                if h > 0:
                    var(h - 1)
                for e in range(2):
                    pe_proj(pe, f"zg{h}_{e}", ht)
                mean(h)
            var(3)

        def stage3_act(act):
            def root(h):
                act.wait_ge(job_done.sem, done(f"var{h}"))
                if h > 0:
                    act.wait_ge(sig("y_ready").sem, h)
                nc.scalar.activation(seg3(wk(7)), slot3(f"var{h}"), ACT.Sqrt, bias=EPSC).then_inc(job_read["act"].up(), 1)

            pair_scalars_act(act)
            for h in range(H):
                for e in range(2):
                    act.wait_ge(job_done.sem, done(f"o{h}_{e}"))
                    nc.scalar.activation(seg3(big(h * 6 + 2 + e)), slot3(f"o{h}_{e}"),
                                         ACT.Sigmoid).then_inc(job_read["act"].up(), 1)
                if h == 0:
                    act.wait_ge(sig("coef_loaded").sem, 16)
                for i in range(h * NS, (h + 1) * NS):
                    pair_act(act, i)
                if h > 0:
                    root(h - 1)
                act.wait_ge(sig("hs_sample").sem, h + 1)
                for e in range(2):
                    act.wait_ge(job_done.sem, done(f"zg{h}_{e}"))
                    nc.scalar.activation(seg3(big(h * 6 + 4 + e)), slot3(f"zg{h}_{e}"),
                                         ACT.Silu).then_inc(job_read["act"].up(), 1)
                act.wait_ge(*read_of(f"mean{h}"))
                nc.scalar.activation(BIG[:, (h * 6 + 2) * W:(h * 6 + 4) * W], hq(h), ACT.Square).then_inc(sig("squares").up(), 1)
            root(3)

        def stage3_dve(dve):
            def finish(h):
                dve.wait_ge(*read_of(f"var{h}"))
                nc.vector.reciprocal(wk(7), wk(7)).then_inc(step.up(), 1)
                dve.wait_ge(step.sem, step.n)
                dve.wait_ge(sig(f"xc_pair{h % 2}").sem, 32 * (h // 2 + 1))
                for e in range(2):
                    x, j = big(h * 6 + e), 2 * h + e
                    nc.vector.scalar_tensor_tensor(out=x, in0=x, scalar=vec(ROW_GHN, j), in1=wk(7),
                                                   op0=ALU.mult, op1=ALU.mult).then_inc(step.up(), 1)
                    dve.wait_ge(step.sem, step.n)
                    nc.vector.scalar_tensor_tensor(out=x, in0=wk(2 * (h % 2) + e),
                                                   scalar=vec(ROW_SKIP, j), in1=x,
                                                   op0=ALU.mult, op1=ALU.add).then_inc(step.up(), 1)
                    dve.wait_ge(step.sem, step.n)
                dve.wait_ge(*read_of(f"zg{h}_1"))
                nc.vector.tensor_tensor(hq(h), hq(h), BIG[:, (h * 6 + 4) * W:(h * 6 + 6) * W],
                                        ALU.mult).then_inc(sig("y_ready").up(), 1)

            pair_scalars_dve(dve)
            dve.wait_ge(sig("coef_loaded").sem, 16)
            for h in range(H):
                for i in range(h * NS, (h + 1) * NS):
                    pair_dve(dve, i)
                pairs = slice(h * NS, (h + 1) * NS)
                c1, c2 = (COEF[:, pairs, x].unsqueeze(1).to_broadcast([P, 2, NS]) for x in range(2))
                v = BIG[:, (h * 6 + 4) * W:(h * 6 + 6) * W].rearrange("p (v w) -> p v w", v=2)[:, :, T:W]
                t0 = HSS[:, 0:16].rearrange("p (v b) -> p v b", v=2)
                t1 = HSS[:, 16:32].rearrange("p (v b) -> p v b", v=2)
                dve.wait_ge(sig("cq_done").sem, sig("cq_done").n)
                nc.vector.tensor_tensor(t0, CQ[:, :, pairs], c1, ALU.mult)
                nc.vector.tensor_tensor(t1, v, c2, ALU.mult).then_inc(step.up(), 1)
                dve.wait_ge(step.sem, step.n)
                nc.vector.tensor_tensor(
                    hq(h).rearrange("p (v w) -> p v w", v=2)[:, :, T:W], t0, t1, ALU.add).then_inc(sig("hs_sample").up(), 1)
                dve.wait_ge(sig("hs_sample").sem, sig("hs_sample").n)
                dve.wait_ge(*read_of(f"o{h}_1"))
                nc.vector.tensor_tensor(hq(h), hq(h), BIG[:, (h * 6 + 2) * W:(h * 6 + 4) * W],
                                        ALU.mult).then_inc(sig("gated").up(), 1)
                if h > 0:
                    finish(h - 1)
                dve.wait_ge(job_done.sem, done(f"mean{h}"))
                dve.wait_ge(sig("gated").sem, sig("gated").n)
                for e in range(2):
                    last = nc.vector.tensor_tensor(seg3(big(h * 6 + e)), seg3(big(h * 6 + e)), slot3(f"mean{h}"),
                                                   ALU.subtract)
                last.then_inc(job_read["dve"].up(), 1)
            finish(3)

        ATT = {}

        def attention(name, base, q, k, nk, mask, v, out, p, pt, stat):
            ATT[name] = dict(base=base, q=q, k=k, nk=nk, mask=mask, v=v, out=out, p=p, pt=pt, stat=stat)

        def score_view(u, nk):
            b = 2 * (u % 2)
            return PS[:, b:b + 2, 0:2 * nk].rearrange("p b (x n) -> p b x n", x=2)

        def attend_pe(pe, name):
            c = ATT[name]
            for i in range(10):
                u = c["base"] + i
                if i < 8:
                    nk = c["nk"](i)
                    if i >= 2:
                        pe.wait_ge(sig("probs_ready").sem, u - 1)
                    for h in range(H):
                        bank = PS[:, 2 * (u % 2) + h // 2, :]
                        if c["mask"] and h % 2 == 0:
                            nc.tensor.matmul(bank[:, 0:2 * nk], BFC[:, M_ID:M_ID + P], c["mask"](i),
                                             start=True, stop=False, skip_group_check=True)
                        last = nc.tensor.matmul(bank[:, (h % 2) * nk:(h % 2 + 1) * nk], c["q"](h, i), c["k"](h, i),
                                                start=not c["mask"], stop=True, skip_group_check=True)
                    last.then_inc(sig("scores_ready").up(), 1)
                if 1 <= i < 9:
                    w, nk = u - 1, c["nk"](i - 1)
                    pe.wait_ge(sig("probs_scaled").sem, w + 1)
                    if i >= 2:
                        pe.wait_ge(sig("turned_copied").sem, w)
                    n = nk // P
                    for h in range(H):
                        for t in range(n):
                            at = (h % 2) * nk + t * P
                            last = nc.tensor.transpose(PS[:, 4 + h // 2, at:at + P],
                                                       c["p"](w)[:, h * nk + t * P:h * nk + (t + 1) * P], ident)
                    last.then_inc(sig("probs_turned").up(), 1)
                if i >= 2:
                    w, nk = u - 2, c["nk"](i - 2)
                    pe.wait_ge(sig("turned_copied").sem, w + 1)
                    if i >= 4:
                        pe.wait_ge(sig("out_read").sem, w - 1)
                    n = nk // P
                    for h in range(H):
                        for t in range(n):
                            at = h * nk + t * P
                            last = nc.tensor.matmul(PS[:, 6 + w % 2, h * P:(h + 1) * P], c["v"](h, t, i - 2),
                                                    c["pt"](w)[:, at:at + P], start=(t == 0), stop=(t == n - 1))
                    last.then_inc(sig("out_ready").up(), 1)
            pe.wait_ge(sig("out_read").sem, c["base"] + 8)

        def attend_act(act, name):
            c = ATT[name]
            negmax, total = c["stat"][0], c["stat"][1]
            for i in range(9):
                u = c["base"] + i
                if i < 8:
                    nk = c["nk"](i)
                    act.wait_ge(sig("max_ready").sem, 2 * (u + 1))
                    if i >= 2:
                        act.wait_ge(sig("probs_turned").sem, u - 1)
                    for h in range(H):
                        last = nc.scalar.activation(c["p"](u)[:, h * nk:(h + 1) * nk],
                                                    PS[:, 2 * (u % 2) + h // 2, (h % 2) * nk:(h % 2 + 1) * nk],
                                                    ACT.Exp, bias=negmax[:, 4 * i + h:4 * i + h + 1], scale=SCALE,
                                                    accum_out=total[:, 4 * i + h:4 * i + h + 1])
                    last.then_inc(sig("probs_ready").up(), 1)
                if i >= 1:
                    w, nk = u - 1, c["nk"](i - 1)
                    act.wait_ge(sig("probs_turned").sem, w + 1)
                    if i >= 3:
                        act.wait_ge(sig("out_ready").sem, w - 1)
                    nc.scalar.activation(
                        c["pt"](w)[:, 0:4 * nk].rearrange("p (b n) -> p b n", b=2), PS[:, 4:6, 0:2 * nk], ACT.Copy).then_inc(sig("turned_copied").up(), 1)

        def attend_dve(dve, name):
            c = ATT[name]
            negmax, total, inv = c["stat"][0], c["stat"][1], c["stat"][2]
            for i in range(10):
                u = c["base"] + i
                if i < 8:
                    nk = c["nk"](i)
                    cols = slice(4 * i, 4 * i + 4)
                    dve.wait_ge(sig("scores_ready").sem, u + 1)
                    own = sig("max_ready")
                    nc.vector.tensor_reduce(negmax[:, cols].rearrange("p (b x) -> p b x", b=2),
                                            score_view(u, nk), AX.X, ALU.max, negate=True).then_inc(own.up(), 1)
                    dve.wait_ge(own.sem, own.n)
                    nc.vector.tensor_scalar(negmax[:, cols], negmax[:, cols], SCALE, None, ALU.mult).then_inc(own.up(), 1)
                if 1 <= i < 9:
                    w, nk = u - 1, c["nk"](i - 1)
                    cols = slice(4 * (i - 1), 4 * i)
                    dve.wait_ge(sig("probs_ready").sem, w + 1)
                    nc.vector.reciprocal(inv[:, cols], total[:, cols]).then_inc(step.up(), 1)
                    dve.wait_ge(step.sem, step.n)
                    for h in range(H):
                        x = c["p"](w)[:, h * nk:(h + 1) * nk]
                        at = 4 * (i - 1) + h
                        last = nc.vector.tensor_scalar(x, x, inv[:, at:at + 1], None, ALU.mult)
                    last.then_inc(sig("probs_scaled").up(), 1)
                if i >= 2:
                    w = u - 2
                    dve.wait_ge(sig("out_ready").sem, w + 1)
                    c["out"](i - 2, PS[:, 6 + w % 2, :].rearrange("p (h n) -> p h n", h=H)).then_inc(sig("out_read").up(), 1)

        SMP = {}
        tile_loaded = [sig(f"tile{n}_loaded") for n in range(4)]
        query_loaded = [sig(f"query{n}_loaded") for n in range(2)]

        def samples(name, nt, base, key, value, query, tiles, queries, prods, misc, free, new=None):
            m = {}
            at = 0
            for what, size in (("scores", nt * HP), ("cols", 4), ("row", nt * P + nt), ("turned", 2 * nt * HP),
                               ("diag", nt * HP), ("qk", nt * HP)):
                m[what] = misc[:, at:at + size]
                at += size
            SMP[name] = dict(nt=nt, base=base, key=key, value=value, query=query, tiles=tiles, queries=queries,
                             prods=prods, m=m, free=free, new=new)

        def tile_count(c, n):
            g = c["first_load"] + n
            return tile_loaded[g % 4], 16 * (g // 4 + 1), g % 4

        def samples_sp(sp, name):
            c = SMP[name]
            n_u = c["nt"] * NS
            c["free"](sp)
            for n in range(2 * n_u):
                s, v, buf = tile_count(c, n)
                if n >= 4:
                    if n - 4 < n_u:
                        sp.wait_ge(sig("key_products").sem, c["base"] + n - 3)
                    else:
                        sp.wait_ge(sig("values_used").sem, c["base"] + n - 4 - n_u + 1)
                b, t = n % n_u // c["nt"], n % n_u % c["nt"]
                src = c["key"](b, t) if n < n_u else c["value"](b, t)
                sp.dma_start(c["tiles"][buf], src).then_inc(s.sem, 16)
                if n < n_u:
                    if n >= 2:
                        sp.wait_ge(sig("key_products").sem, c["base"] + n - 1)
                    u = c["base"] + n
                    sp.dma_start(c["queries"][u % 2].rearrange("p (h d) -> p h d", h=H),
                                 c["query"](b, t).partition_broadcast(P)).then_inc(query_loaded[u % 2].sem, 16)

        def samples_pool(pool, name):
            c = SMP[name]
            for n in range(c["nt"] * NS):
                s, v, buf = tile_count(c, n)
                u = c["base"] + n
                pool.wait_ge(s.sem, v)
                pool.wait_ge(query_loaded[u % 2].sem, 16 * (u // 2 + 1))
                if n >= 2:
                    pool.wait_ge(sig("key_sums").sem, u - 1)
                nc.gpsimd.tensor_tensor(c["prods"][u % 2], c["tiles"][buf],
                                        c["queries"][u % 2], ALU.mult).then_inc(sig("key_products").up(), 1)

        def samples_scores_dve(dve, name):
            c = SMP[name]
            sc = c["m"]["scores"].rearrange("p (t h b) -> p t h b", t=c["nt"], h=H)
            for n in range(c["nt"] * NS):
                b, t = n // c["nt"], n % c["nt"]
                u = c["base"] + n
                dve.wait_ge(sig("key_products").sem, u + 1)
                nc.vector.tensor_reduce(
                    sc[:, t, :, b:b + 1], c["prods"][u % 2].rearrange("p (h d) -> p h d", h=H), AX.X, ALU.add).then_inc(sig("key_sums").up(), 1)
            if c["new"]:
                q, k, _ = c["new"]
                qk = c["m"]["qk"].rearrange("p (t n) -> p t n", t=c["nt"])
                for t in range(c["nt"]):
                    last = nc.vector.tensor_tensor(qk[:, t, :].rearrange("p (h b) -> p h b", h=H), q(t),
                                                   k(t).rearrange("p (h b) -> p h b", h=H), ALU.mult)
                last.then_inc(sig("new_products").up(), 1)

        def samples_dve(dve, name, finish):
            c = SMP[name]
            m, nt = c["m"], c["nt"]
            nr = nt * P + (nt if c["new"] else 0)
            row, cols = m["row"][0:HP, 0:nr], m["cols"][0:HP, :]
            dve.wait_ge(*read_of(f"ss{name}"))
            nc.vector.tensor_reduce(cols[:, 0:1], row, AX.X, ALU.max, negate=True).then_inc(step.up(), 1)
            dve.wait_ge(step.sem, step.n)
            nc.vector.tensor_scalar(cols[:, 0:1], cols[:, 0:1], SCALE, None, ALU.mult).then_inc(sig("sample_max").up(), 1)
            dve.wait_ge(sig("sample_exp").sem, c["order"] + 1)
            nc.vector.reciprocal(cols[:, 2:3], cols[:, 1:2]).then_inc(step.up(), 1)
            dve.wait_ge(step.sem, step.n)
            ins = nc.vector.tensor_scalar(row, row, cols[:, 2:3], None, ALU.mult)
            if c["new"]:
                ins.then_inc(step.up(), 1)
                dve.wait_ge(step.sem, step.n)
                for t in range(nt):
                    ins = nc.vector.tensor_scalar(m["diag"][0:HP, t * HP:(t + 1) * HP], ident[0:HP, 0:HP],
                                                  row[:, nt * P + t:nt * P + t + 1], None, ALU.mult)
            ins.then_inc(sig("sample_probs").up(), 1)
            dve.wait_ge(job_done.sem, done(f"so{name}"))
            s = slot_of(f"so{name}")
            finish(PS[:, s, 0:HP])

        def samples_act(act, name):
            c = SMP[name]
            m, nt = c["m"], c["nt"]
            nr = nt * P + (nt if c["new"] else 0)
            row, cols = m["row"][0:HP, 0:nr], m["cols"][0:HP, :]
            act.wait_ge(job_done.sem, done(f"ss{name}"))
            nc.scalar.activation(row, PS[0:HP, slot_of(f"ss{name}"), 0:nr], ACT.Copy).then_inc(job_read["act"].up(), 1)
            act.wait_ge(sig("sample_max").sem, c["order"] + 1)
            nc.scalar.activation(row, row, ACT.Exp, bias=cols[:, 0:1], scale=SCALE,
                                 accum_out=cols[:, 1:2]).then_inc(sig("sample_exp").up(), 1)
            act.wait_ge(job_done.sem, done(f"sp{name}"))
            n = nt * HP * (2 if c["new"] else 1)
            nc.scalar.activation(m["turned"][:, 0:n], PS[:, slot_of(f"sp{name}"), 0:n],
                                 ACT.Copy).then_inc(job_read["act"].up(), 1)

        def samples_pe(pe, name):
            c = SMP[name]
            m, nt = c["m"], c["nt"]
            pe.wait_ge(*slot_free(f"ss{name}"))
            s = slot_of(f"ss{name}")
            pe.wait_ge(sig("key_sums").sem, c["base"] + nt * NS)
            for t in range(nt):
                last = nc.tensor.transpose(PS[0:HP, s, t * P:(t + 1) * P], m["scores"][:, t * HP:(t + 1) * HP], ident)
            if c["new"]:
                pe.wait_ge(sig("new_products").sem, 1)
                for t in range(nt):
                    last = nc.tensor.matmul(PS[0:HP, s, nt * P + t:nt * P + t + 1],
                                            m["qk"][:, t * HP:(t + 1) * HP], ones[:, 0:1], start=True, stop=True)
            last.then_inc(job_done.up(), 1)
            pe.wait_ge(*slot_free(f"sp{name}"))
            s = slot_of(f"sp{name}")
            pe.wait_ge(sig("sample_probs").sem, c["order"] + 1)
            for t in range(nt):
                last = nc.tensor.transpose(PS[:, s, t * HP:(t + 1) * HP], m["row"][0:HP, t * P:(t + 1) * P],
                                           ident[0:HP, 0:HP])
            if c["new"]:
                last = nc.tensor.matmul(PS[:, s, nt * HP:2 * nt * HP], ones[0:HP, :], m["diag"][0:HP, :],
                                        start=True, stop=True)
            last.then_inc(job_done.up(), 1)
            pe.wait_ge(*slot_free(f"so{name}"))
            s = slot_of(f"so{name}")
            pe.wait_ge(*read_of(f"sp{name}"))
            n_u = nt * NS
            for n in range(n_u):
                b, t = n // nt, n % nt
                sem, v, buf = tile_count(c, n_u + n)
                pe.wait_ge(sem.sem, v)
                for h in range(H):
                    at = t * HP + h * NS + b
                    last = nc.tensor.matmul(PS[:, s, h * NS + b:h * NS + b + 1], c["tiles"][buf][:, h * P:(h + 1) * P],
                                            m["turned"][:, at:at + 1], start=(n == 0 and h == 0), stop=True,
                                            skip_group_check=True)
                last.then_inc((sig("values_used") if n < n_u - 1 else job_done).up(), 1)

        def query_rows_pe(pe, name, srcs):
            pe.wait_ge(*slot_free(name))
            s = slot_of(name)
            for i, src in enumerate(srcs):
                last = nc.tensor.transpose(PS[0:HP, s + i // 4, (i % 4) * P:(i % 4 + 1) * P], src, ident)
            last.then_inc(job_done.up(), 1)

        MKV = WK[:, 0:2048].rearrange("p (t n) -> p t n", t=2)
        MKT = WK[:, 2 * WT:2 * WT + D]
        STAT = WK[:, 7 * WT:7 * WT + 128]

        def cols4(tile0, stride, lo, hi):
            return BIG[:, :].rearrange("p (i w) -> p i w", w=W)[:, tile0:tile0 + 3 * stride + 1:stride, lo:hi]

        def memory_attention(name, base, q0, q_stride, z0, z_stride):
            def out(i, ps):
                c = slice(i * P, (i + 1) * P)
                return nc.vector.tensor_tensor(cols4(q0, q_stride, c.start, c.stop), ps,
                                               cols4(z0, z_stride, c.start, c.stop), ALU.mult)
            attention(name, base,
                      q=lambda h, i: big(q0 + h * q_stride, i * P, (i + 1) * P),
                      k=lambda h, i: MKT[:, h * NMEM:(h + 1) * NMEM],
                      nk=lambda i: NMEM, mask=None,
                      v=lambda h, t, i: MKV[:, t, 512 + h * P:512 + (h + 1) * P],
                      out=out, p=lambda u: wk(3 + u % 2, 0, D), pt=lambda u: wk(5 + u % 2, 0, D),
                      stat=(STAT[:, 0:32], STAT[:, 32:64], STAT[:, 64:96]))

        memory_attention("memA", 0, 2, 6, 3, 6)
        memory_attention("memB", 32, 16, 1, 20, 1)

        def memory_samples(name, l, base, order, first_load, tiles, other, q_row, free):
            kv = a["cache_mem_kv"][l].rearrange("b (t p) x h d -> b t p x (h d)", p=P)
            samples(name, 2, base, key=lambda b, t: kv[b, t, :, 0, :], value=lambda b, t: kv[b, t, :, 1, :],
                    query=lambda b, t: qs_d[q_row].rearrange("(h b) d -> b h d", b=NS)[b],
                    tiles=[BIG[:, tiles * W + 512 * n:tiles * W + 512 * (n + 1)] for n in range(4)],
                    queries=[BIG[:, other * W + 512 * n:other * W + 512 * (n + 1)] for n in range(2)],
                    prods=[BIG[:, other * W + 512 * (n + 2):other * W + 512 * (n + 3)] for n in range(2)],
                    misc=TRIG[:, 0:1024], free=free)
            SMP[name].update(order=order, first_load=first_load)

        def memory_jobs(x, l, q_tile, z_tile, w0):
            def pe_part(pe):
                for h in range(H):
                    pe_proj(pe, f"qm{x}{h}", ht)
                for h in range(H):
                    pe_proj(pe, f"zm{x}{h}", ht)
                pe.wait_ge(sig("query_cols").sem, l + 1)
                query_rows_pe(pe, f"qs{x}", [HSS])
                pe.wait_ge(*slot_free(f"mk{x}"))
                s = slot_of(f"mk{x}")
                pe.wait_ge(sig("memory_loaded").sem, 16 * (l + 1))
                for h in range(H):
                    for t in range(2):
                        at = (h % 2) * NMEM + t * P
                        last = nc.tensor.transpose(PS[:, s + h // 2, at:at + P], MKV[:, t, h * P:(h + 1) * P], ident)
                last.then_inc(job_done.up(), 1)
                pe.wait_ge(*read_of(f"mk{x}"))

            def act_part(act):
                for h in range(H):
                    act.wait_ge(job_done.sem, done(f"qm{x}{h}"))
                    nc.scalar.activation(seg3(big(q_tile(h))), slot3(f"qm{x}{h}"), ACT.Copy).then_inc(job_read["act"].up(), 1)
                act.wait_ge(*read_of(f"qm{x}3"))
                stride = q_tile(1) - q_tile(0)
                nc.scalar.activation(HSS.rearrange("p (h b) -> p h b", h=H),
                                     cols4(q_tile(0), stride, T, W), ACT.Copy).then_inc(sig("query_cols").up(), 1)
                for h in range(H):
                    act.wait_ge(job_done.sem, done(f"zm{x}{h}"))
                    nc.scalar.activation(seg3(big(z_tile(h))), slot3(f"zm{x}{h}"), ACT.Silu).then_inc(job_read["act"].up(), 1)
                act.wait_ge(job_done.sem, done(f"qs{x}"))
                rows = TRIG[0:HP, 1100:1100 + P]
                nc.scalar.activation(rows, PS[0:HP, slot_of(f"qs{x}"), 0:P], ACT.Copy).then_inc(job_read["act"].up(), 1)
                act.wait_ge(*read_of(f"qs{x}"))
                act.dma_start(qs_d[l], rows).then_inc(sig("query_rows_saved").sem, 16)
                act.wait_ge(job_done.sem, done(f"mk{x}"))
                s = slot_of(f"mk{x}")
                nc.scalar.activation(MKT.rearrange("p (b n) -> p b n", b=2), PS[:, s:s + 2, :],
                                     ACT.Copy).then_inc(job_read["act"].up(), 1)
            return pe_part, act_part

        def free_a(sp):
            sp.wait_ge(sig("query_rows_saved").sem, 16)
            sp.wait_ge(sig("y_ready").sem, 4)

        memory_samples("A", 0, 0, 0, 0, 4, 10, 0, free_a)
        memA_pe, memA_act = memory_jobs("A", 0, lambda h: h * 6 + 2, lambda h: h * 6 + 3, 0)

        def sample_memory_out(q_tile, z_tile, stride_q, stride_z, reader):
            def finish(ps):
                nc.vector.tensor_tensor(
                    cols4(q_tile, stride_q, T, W), ps.rearrange("p (h b) -> p h b", h=H),
                    cols4(z_tile, stride_z, T, W), ALU.mult).then_inc(job_read["dve"].up(), 1)
            return finish

        def load_memory_kv(sp, l):
            sp.dma_start(MKV, o["memkv_p"][l, 0].rearrange("(t p) x h d -> p t (x h d)", p=P))\
                .then_inc(sig("memory_loaded").sem, 16)

        def stage4_sp(sp):
            for n in ("qmA0", "qmA1", "qmA2"):
                load_item(sp, n)
            sp.wait_ge(sig("y_ready").sem, 4)
            sp.wait_ge(sig("memkv_saved").sem, 64)
            load_memory_kv(sp, 0)
            for n in ("qmA3", "zmA0", "zmA1", "zmA2", "zmA3"):
                load_item(sp, n)
            for n in range(3):
                load_item(sp, f"outA{n}")
            samples_sp(sp, "A")

        def stage4_pool(pool):
            for h in range(H):
                scale_item(pool, f"qmA{h}")
            for h in range(H):
                scale_item(pool, f"zmA{h}")
            samples_pool(pool, "A")

        def stage4_pe(pe):
            memA_pe(pe)
            attend_pe(pe, "memA")
            samples_pe(pe, "A")

        def stage4_act(act):
            act.wait_ge(job_done.sem, done("var3"))
            memA_act(act)
            attend_act(act, "memA")
            samples_act(act, "A")

        def stage4_dve(dve):
            dve.wait_ge(*read_of("zmA3"))
            attend_dve(dve, "memA")
            samples_scores_dve(dve, "A")
            samples_dve(dve, "A", sample_memory_out(2, 3, 6, 6, "A"))

        def xt5(kt):
            return big((kt // 2) * 6 + 4 + kt % 2)

        def out_pe(pe, x, src, kts):
            for n in range(KT):
                if n == 0:
                    pe.wait_ge(*read_of(f"so{x}"))
                pe_proj(pe, f"out{x}{n}", src, kts=kts)
            norm_pe(pe, f"post{x}")

        def out_act(act, x):
            for n in range(KT):
                act.wait_ge(job_done.sem, done(f"out{x}{n}"))
                nc.scalar.activation(seg3(ht(n)), slot3(f"out{x}{n}"), ACT.Copy).then_inc(job_read["act"].up(), 1)
            act.wait_ge(*read_of(f"out{x}7"))
            norm_act(act, f"post{x}", ht)

        def out_dve(dve, x, l, xt, done):
            norm_dve(dve, f"post{x}")
            dve.wait_ge(sig(f"x{x}_reloaded").sem, 16 * KT)
            for kt in range(KT):
                nc.vector.scalar_tensor_tensor(out=ht(kt), in0=ht(kt), scalar=vec(ROW_GPOST + l, kt),
                                               in1=wk(7), op0=ALU.mult, op1=ALU.mult).then_inc(step.up(), 1)
                dve.wait_ge(step.sem, step.n)
                nc.vector.tensor_tensor(xt(kt), ht(kt), xt(kt), ALU.add).then_inc(done.up(), 1)

        def ya_src(kt, lo, hi):
            return big((kt // 2) * 6 + kt % 2, lo, hi) if kt < KT else big((kt - KT) * 6 + 2, lo, hi)

        def stage5_sp(sp):
            for n in range(3, KT):
                load_item(sp, f"outA{n}")
            sp.wait_ge(job_done.sem, done("soA"))
            for kt in range(KT):
                sp.dma_start(xt5(kt), xt_d[kt]).then_inc(sig("xA_reloaded").sem, 16)

        def stage5_pe(pe):
            out_pe(pe, "A", ya_src, 12)
            norm_pe(pe, "normB")

        def stage5_act(act):
            out_act(act, "A")
            norm_act(act, "normB", xt5, src_ready=lambda kt: act.wait_ge(sig("x1_ready").sem, kt + 1))
            act.wait_ge(sig("xA_reloaded").sem, 16 * KT)
            for kt in range(KT):
                act.dma_start(xt_d[kt], xt5(kt)).then_inc(sig("x1_saved").sem, 16)

        def stage5_dve(dve):
            out_dve(dve, "A", 0, xt5, sig("x1_ready"))
            norm_dve(dve, "normB")
            for kt in range(KT):
                nc.vector.tensor_tensor(ht(kt), xt5(kt), wk(7), ALU.mult).then_inc(sig("hb_ready").up(), 1)

        COS, SIN = TRIG[:, 0:W], TRIG[:, W:2 * W]
        VN = WK[:, 4096:8192].rearrange("p (i n) -> p i n", i=8)
        GSTAT = WK[:, 8192:8320]
        KN = [big(20, 0, 512), big(21, 0, 512)]
        OWN = [7], [1, 3, 5, 7], list(range(8))

        def perm(ap, d):
            return ap.rearrange("p (r j) -> p j r", r=d)

        def natural(ap, d):
            return ap.rearrange("p (j r) -> p j r", r=d)

        def k_tile(h):
            return 12 + h

        def v_tile(h):
            return 16 + h

        def group_attention(g):
            def nk(i):
                return 2 * P if (g == 0 and i > 0) or (g == 1 and i % 2 == 1) else P

            def mask(i):
                if g == 2:
                    return BFC[:, M_PAIR:M_PAIR + 2 * P]
                both = BFC[:, M_BAND:M_BAND + 4 * P]
                return both if nk(i) == 2 * P else both.rearrange("p (x n) -> p x n", x=2)[:, :, P:2 * P]

            def out(i, ps):
                at = g * 4
                dst = BIG[:, :].rearrange("p (i w) -> p i w", w=W)[:, at:at + 4, i * P:(i + 1) * P]
                return nc.vector.tensor_copy(dst, ps)

            attention(f"win{g}", 8 + 8 * g,
                      q=lambda h, i: big(4 * g + h, i * P, (i + 1) * P),
                      k=lambda h, i: big(k_tile(h), (i + 1) * P - nk(i), (i + 1) * P), nk=nk, mask=mask,
                      v=lambda h, t, i: VN[:, i + 1 - nk(i) // P + t, h * P:(h + 1) * P],
                      out=out, p=lambda u: WK[:, (u % 2) * D:(u % 2 + 1) * D],
                      pt=lambda u: WK[:, (2 + u % 2) * D:(3 + u % 2) * D],
                      stat=(GSTAT[:, 0:32], GSTAT[:, 32:64], GSTAT[:, 96:128]))

        for g in range(3):
            group_attention(g)

        def group_names(g):
            return [f"k{g}{h}" for h in range(H)] + [f"v{g}{h}" for h in range(H)] + [f"q{g}{h}" for h in range(H)]

        def stage6_sp(sp):
            for n in group_names(0)[:3]:
                load_item(sp, n)
            sp.wait_ge(sig("nm_saved").sem, 16 * 8)
            sp.wait_ge(job_done.sem, done("so" + "A"))
            sp.dma_start(TRIG[:, :], a["c_trig"]).then_inc(sig("layer_b_constants").sem, 16)
            sp.dma_start(MASKF, a["c_masks"]).then_inc(sig("layer_b_constants").sem, 16)
            for g in range(3):
                nxt = group_names(g + 1) if g < 2 else [f"zgB{h}" for h in range(H)]
                for n in group_names(g)[3:] + nxt[:3]:
                    load_item(sp, n)

        def stage6_pool(pool):
            for n in group_names(0)[:3]:
                scale_item(pool, n)
            pool.wait_ge(sig("layer_b_constants").sem, 32)
            nc.gpsimd.tensor_copy(BFC, MASKF).then_inc(sig("masks_cast").up(), 1)
            pool.wait_ge(sig("x1_saved").sem, 16 * KT)
            for g, d in enumerate(STRIDES):
                nxt = group_names(g + 1) if g < 2 else [f"zgB{h}" for h in range(H)]
                ahead = group_names(g)[3:] + nxt[:3]
                for x in range(3):
                    for h in range(H):
                        move(pool, g, d, x, h)
                        scale_item(pool, ahead[x * H + h])

        def move(pool, g, d, x, h):
            n = g * 8 + (h if x == 0 else H + h)
            if x == 1:
                pool.wait_ge(*read_of(f"v{g}{h}"))
                dst, src = big(v_tile(h)), big(20 + h)
                nc.gpsimd.tensor_copy(KVS[:, g, 1, h * NS:(h + 1) * NS], src[:, T:W])
                nc.gpsimd.tensor_copy(perm(dst[:, 0:T], d), natural(src[:, 0:T], d)).then_inc(sig("values_moved").up(), 1)
                return
            tmp = 20 + 2 * (n % 2)
            pool.wait_ge(*read_of(f"{'kvq'[x]}{g}{h}"))
            dst = big(k_tile(h)) if x == 0 else big(4 * g + h)
            tail = KVS[:, g, 0, h * NS:(h + 1) * NS] if x == 0 else dst[:, T:W]
            nc.gpsimd.tensor_tensor(tail, big(tmp, T, W), big(tmp + 1, T, W), ALU.add)
            if x == 0 and g > 0:
                pool.wait_ge(sig("out_read").sem, 8 + 8 * g)
            nc.gpsimd.tensor_tensor(perm(dst[:, 0:T], d), natural(big(tmp, 0, T), d),
                                    natural(big(tmp + 1, 0, T), d), ALU.add).then_inc(sig("rotated").up(), 1)

        def rotate(dve, g, x, h):
            name = f"{'kvq'[x]}{g}{h}"
            n = g * 8 + (h if x == 0 else H + h)
            tmp = 20 + 2 * (n % 2)
            if n >= 2:
                dve.wait_ge(sig("rotated").sem, n - 1)
            if x == 2 and h < 2:
                dve.wait_ge(sig("values_moved").sem, g * 4 + 4)
            if x == 0 and h == 0 and g > 0:
                dve.wait_ge(sig("window_rows_stored").sem, 16 * (0, 2, 10)[g])
                dve.wait_ge(sig("lse_saved").sem, 16 * g)
            dve.wait_ge(job_done.sem, done(name))
            s = slot_of(name)
            nc.vector.tensor_tensor(seg3(big(tmp)), slot3(name), seg3(COS), ALU.mult)
            last = None
            for lo, hi in ((0, 64), (64, 0)):
                last = nc.vector.tensor_tensor(seg3(big(tmp + 1))[hi:hi + 64], PS[lo:lo + 64, s:s + 3, 0:SEG],
                                               seg3(SIN)[lo:lo + 64], ALU.mult)
            last.then_inc(job_read["dve"].up(), 1)

        def stage6_dve(dve):
            dve.wait_ge(sig("layer_b_constants").sem, 32)
            dve.wait_ge(sig("x1_saved").sem, 16 * KT)
            for g in range(3):
                for x in (0, 2):
                    for h in range(H):
                        rotate(dve, g, x, h)
                attend_dve(dve, f"win{g}")
                dve.wait_ge(sig("log_sums").sem, g + 1)
                nc.vector.tensor_tensor(GSTAT[:, 64:96], GSTAT[:, 64:96], GSTAT[:, 0:32],
                                        ALU.subtract).then_inc(sig("lse_ready").up(), 1)

        def stage6_pe(pe):
            pe.wait_ge(sig("hb_ready").sem, KT)
            for g in range(3):
                for n in group_names(g):
                    pe_proj(pe, n, ht)
                pe.wait_ge(*read_of(f"q{g}3"))
                for i in range(8):
                    u = 8 * g + i
                    if i == 0:
                        pe.wait_ge(sig("values_moved").sem, 4 * g + 4)
                        pe.wait_ge(sig("rotated").sem, 8 * g + 8)
                    if i >= 2:
                        pe.wait_ge(sig("rows_copied").sem, u - 1)
                    b = 2 * (i % 2)
                    for h in range(H):
                        last = nc.tensor.transpose(PS[:, b, h * P:(h + 1) * P], big(v_tile(h), i * P, (i + 1) * P),
                                                   ident)
                    if i in OWN[g]:
                        for h in range(H):
                            last = nc.tensor.transpose(PS[:, b + 1, h * P:(h + 1) * P],
                                                       big(k_tile(h), i * P, (i + 1) * P), ident)
                    last.then_inc(sig("rows_turned").up(), 1)
                pe.wait_ge(sig("rows_copied").sem, 8 * g + 8)
                if g == 0:
                    pe.wait_ge(sig("masks_cast").sem, 1)
                attend_pe(pe, f"win{g}")
                pe.wait_ge(*slot_free(f"lse{g}"))
                pe.wait_ge(sig("lse_ready").sem, g + 1)
                nc.tensor.transpose(PS[0:HP, slot_of(f"lse{g}"), 0:P], GSTAT[:, 64:96], ident).then_inc(job_done.up(), 1)

        def window_rows(g, i, x, part):
            w = o[f"win{g}_p"][0].rearrange("(j r) x h d -> x r j (h d)", r=STRIDES[g])[x]
            if g == 0:
                return w[0]
            if g == 1:
                return w[i // 2]
            return w[2 * i + part]

        def stage6_act(act):
            def evac_v(g, h):
                act.wait_ge(job_done.sem, done(f"v{g}{h}"))
                if h == 0:
                    act.wait_ge(sig("rotated").sem, 8 * g + 4)
                nc.scalar.activation(seg3(big(20 + h)), slot3(f"v{g}{h}"), ACT.Copy).then_inc(job_read["act"].up(), 1)

            stored = sig("window_rows_stored")
            for g in range(3):
                for h in range(H):
                    evac_v(g, h)
                kn = 0
                act.wait_ge(sig("rotated").sem, 8 * g + 8)
                for i in range(8):
                    u = 8 * g + i
                    act.wait_ge(sig("rows_turned").sem, u + 1)
                    b = 2 * (i % 2)
                    ins = nc.scalar.activation(VN[:, i, :], PS[:, b, :], ACT.Copy)
                    if i in OWN[g]:
                        if kn >= 2:
                            act.wait_ge(stored.sem, stored.n)
                        ins = nc.scalar.activation(KN[kn % 2], PS[:, b + 1, :], ACT.Copy)
                    ins.then_inc(sig("rows_copied").up(), 1)
                    if i in OWN[g]:
                        act.wait_ge(sig("rows_copied").sem, sig("rows_copied").n)
                        parts = 2 if g == 2 else 1
                        n = P // parts
                        for x, src in ((0, KN[kn % 2]), (1, VN[:, i, :])):
                            for part in range(parts):
                                act.dma_start(window_rows(g, i, x, part),
                                              src[part * n:(part + 1) * n, :]).then_inc(stored.up(16), 16)
                        kn += 1
                attend_act(act, f"win{g}")
                nc.scalar.activation(GSTAT[:, 64:96], GSTAT[:, 32:64], ACT.Ln).then_inc(sig("log_sums").up(), 1)
                rows = big(23, 0, P)[0:HP, :]
                act.wait_ge(job_done.sem, done(f"lse{g}"))
                nc.scalar.activation(rows, PS[0:HP, slot_of(f"lse{g}"), 0:P], ACT.Copy).then_inc(job_read["act"].up(), 1)
                act.wait_ge(*read_of(f"lse{g}"))
                act.dma_start(ls_d[g].rearrange("i h t -> (i h) t"), rows).then_inc(sig("lse_saved").sem, 16)
                act.wait_ge(stored.sem, stored.n)
                act.wait_ge(sig("lse_saved").sem, 16 * (g + 1))

        def lrow(i, lo=0, hi=T):
            return WK[0:H, i * WT + lo:i * WT + hi]

        SQB = XTRA[:, 1600:1696].rearrange("p (g n) -> p g n", g=3)
        RQ = WK[32:64, 0:9 * P]
        wins = [a[f"cache_win{g}"].rearrange("b (r d) x h e -> b r d x (h e)", d=STRIDES[g])[:, :, 0]
                for g in range(3)]

        def free_d(sp):
            sp.wait_ge(sig("query_rows_saved_d").sem, 48)
            sp.wait_ge(sig("rotated").sem, 24)

        samples("D", 3, 16, key=lambda b, t: wins[t][b, :, 0, :], value=lambda b, t: wins[t][b, :, 1, :],
                query=lambda b, t: qs_d[2 + t].rearrange("(h b) d -> b h d", b=NS)[b],
                tiles=[TRIG[:, 512 * n:512 * (n + 1)] for n in range(4)],
                queries=[WK[:, 6 * WT + 512 * n:6 * WT + 512 * (n + 1)] for n in range(2)],
                prods=[WK[:, 7 * WT + 512 * n:7 * WT + 512 * (n + 1)] for n in range(2)],
                misc=XTRA[:, 1696:3072], free=free_d,
                new=(lambda t: cols4(4 * t, 1, T, W), lambda t: KVS[:, t, 0, :], lambda t: KVS[:, t, 1, :]))
        SMP["D"].update(order=1, first_load=32)

        def free_b(sp):
            sp.wait_ge(sig("query_rows_saved").sem, 32)

        memory_samples("B", 1, 40, 2, 80, 4, 6, 1, free_b)
        memB_pe, memB_act = memory_jobs("B", 1, lambda h: 16 + h, lambda h: 20 + h, 0)

        def stage7_sp(sp):
            load_item(sp, "zgB3")
            for n in ("qmB0", "qmB1"):
                load_item(sp, n)
            for g in range(3):
                sp.wait_ge(sig("lse_saved").sem, 16 * 3)
                sp.dma_start(lrow(g).rearrange("h (i t) -> h i t", i=8), ls_d[g].rearrange("i h t -> h i t"))\
                    .then_inc(sig("lse_loaded").sem, 16)
            samples_sp(sp, "D")
            for n in ("qmB2", "qmB3", "zmB0", "zmB1", "zmB2", "zmB3"):
                load_item(sp, n)
            sp.wait_ge(job_done.sem, done("soD"))
            sp.wait_ge(*read_of("wb3_2"))
            load_memory_kv(sp, 1)
            for n in range(3):
                load_item(sp, f"outB{n}")
            samples_sp(sp, "B")
            for n in range(3, KT):
                load_item(sp, f"outB{n}")
            sp.wait_ge(sig("yd_ready").sem, 4)
            sp.wait_ge(job_done.sem, done("soB"))
            for kt in range(KT):
                sp.dma_start(big(8 + kt), xt_d[kt]).then_inc(sig("xB_reloaded").sem, 16)

        def stage7_pool(pool):
            scale_item(pool, "zgB3"), scale_item(pool, "qmB0"), scale_item(pool, "qmB1")
            samples_pool(pool, "D")
            for n in ("qmB2", "qmB3", "zmB0", "zmB1", "zmB2", "zmB3"):
                scale_item(pool, n)
            samples_pool(pool, "B")

        def stage7_pe(pe):
            pe.wait_ge(sig("pair_query_cols").sem, 1)
            query_rows_pe(pe, "qsD", [SQB[:, g, :] for g in range(3)] + [KVS[:, g, x, :] for g in range(3)
                                                                       for x in range(2)])
            for h in range(H):
                pe_proj(pe, f"zgB{h}", ht)
            for h in range(H):
                for g in range(3):
                    name = f"wb{h}_{g}"
                    pe.wait_ge(*slot_free(name))
                    if h == 0 and g == 0:
                        pe.wait_ge(sig("weights_ready").sem, 1)
                    s = slot_of(name)
                    for b in range(2):
                        last = nc.tensor.matmul(PS[:, s + b, :], CST[0:H, C_SEL + h * P:C_SEL + (h + 1) * P],
                                                lrow((0, 3, 4)[g], b * 512, (b + 1) * 512), start=True, stop=True)
                    last.then_inc(job_done.up(), 1)
            samples_pe(pe, "D")
            pe.wait_ge(sig("yd_ready").sem, 4)
            memB_pe(pe)
            attend_pe(pe, "memB")
            samples_pe(pe, "B")
            out_pe(pe, "B", lambda kt, lo, hi: big(kt if kt < H else 12 + kt, lo, hi), KT)
            for t in range(9):
                name = f"yt{t}"
                pe.wait_ge(*slot_free(name))
                s = slot_of(name)
                if t == 0:
                    pe.wait_ge(sig("y_out_ready").sem, KT)
                n = P if t < 8 else NS
                for kt in range(KT):
                    last = nc.tensor.transpose(PS[0:n, s + kt // 4, (kt % 4) * P:(kt % 4 + 1) * P],
                                               big(8 + kt, t * P, t * P + n), ident)
                last.then_inc(job_done.up(), 1)

        def stage7_act(act):
            nc.scalar.activation(
                SQB.rearrange("p g (h b) -> p (g h) b", h=H),
                BIG[:, :].rearrange("p (i w) -> p i w", w=W)[:, 0:12, T:W], ACT.Copy).then_inc(sig("pair_query_cols").up(), 1)
            act.wait_ge(job_done.sem, done("qsD"))
            s = slot_of("qsD")
            nc.scalar.activation(RQ[:, 0:8 * P].rearrange("p (b n) -> p b n", b=2), PS[0:HP, s:s + 2, :], ACT.Copy)
            nc.scalar.activation(RQ[:, 8 * P:9 * P], PS[0:HP, s + 2, 0:P], ACT.Copy).then_inc(job_read["act"].up(), 1)
            act.wait_ge(*read_of("qsD"))
            for g in range(3):
                act.dma_start(qs_d[2 + g], RQ[:, g * P:(g + 1) * P]).then_inc(sig("query_rows_saved_d").sem, 16)
            for g in range(3):
                for x in range(2):
                    at = (3 + 2 * g + x) * P
                    for h in range(H):
                        act.dma_start(o[f"win{g}_s"][:, 0, x, h, :], RQ[h * NS:(h + 1) * NS, at:at + P])\
                            .then_inc(sig("new_rows_saved").sem, 16)
            for h in range(H):
                act.wait_ge(job_done.sem, done(f"zgB{h}"))
                nc.scalar.activation(seg3(big(12 + h)), slot3(f"zgB{h}"), ACT.Silu).then_inc(job_read["act"].up(), 1)
            act.wait_ge(sig("lse_shifted").sem, 1)
            nc.scalar.activation(lrow(0), lrow(0), ACT.Exp).then_inc(sig("lse_exp").up(), 1)
            nc.scalar.activation(WK[0:H, 3 * WT:5 * WT].rearrange("h (i n) -> h i n", i=2)[:, :, 0:T],
                                 WK[0:H, 3 * WT:5 * WT].rearrange("h (i n) -> h i n", i=2)[:, :, 0:T],
                                 ACT.Exp).then_inc(sig("lse_exp").up(), 1)
            samples_act(act, "D")
            memB_act(act)
            attend_act(act, "memB")
            samples_act(act, "B")
            out_act(act, "B")
            yo = sig("y_rows_copied")
            for t in range(9):
                n = P if t < 8 else NS
                name = f"yt{t}"
                act.wait_ge(job_done.sem, done(name))
                if t >= 2:
                    act.wait_ge(sig(f"y{t % 2}_saved").sem, 16 * (t // 2))
                s = slot_of(name)
                row = WK[0:n, (t % 2) * WT:(t % 2) * WT + D]
                nc.scalar.activation(row.rearrange("p (b n) -> p b n", b=2),
                                     PS[0:n, s:s + 2, :], ACT.Copy).then_inc(job_read["act"].up(), 1)
                act.wait_ge(*read_of(name))
                dst = o["y_prompt"][0, t * P:(t + 1) * P, :] if t < 8 else o["y_sample"].rearrange("b t d -> (b t) d")
                act.dma_start(dst, row).then_inc(sig(f"y{t % 2}_saved").sem, 16)
            act.wait_ge(sig("y0_saved").sem, 16 * 5)
            act.wait_ge(sig("y1_saved").sem, 16 * 4)
            act.wait_ge(sig("new_rows_saved").sem, 16 * 24)
            act.wait_ge(sig("window_rows_stored").sem, sig("window_rows_stored").n)

        def stage7_dve(dve):
            def do(ins):
                ins.then_inc(step.up(), 1)
                dve.wait_ge(step.sem, step.n)

            dve.wait_ge(sig("lse_loaded").sem, 16 * 3)
            dve.wait_ge(sig("new_rows_saved").sem, 16 * 24)
            dve.wait_ge(sig("query_rows_saved_d").sem, 48)
            l0 = lrow(0)

            def tok(i, d):
                return lrow(i).rearrange("h (r j) -> h j r", r=d)

            def nat(i, d):
                return lrow(i).rearrange("h (j r) -> h j r", r=d)

            mx = 5
            do(nc.vector.tensor_tensor(nat(mx, 4), nat(0, 4), tok(1, 4), ALU.max))
            do(nc.vector.tensor_tensor(nat(mx, 16), nat(mx, 16), tok(2, 16), ALU.max))
            nc.vector.tensor_tensor(lrow(0), lrow(0), lrow(mx), ALU.subtract)
            nc.vector.tensor_tensor(nat(3, 4), tok(1, 4), nat(mx, 4), ALU.subtract)
            nc.vector.tensor_tensor(nat(4, 16), tok(2, 16), nat(mx, 16), ALU.subtract).then_inc(sig("lse_shifted").up(), 1)
            samples_scores_dve(dve, "D")
            dve.wait_ge(sig("lse_exp").sem, 2)
            do(nc.vector.tensor_tensor(lrow(1), lrow(0), lrow(3), ALU.add))
            do(nc.vector.tensor_tensor(lrow(1), lrow(1), lrow(4), ALU.add))
            do(nc.vector.reciprocal(lrow(1), lrow(1)))
            for i in (0, 3, 4):
                ins = nc.vector.tensor_tensor(lrow(i), lrow(i), lrow(1), ALU.mult)
            ins.then_inc(sig("weights_ready").up(), 1)
            for h in range(H):
                for g, d in enumerate(STRIDES):
                    name = f"wb{h}_{g}"
                    dve.wait_ge(job_done.sem, done(name))
                    s = slot_of(name)
                    x = perm(big(4 * g + h, 0, T), d)
                    nc.vector.tensor_tensor(
                        x, x, natural(PS[:, s:s + 2, :].rearrange("p b n -> p (b n)"), d), ALU.mult).then_inc(job_read["dve"].up(), 1)
                dve.wait_ge(*read_of(f"wb{h}_2"))
                y = big(h, 0, T)
                for g, d in ((1, 4), (2, 16)):
                    do(nc.vector.tensor_tensor(natural(y, d), natural(y, d), perm(big(4 * g + h, 0, T), d), ALU.add))

            def windows_out(ps):
                m = SMP["D"]["m"]
                y = m["qk"][:, 0:HP]
                t = m["qk"][:, HP:2 * HP]
                nc.vector.tensor_copy(y, ps).then_inc(job_read["dve"].up(), 1)
                for g in range(3):
                    p_new = m["turned"][:, (3 + g) * HP:(4 + g) * HP]
                    if g == 0:
                        dve.wait_ge(*read_of("soD"))
                    do(nc.vector.tensor_tensor(t, p_new, KVS[:, g, 1, :], ALU.mult))
                    do(nc.vector.tensor_tensor(y, y, t, ALU.add))
                do(nc.vector.tensor_copy(cols4(0, 1, T, W), y.rearrange("p (h b) -> p h b", h=H)))
                dve.wait_ge(*read_of("zgB3"))
                for h in range(H):
                    nc.vector.tensor_tensor(big(h), big(h), big(12 + h), ALU.mult).then_inc(sig("yd_ready").up(), 1)

            samples_dve(dve, "D", windows_out)
            dve.wait_ge(*read_of("zmB3"))
            attend_dve(dve, "memB")
            samples_scores_dve(dve, "B")
            samples_dve(dve, "B", sample_memory_out(16, 20, 1, 1, "B"))
            out_dve(dve, "B", 1, lambda kt: big(8 + kt), sig("y_out_ready"))

        with nc.Block() as block:
            @block.sync
            def _(sp):
                stage0_sp(sp)
                stage1_sp(sp)
                gates_sp(sp)
                stage2_end_sp(sp)
                stage3_sp(sp)
                stage4_sp(sp)
                stage5_sp(sp)
                stage6_sp(sp)
                stage7_sp(sp)
                sp.wait_ge(sig("n_saved").sem, 16 * 9)
                sp.wait_ge(s_out.sem, 16)
                sp.wait_ge(sig("x1_saved").sem, 128)
                sp.wait_ge(sig("cs0_saved").sem, 256)
                sp.wait_ge(sig("cs1_saved").sem, 256)
                sp.wait_ge(sig("nm_saved").sem, 128)
                sp.wait_ge(sig("memkv_saved").sem, 64)
                sp.wait_ge(sig("conv_saved").sem, 32)

            @block.gpsimd
            def _(pool):
                stage0_pool(pool)
                stage1_pool(pool)
                stage3_pool(pool)
                stage4_pool(pool)
                stage6_pool(pool)
                stage7_pool(pool)

            @block.scalar
            def _(act):
                stage0_act(act)
                stage1_act(act)
                stage2_act(act)
                stage2_end_act(act)
                stage3_act(act)
                stage4_act(act)
                stage5_act(act)
                stage6_act(act)
                stage7_act(act)
                for b in range(2):
                    act.wait_ge(sig(f"c{b}_saved").sem, 32)

            @block.vector
            def _(dve):
                stage0_dve(dve)
                stage1_dve(dve)
                stage2_dve(dve)
                stage3_dve(dve)
                stage4_dve(dve)
                stage5_dve(dve)
                stage6_dve(dve)
                stage7_dve(dve)

            @block.tensor
            def _(pe):
                stage0_pe(pe)
                stage1_pe(pe)
                stage2_pe(pe)
                stage2_end_pe(pe)
                stage3_pe(pe)
                stage4_pe(pe)
                stage5_pe(pe)
                stage6_pe(pe)
                stage7_pe(pe)


_INS = ['x_prompt', 'x_sample', 'mem_prompt', 'state_conv', 'state_C', 'state_n', 'state_m', 'cache_win0',
        'cache_win1', 'cache_win2', 'cache_mem_kv', 'g_pre', 'g_post', 'w_in_a', 'conv_w_a', 'conv_b_a', 'w_q_a',
        'w_k_a', 'w_v_a', 'w_if_a', 'b_if_a', 'g_hn_a', 'skip_a', 'w_out_a', 'g_kv', 'w_kv_b', 'w_in_b',
        'w_out_b', 'w_mkv']
_OUTS = {'y_prompt': (1, 1024, 1024), 'y_sample': (8, 1, 1024), 'conv_p': (1, 1, 3, 1024),
         'C_p': (1, 1, 4, 256, 256), 'n_p': (1, 1, 4, 256), 'm_p': (1, 1, 4), 'win0_p': (1, 128, 2, 4, 128),
         'win1_p': (1, 512, 2, 4, 128), 'win2_p': (1, 1024, 2, 4, 128), 'memkv_p': (2, 1, 256, 2, 4, 128),
         'conv_s': (1, 8, 3, 1024), 'C_s': (1, 8, 4, 256, 256), 'n_s': (1, 8, 4, 256), 'm_s': (1, 8, 4),
         'win0_s': (8, 1, 2, 4, 128), 'win1_s': (8, 1, 2, 4, 128), 'win2_s': (8, 1, 2, 4, 128)}


def constants():
    import numpy as np
    c = np.zeros((P, C_END), np.float32)
    i, j = np.arange(P)[:, None], np.arange(P)[None, :]
    c[:, C_ID:C_ID + P] = i == j
    c[:, C_ONE:C_ONE + P] = 1.0
    c[:, C_AVG_D:C_AVG_D + P] = 1.0 / D
    c[:, C_AVG_H:C_AVG_H + P] = 1.0 / 256
    c[:, C_CAUSAL:C_CAUSAL + P] = i <= j
    prev = np.where(j >= i, 0.0, NEG)
    own = np.where(j <= i, 0.0, NEG)
    pair = np.where((j <= i) & (i // 64 == j // 64), 0.0, NEG)
    masks = np.concatenate([i == j, prev, own, prev, own, pair, pair], 1).astype(np.float32)
    for h in range(H):
        c[h, C_SEL + h * P:C_SEL + (h + 1) * P] = 1.0
    half = P // 2
    inv = (10000.0 ** (-np.arange(half) / half)).astype(np.float32)
    pos = np.concatenate([np.arange(T, dtype=np.float32), np.full(NS, 2048, np.float32)])
    ang = (inv[:, None] * pos[None, :]).astype(np.float32)
    cos, sin = np.cos(ang).astype(np.float32), np.sin(ang).astype(np.float32)
    trig = np.concatenate([np.concatenate([cos, cos], 0), np.concatenate([sin, -sin], 0)], 1)
    return {'c_block': c, 'c_masks': masks, 'c_trig': trig}


def kernel(**inputs):
    import numpy as _np
    import concourse.bacc as _bacc
    from concourse.bass_utils import run_bass_kernel_spmd as _run

    nc = _bacc.Bacc("TRN2", target_bir_lowering=False, num_devices=1)
    arrays, a, o = {}, {}, {}
    for name, value in [(n, _np.ascontiguousarray(inputs[n])) for n in _INS] + list(constants().items()):
        arrays[f"in_{name}"] = value
        a[name] = nc.dram_tensor(f"in_{name}", value.shape, mybir.dt.from_np(value.dtype), kind="ExternalInput").ap()
    for name, shape in _OUTS.items():
        o[name] = nc.dram_tensor(f"out_{name}", shape, F32, kind="ExternalOutput").ap()
    build(nc, a, o)
    r = _run(nc, [arrays], core_ids=[0])
    return tuple(r.results[0][f"out_{name}"] for name in _OUTS)
```

```python
from contextlib import ExitStack

import concourse.bass as bass
from concourse import mybir

F32 = mybir.dt.float32
BF16 = mybir.dt.bfloat16
ALU = mybir.AluOpType
ACT = mybir.ActivationFunctionType
AX = mybir.AxisListType

P = 128
T = 1024
NS = 8
W = T + NS
SEG = W // 3
D = 1024
KT = D // P
H = 4
HP = H * NS
CH = 128
NCH = T // CH
NMEM = 256
EPS = 1e-6
SCALE = 128 ** -0.5
STRIDES = (1, 4, 16)
NEG = -1e30

ROW_STATE, ROW_CW, ROW_CB, ROW_GPRE, ROW_GPOST, ROW_GHN, ROW_SKIP, ROW_GKV, NROW = 0, 24, 28, 29, 31, 33, 34, 35, 36

C_ID, C_ONE, C_AVG_D, C_AVG_H, C_CAUSAL, C_SEL = 0, 128, 256, 384, 512, 640
C_END = C_SEL + H * P
M_ID, M_BAND, M_PAIR, M_END = 0, 128, 640, 896


class Signal:

    def __init__(self, sem):
        self.sem, self.n = sem, 0

    def up(self, by=1):
        self.n += by
        return self.sem


def build(nc, a, o):
    with ExitStack() as ctx:
        def sb(name, shape, dt=F32):
            return ctx.enter_context(nc.sbuf_tensor(name, shape, dt))

        signals = {}

        def sig(name):
            if name not in signals:
                signals[name] = Signal(ctx.enter_context(nc.semaphore(name)))
            return signals[name]

        HT = sb("HT", [P, KT * W])
        BIG = sb("BIG", [P, 24 * W])
        WT = 1040
        WK = sb("WK", [P, 8 * WT])
        SLOT = 1536
        NSLOT = 3
        RING = sb("RING", [P, NSLOT * SLOT])
        TRIG = sb("TRIG", [P, 2 * W])
        CST = sb("CST", [P, C_END])
        VEC = sb("VEC", [P, KT, NROW])
        XTRA = sb("XTRA", [P, NCH * 3 * CH])
        RR = XTRA[0:H, :].rearrange("h (c x t) -> h c x t", c=NCH, x=3)
        MASKF = XTRA[:, 0:M_END]
        BFC = XTRA[:, M_END:M_END + M_END // 2].bitcast(BF16)
        KVS = XTRA[:, 1408:1600].rearrange("p (g x n) -> p g x n", g=3, x=2)
        SM = sb("SM", [P, 360])
        PS = ctx.enter_context(nc.psum_tensor("PS", [P, 8, 512], F32))

        def dram(name, shape):
            return nc.dram_tensor(name, shape, F32, kind="Internal").ap()

        xt_d = dram("xt_scratch", [KT, P, W])
        xc_d = dram("xc_scratch", [KT, P, W])
        sg_d = dram("sample_gates", [2, H, NS])
        qw_d = dram("sample_q_and_weighted_k", [HP, 512])
        cf_d = dram("sample_coef", [HP, 3])
        qs_d = dram("sample_query", [5, HP, P])
        ls_d = dram("window_lse", [3, 8, H, P])

        ident = CST[:, C_ID:C_ID + P]
        ones = CST[:, C_ONE:C_ONE + P]
        avg_d = CST[:, C_AVG_D:C_AVG_D + P]
        avg_h = CST[:, C_AVG_H:C_AVG_H + P]
        causal = CST[:, C_CAUSAL:C_CAUSAL + P]

        def big(i, lo=0, hi=W):
            return BIG[:, i * W + lo:i * W + hi]

        def ht(i, lo=0, hi=W):
            return HT[:, i * W + lo:i * W + hi]

        def wk(i, lo=0, hi=W):
            return WK[:, i * WT + lo:i * WT + hi]

        def seg3(ap):
            return ap.rearrange("p (b n) -> p b n", b=3)

        def vec(row, kt):
            return VEC[:, kt, row:row + 1]

        QKVN = XTRA[64:96, 0:768]
        SN, TMP32, WK32, NN32 = (XTRA[64:96, at:at + 256] for at in (768, 1024, 1280, 1536))
        SC32 = XTRA[64:96, 1792:1824]

        SQC = WK[:, 7 * WT:7 * WT + 6 * HP].rearrange("p (i h b) -> p i h b", i=6, h=H)

        ACOL = SM[:, 0:32].rearrange("p (c h) -> p c h", h=H)
        UT = SM[:, 32:120].rearrange("p (j n) -> p j n", n=11)
        MPV = SM[0:H, 120:129]
        BIAS = SM[0:H, 129:131]
        EPSC = SM[:, 131:132]
        COEF = SM[:, 132:132 + 96].rearrange("p (i k) -> p i k", k=3)
        CQ = SM[:, 228:292].rearrange("p (v i) -> p v i", v=2)
        HSS = SM[:, 312:344]

        jobs, items = [], []

        def job(name, reader="act"):
            jobs.append((name, reader))

        def item(name, loads, scale_row=None, release=None, kts=KT):
            items.append(dict(name=name, loads=loads, scale=scale_row, release=release, kts=kts))

        def tile_of(w, n0, kts=KT):
            return w[:, n0:n0 + P].rearrange("(k p) n -> p k n", p=P), kts * P

        def proj(name, w, n0, scale_row=None, reader="act", kts=KT):
            job(name, reader)
            item(name, [tile_of(w, n0, kts)], scale_row, ("job", name), kts)

        w_in_a, w_in_b, w_kv = a["w_in_a"][0], a["w_in_b"][0], a["w_kv_b"]
        for ft in range(KT):
            job(f"xt{ft}")
        for l in range(2):
            for kt in range(KT):
                item(f"mkv{l}_{kt}", [(a["w_mkv"][l][kt * P:(kt + 1) * P, :], D)], None, ("mkv", l * KT + kt + 1))
        job("norm0")

        def qkv_jobs(h):
            item(f"qkv{h}", [(a[w][0, h].rearrange("(k p) n -> p k n", p=P), 512) for w in ("w_q_a", "w_k_a", "w_v_a")],
                 None, ("job", f"v{h}_1"))
            for x in "qkv":
                for e in range(2):
                    job(f"{x}{h}_{e}")

        def u_jobs(h):
            for e in range(2):
                proj(f"u{2 * h + e}", w_in_a, (2 * h + e) * P)

        u_jobs(0)
        for h in range(H):
            if h + 1 < H:
                u_jobs(h + 1)
            qkv_jobs(h)
        job("gates")
        job("acol")
        job("rows_u")
        job("rows_s")

        def oz_jobs(h, first, part):
            for e in range(2):
                proj(f"{part}{h}_{e}", w_in_a, first + (2 * h + e) * P)

        for h in range(H):
            oz_jobs(h, D, "o")
            if h > 0:
                job(f"var{h - 1}")
            oz_jobs(h, 2 * D, "zg")
            job(f"mean{h}", "dve")
        job("var3")
        def memory_branch_jobs(x, w, first, after_qm=lambda h: None):
            row = None if x == "A" else ROW_GPRE + 1
            for h in range(H):
                proj(f"qm{x}{h}", w, first + h * P, row)
                after_qm(h)
            for h in range(H):
                proj(f"zm{x}{h}", w, first + (H + h) * P, row)
                if h == 0:
                    job(f"qs{x}")
            job(f"ss{x}")
            job(f"mk{x}")
            job(f"sp{x}")

        memory_branch_jobs("A", w_in_a, 3 * D)
        for n in range(KT):
            proj(f"outA{n}", a["w_out_a"][0], n * P, kts=12)
        job("postA")
        job("normB")
        for g in range(3):
            for h in range(H):
                proj(f"k{g}{h}", w_kv, (2 * g * H + h) * P, ROW_GKV, "dve")
            for h in range(H):
                proj(f"v{g}{h}", w_kv, ((2 * g + 1) * H + h) * P, ROW_GKV)
            for h in range(H):
                proj(f"q{g}{h}", w_in_b, (g * H + h) * P, ROW_GPRE + 1, "dve")
            job(f"lse{g}")
        job("qsD")
        for h in range(H):
            proj(f"zgB{h}", w_in_b, (3 * H + h) * P, ROW_GPRE + 1)
        for h in range(H):
            job(f"wb{h}_0", "dve")
            job(f"wb{h}_1", "dve")
            job(f"wb{h}_2", "dve")
        memory_branch_jobs("B", w_in_b, 4 * H * P, lambda h: job(("ssD", "spD")[h]) if h < 2 else None)
        for n in range(KT):
            proj(f"outB{n}", a["w_out_b"][0], n * P)
        job("postB")
        for t in range(9):
            job(f"yt{t}")

        JOB = {name: g for g, (name, _) in enumerate(jobs)}
        ITEM = {it["name"]: n for n, it in enumerate(items)}
        job_done = sig("job_done")
        job_read = {"act": sig("job_read_by_act"), "dve": sig("job_read_by_dve")}

        def slot_of(name):
            return 3 * (JOB[name] % 2)

        def slot3(name):
            s = slot_of(name)
            return PS[:, s:s + 3, 0:SEG]

        def read_count(g):
            r = jobs[g][1]
            return r, sum(1 for _, x in jobs[:g + 1] if x == r)

        def read_of(name):
            r, n = read_count(JOB[name])
            return job_read[r].sem, n

        def slot_free(name):
            r, n = read_count(JOB[name] - 2)
            return job_read[r].sem, n

        def done(name):
            return JOB[name] + 1

        slot_loaded = [sig(f"ring{s}_loaded") for s in range(NSLOT)]
        scaled = sig("weights_scaled")
        loaded_at, n_loaded = [], [0] * NSLOT
        for n, it in enumerate(items):
            n_loaded[n % NSLOT] += 16 * len(it["loads"])
            loaded_at.append(n_loaded[n % NSLOT])
        scaled_at = [sum(1 for x in items[:n + 1] if x["scale"] is not None) for n in range(len(items))]

        def released(n):
            kind, v = items[n]["release"]
            return (job_done.sem, done(v)) if kind == "job" else (sig("memkv_steps").sem, v)

        def load_item(sp, name):
            n = ITEM[name]
            it = items[n]
            if n >= NSLOT:
                sp.wait_ge(*released(n - NSLOT))
            at = (n % NSLOT) * SLOT
            for src, size in it["loads"]:
                dst = RING[:, at:at + size]
                if len(src.shape) == 3:
                    dst = dst.rearrange("p (k n) -> p k n", k=src.shape[1])
                sp.dma_start(dst, src).then_inc(slot_loaded[n % NSLOT].sem, 16)
                at += size

        def load_ahead(act, name):
            load_item(act, items[ITEM[name] + NSLOT]["name"])

        def scale_item(pool, name):
            n = ITEM[name]
            it = items[n]
            pool.wait_ge(slot_loaded[n % NSLOT].sem, loaded_at[n])
            at = (n % NSLOT) * SLOT
            w = RING[:, at:at + D].rearrange("p (k n) -> p k n", k=KT)
            g = VEC[:, :, it["scale"]:it["scale"] + 1].to_broadcast([P, KT, P])
            nc.gpsimd.tensor_tensor(w, w, g, ALU.mult).then_inc(scaled.up(), 1)

        def ring(name):
            at = (ITEM[name] % NSLOT) * SLOT
            return RING[:, at:at + SLOT]

        def weights_of(name):
            n = ITEM[name]
            if items[n]["scale"] is None:
                return slot_loaded[n % NSLOT].sem, loaded_at[n]
            return scaled.sem, scaled_at[n]

        def pe_proj(pe, name, rhs, kts=KT, before=None):
            pe.wait_ge(*slot_free(name))
            pe.wait_ge(*weights_of(name))
            w = ring(name)
            s = slot_of(name)
            for kt in range(kts):
                if before:
                    before(kt)
                for b in range(3):
                    last = nc.tensor.matmul(PS[:, s + b, 0:SEG], w[:, kt * P:(kt + 1) * P],
                                            rhs(kt, b * SEG, (b + 1) * SEG), start=(kt == 0), stop=(kt == kts - 1))
            last.then_inc(job_done.up(), 1)

        XN = BIG[:, 0:8 * D].rearrange("p (t d) -> p t d", t=8)
        MEMN = BIG[:, 8 * D:10 * D].rearrange("p (t d) -> p t d", t=2)
        XS = BIG[0:NS, 10 * D:11 * D]
        PAR = BIG[0:NROW, 11 * D:12 * D]
        MEMT = HT[:, 0:8 * NMEM].rearrange("p (k n) -> p k n", k=KT)

        def xt0(kt, lo=0, hi=W):
            return big(12 + kt, lo, hi)

        WIF = TRIG[:, 0:24 * 36].rearrange("p (i n) -> p i n", i=24)
        s_const, s_x, s_gate_w = sig("constants_loaded"), sig("inputs_loaded"), sig("gate_weights_loaded")
        s_zero = sig("pads_zeroed")
        N_X = 8 + 2 + 1 + 8

        def stage0_sp(sp):
            sp.dma_start(CST[:, :], a["c_block"]).then_inc(s_const.sem, 16)
            for t in range(8):
                sp.dma_start(XN[:, t, :], a["x_prompt"][0, t * P:(t + 1) * P, :]).then_inc(s_x.sem, 16)
            sp.dma_start(MEMN, a["mem_prompt"][0].rearrange("(t p) d -> p t d", p=P)).then_inc(s_x.sem, 16)
            sp.dma_start(XS, a["x_sample"].rearrange("b t d -> (b t) d")).then_inc(s_x.sem, 16)
            sp.dma_start(PAR[ROW_STATE:24, :], a["state_conv"].rearrange("a b r d -> (a b r) d")).then_inc(s_x.sem, 16)
            for row, n, name in ((ROW_CW, 4, "conv_w_a"), (ROW_CB, 1, "conv_b_a"), (ROW_GPRE, 2, "g_pre"),
                                 (ROW_GPOST, 2, "g_post"), (ROW_GHN, 1, "g_hn_a"), (ROW_SKIP, 1, "skip_a")):
                src = a[name]
                if len(src.shape) == 3:
                    src = src[0]
                sp.dma_start(PAR[row:row + n, :], src).then_inc(s_x.sem, 16)
            sp.dma_start(PAR[ROW_GKV:NROW, :], a["g_kv"].rearrange("(a d) -> a d", a=1)).then_inc(s_x.sem, 16)
            for i in range(2):
                sp.dma_start(BIAS[:, i:i + 1], a["b_if_a"][0, i * H:(i + 1) * H].rearrange("(h a) -> h a", a=1))\
                    .then_inc(s_x.sem, 16)
            for l in range(2):
                for kt in range(KT):
                    load_item(sp, f"mkv{l}_{kt}")
                    if l == 0 and kt == 3:
                        sp.wait_ge(s_zero.sem, 1)
                        src = a["w_if_a"][0].rearrange("(i p) n -> p i n", p=P)
                        sp.dma_start(WIF[:, :, 0:H], src[:, :, 0:H]).then_inc(s_gate_w.sem, 16)
                        sp.dma_start(WIF[:, :, 32:36], src[:, :, H:2 * H]).then_inc(s_gate_w.sem, 16)

        INPUTS = 16 * (8 + 1 + 1 + 1 + 6 + 1 + 2)

        def stage0_pool(pool):
            nc.gpsimd.memset(TRIG[:, 0:24 * 36], 0.0).then_inc(s_zero.up(), 1)
            for ub in range(4):
                nc.gpsimd.memset(wk(ub, 0, 3), 0.0).then_inc(s_zero.up(), 1)
            nc.gpsimd.memset(EPSC, EPS).then_inc(s_zero.up(), 1)

        def stage0_pe(pe):
            pe.wait_ge(s_const.sem, 16)
            pe.wait_ge(s_x.sem, INPUTS)
            for ft in range(KT):
                if ft >= 2:
                    pe.wait_ge(*slot_free(f"xt{ft}"))
                s = slot_of(f"xt{ft}")
                c = slice(ft * P, (ft + 1) * P)
                for t in range(8):
                    nc.tensor.transpose(PS[:, s + t // 4, (t % 4) * P:(t % 4 + 1) * P], XN[:, t, c], ident)
                for t in range(2):
                    nc.tensor.transpose(PS[:, s + 2, t * P:(t + 1) * P], MEMN[:, t, c], ident)
                nc.tensor.transpose(PS[:, s + 2, 256:256 + NS], XS[:, c], ident[0:NS, 0:NS])
                last = nc.tensor.transpose(PS[:, s + 2, 264:264 + NROW], PAR[:, c], ident[0:NROW, 0:NROW])
                last.then_inc(job_done.up(), 1)
            pe.wait_ge(*read_of("xt7"))
            for l in range(2):
                for kt in range(KT):
                    pe.wait_ge(*weights_of(f"mkv{l}_{kt}"))
                    w = ring(f"mkv{l}_{kt}")
                    for nt in range(2):
                        for half in range(2):
                            last = nc.tensor.matmul(PS[:, 4 * l + 2 * nt + half, :], MEMT[:, kt, nt * P:(nt + 1) * P],
                                                    w[:, half * 512:(half + 1) * 512],
                                                    start=(kt == 0), stop=(kt == KT - 1))
                    last.then_inc(sig("memkv_steps").up(), 1)
            pe.wait_ge(sig("memkv_read").sem, 4)
            norm_pe(pe, "norm0")

        def stage0_act(act):
            own = sig("xt_copied")
            for ft in range(KT):
                act.wait_ge(job_done.sem, done(f"xt{ft}"))
                s = slot_of(f"xt{ft}")
                if ft == 0:
                    act.wait_ge(s_zero.sem, 6)
                nc.scalar.activation(xt0(ft, 0, T).rearrange("p (b n) -> p b n", b=2), PS[:, s:s + 2, :], ACT.Copy)
                nc.scalar.activation(xt0(ft, T, W), PS[:, s + 2, 256:256 + NS], ACT.Copy).then_inc(own.up(), 1)
                nc.scalar.activation(MEMT[:, ft, :], PS[:, s + 2, 0:256], ACT.Copy)
                nc.scalar.activation(VEC[:, ft, :], PS[:, s + 2, 264:264 + NROW], ACT.Copy).then_inc(job_read["act"].up(), 1)
                act.wait_ge(own.sem, own.n)
                act.dma_start(xt_d[ft], xt0(ft)).then_inc(sig("xt_saved").sem, 16)
            own2 = sig("memkv_read")
            for l in range(2):
                act.wait_ge(sig("memkv_steps").sem, KT * (l + 1))
                for nt in range(2):
                    i = 2 * l + nt
                    dst = BIG[:, i * D:(i + 1) * D]
                    nc.scalar.activation(dst.rearrange("p (b n) -> p b n", b=2),
                                         PS[:, 4 * l + 2 * nt:4 * l + 2 * nt + 2, :], ACT.Copy).then_inc(own2.up(), 1)
                    act.wait_ge(own2.sem, own2.n)
                    act.dma_start(o["memkv_p"][l, 0, nt * P:(nt + 1) * P].rearrange("n a h d -> n (a h d)"), dst)\
                        .then_inc(sig("memkv_saved").sem, 16)
            norm_act(act, "norm0", xt0)

        def norm_act(act, name, src, order=range(KT), src_ready=None):
            for i, kt in enumerate(order):
                if i >= 2:
                    act.wait_ge(sig(f"sq_used_{name}").sem, i - 1)
                if src_ready:
                    src_ready(kt)
                nc.scalar.activation(wk(5 + i % 2), src(kt), ACT.Square).then_inc(sig(f"sq_{name}").up(), 1)
            root_act(act, name)

        def root_act(act, name):
            act.wait_ge(job_done.sem, done(name))
            nc.scalar.activation(seg3(wk(7)), slot3(name), ACT.Ln, bias=EPSC).then_inc(job_read["act"].up(), 1)
            act.wait_ge(*read_of(name))
            nc.scalar.activation(wk(7), wk(7), ACT.Exp, scale=-0.5).then_inc(sig("inverse_root").up(), 1)

        def norm_pe(pe, name):
            pe.wait_ge(*slot_free(name))
            s = slot_of(name)
            for i in range(KT):
                pe.wait_ge(sig(f"sq_{name}").sem, i + 1)
                for b in range(3):
                    last = nc.tensor.matmul(PS[:, s + b, 0:SEG], avg_d, wk(5 + i % 2, b * SEG, (b + 1) * SEG),
                                            start=(i == 0), stop=(i == KT - 1))
                last.then_inc((sig(f"sq_used_{name}") if i < KT - 1 else job_done).up(), 1)

        step = sig("vector_steps")

        def stage0_dve(dve):
            dve.wait_ge(sig("inverse_root").sem, 1)
            for kt in range(KT):
                nc.vector.scalar_tensor_tensor(out=ht(kt), in0=xt0(kt), scalar=vec(ROW_GPRE, kt), in1=wk(7),
                                               op0=ALU.mult, op1=ALU.mult).then_inc(sig("h_ready").up(), 1)

        def ub_of(j):
            return (j // 2 % 2) * 2 + j % 2

        def stage1_sp(sp):
            for h in range(H):
                if h == 0:
                    load_item(sp, "u0"), load_item(sp, "u1")
                if h + 1 < H:
                    load_item(sp, f"u{2 * h + 2}"), load_item(sp, f"u{2 * h + 3}")
                load_item(sp, f"qkv{h}")
            sp.dma_start(o["conv_s"][0, :, 0:2, :], a["state_conv"][0, :, 1:3, :]).then_inc(s_out.sem, 16)

        def stage1_pe(pe):
            pe.wait_ge(sig("h_ready").sem, 1)

            def u(j):
                pe_proj(pe, f"u{j}", ht, before=(lambda kt: pe.wait_ge(sig("h_ready").sem, kt + 1)) if j == 0 else None)

            u(0), u(1)
            for h in range(H):
                if h + 1 < H:
                    u(2 * h + 2), u(2 * h + 3)
                pe.wait_ge(*weights_of(f"qkv{h}"))
                w = ring(f"qkv{h}")
                for x in range(3):
                    for e in range(2):
                        name = f"{'qkv'[x]}{h}_{e}"
                        pe.wait_ge(*slot_free(name))
                        if x < 2:
                            pe.wait_ge(sig("xc_ready").sem, 2 * h + 2)
                        s = slot_of(name)
                        for kt in range(2):
                            ub = ub_of(2 * h + kt)
                            for b in range(3):
                                rhs = wk(4 + ub, b * SEG, (b + 1) * SEG) if x < 2 else \
                                    wk(ub, 3 + b * SEG, 3 + (b + 1) * SEG)
                                c = (x * 2 + kt) * 256 + e * P
                                last = nc.tensor.matmul(PS[:, s + b, 0:SEG], w[:, c:c + P], rhs,
                                                        start=(kt == 0), stop=(kt == 1))
                        last.then_inc(job_done.up(), 1)
            pe.wait_ge(*slot_free("gates"))
            pe.wait_ge(*read_of("v3_1"))
            pe.wait_ge(s_gate_w.sem, 32)
            s = slot_of("gates")
            for i in range(24):
                for b in range(3):
                    last = nc.tensor.matmul(PS[0:36, s + b, 0:SEG], WIF[:, i, :], big(i, b * SEG, (b + 1) * SEG),
                                            start=(i == 0), stop=(i == 23))
            last.then_inc(job_done.up(), 1)
            pe.wait_ge(*slot_free("acol"))
            s = slot_of("acol")
            pe.wait_ge(sig("a_rows_ready").sem, 1)
            for c in range(NCH):
                last = nc.tensor.transpose(PS[:, s, c * H:(c + 1) * H], WK[0:H, 4 * WT + c * CH:4 * WT + (c + 1) * CH],
                                           ident[0:H, 0:H])
            last.then_inc(job_done.up(), 1)

            pe.wait_ge(*slot_free("rows_u"))
            s = slot_of("rows_u")
            for j in range(8):
                last = nc.tensor.transpose(PS[0:11, s + j // 4, (j % 4) * P:(j % 4 + 1) * P], UT[:, j, :], ident)
            last.then_inc(job_done.up(), 1)
            pe.wait_ge(*slot_free("rows_s"))
            s = slot_of("rows_s")
            pe.wait_ge(sig("sample_cols").sem, 1)
            for i in range(6):
                last = nc.tensor.transpose(PS[0:HP, s + i // 4, (i % 4) * P:(i % 4 + 1) * P], SQC[:, i, :, :]
                                           .rearrange("p h b -> p (h b)"), ident)
            last.then_inc(job_done.up(), 1)

        def stage1_act(act):
            def evac_u(j):
                act.wait_ge(job_done.sem, done(f"u{j}"))
                ub = ub_of(j)
                if j == 0:
                    act.wait_ge(job_done.sem, done("norm0"))
                if j >= 4:
                    act.wait_ge(job_done.sem, done(f"v{j // 2 - 2}_1"))
                s = slot_of(f"u{j}")
                nc.scalar.activation(UT[:, j, :], PS[:, s + 2, SEG - 11:SEG], ACT.Copy)
                nc.scalar.activation(seg3(wk(ub, 3, 3 + W)), slot3(f"u{j}"), ACT.Copy).then_inc(job_read["act"].up(), 1)

            def silu(j):
                act.wait_ge(sig("conv_done").sem, j + 1)
                ub = ub_of(j)
                nc.scalar.activation(wk(4 + ub), wk(4 + ub), ACT.Silu).then_inc(sig("xc_ready").up(), 1)
                act.wait_ge(sig("xc_ready").sem, j + 1)
                act.dma_start(xc_d[j], wk(4 + ub)).then_inc(sig(f"xc{ub}_saved").sem, 16)

            evac_u(0), evac_u(1)
            act.wait_ge(sig("memkv_saved").sem, 64)
            act.wait_ge(sig("xt_saved").sem, 16 * KT)
            for h in range(H):
                if h + 1 < H:
                    evac_u(2 * h + 2)
                silu(2 * h)
                if h + 1 < H:
                    evac_u(2 * h + 3)
                silu(2 * h + 1)
                for x in range(3):
                    for e in range(2):
                        name = f"{'qkv'[x]}{h}_{e}"
                        act.wait_ge(job_done.sem, done(name))
                        nc.scalar.activation(
                            seg3(big(h * 6 + 2 * x + e)), slot3(name), ACT.Copy, scale=1.0 / 16 if x == 1 else 1.0).then_inc(job_read["act"].up(), 1)
            tiles = BIG[:, :].rearrange("p (h i w) -> p i h w", h=H, i=6)
            act.wait_ge(*read_of("v3_1"))
            for ub in range(4):
                act.wait_ge(sig(f"xc{ub}_saved").sem, 32)
            nc.scalar.activation(SQC, tiles[:, :, :, T:W], ACT.Copy).then_inc(sig("sample_cols").up(), 1)
            act.wait_ge(job_done.sem, done("gates"))
            s = slot_of("gates")
            nc.scalar.activation(seg3(WK[0:H, 0:W]), PS[0:H, s:s + 3, 0:SEG], ACT.Identity, bias=BIAS[:, 0:1])
            nc.scalar.activation(seg3(WK[0:H, WT:WT + W]), PS[32:32 + H, s:s + 3, 0:SEG],
                                 ACT.Identity, bias=BIAS[:, 1:2]).then_inc(job_read["act"].up(), 1)
            g = sig("gate_act")
            act.wait_ge(*read_of("gates"))
            nc.scalar.activation(WK[0:H, 2 * WT:2 * WT + W], WK[0:H, WT:WT + W], ACT.Abs).then_inc(g.up(), 1)
            act.wait_ge(g.sem, g.n)
            nc.scalar.activation(WK[0:H, 2 * WT:2 * WT + W], WK[0:H, 2 * WT:2 * WT + W], ACT.Exp, scale=-1.0).then_inc(g.up(), 1)
            act.wait_ge(g.sem, g.n)
            nc.scalar.activation(WK[0:H, 2 * WT:2 * WT + W], WK[0:H, 2 * WT:2 * WT + W], ACT.Ln, bias=1.0).then_inc(g.up(), 1)
            act.wait_ge(job_done.sem, done("acol"))
            nc.scalar.activation(SM[:, 0:32], PS[:, slot_of("acol"), 0:32], ACT.Copy).then_inc(job_read["act"].up(), 1)
            act.wait_ge(job_done.sem, done("rows_u"))
            s = slot_of("rows_u")
            UR = WK[32:43, 0:D]
            nc.scalar.activation(UR.rearrange("p (b n) -> p b n", b=2), PS[0:11, s:s + 2, :],
                                 ACT.Copy).then_inc(job_read["act"].up(), 1)
            act.wait_ge(*read_of("rows_u"))
            act.dma_start(o["conv_p"][0, 0], UR[0:3, :]).then_inc(sig("conv_saved").sem, 16)
            act.dma_start(o["conv_s"][0, :, 2, :], UR[3:11, :]).then_inc(sig("conv_saved").sem, 16)
            act.wait_ge(job_done.sem, done("rows_s"))
            s = slot_of("rows_s")
            nc.scalar.activation(QKVN[:, 0:512], PS[0:HP, s, :], ACT.Copy)
            nc.scalar.activation(QKVN[:, 512:768], PS[0:HP, s + 1, 0:256], ACT.Copy).then_inc(job_read["act"].up(), 1)
            act.wait_ge(sig("rows_ready").sem, 1)
            nc.scalar.activation(RR[:, :, 1:3, :], RR[:, :, 1:3, :], ACT.Exp).then_inc(sig("rows_exp").up(), 1)

        def stage1_dve(dve):
            for j in range(8):
                dve.wait_ge(*read_of(f"u{j}"))
                ub = ub_of(j)
                if j == 0:
                    dve.wait_ge(s_zero.sem, 6)
                if j >= 4:
                    dve.wait_ge(job_done.sem, done(f"k{j // 2 - 2}_1"))
                    dve.wait_ge(sig(f"xc{ub}_saved").sem, 16)
                x = wk(4 + ub)
                new = wk(ub, 3 + T, 3 + W)
                old = VEC[:, j, 0:24].rearrange("p (b r) -> p b r", r=3)
                cw = [vec(ROW_CW + i, j) for i in range(4)]
                nc.vector.tensor_scalar(x[:, 0:T], wk(ub, 3, 3 + T), cw[3], vec(ROW_CB, j), ALU.mult, ALU.add)
                nc.vector.tensor_scalar(x[:, T:W], new, cw[3], vec(ROW_CB, j), ALU.mult, ALU.add).then_inc(step.up(), 1)
                for i in range(3):
                    dve.wait_ge(step.sem, step.n)
                    nc.vector.scalar_tensor_tensor(out=x[:, 0:T], in0=wk(ub, i, i + T), scalar=cw[i], in1=x[:, 0:T],
                                                   op0=ALU.mult, op1=ALU.add)
                    last = nc.vector.scalar_tensor_tensor(out=x[:, T:W], in0=old[:, :, i], scalar=cw[i],
                                                          in1=x[:, T:W], op0=ALU.mult, op1=ALU.add)
                    if i < 2:
                        last.then_inc(step.up(), 1)
                last.then_inc(sig("conv_done").up(), 1)

            def row(i, lo=0, hi=W):
                return WK[0:H, i * WT + lo:i * WT + hi]

            dve.wait_ge(*read_of("gates"))
            dve.wait_ge(sig("gate_act").sem, 3)
            nc.vector.memset(MPV[:, 0:1], 0.0)
            nc.vector.scalar_tensor_tensor(out=row(1), in0=row(1), scalar=0.0, in1=row(2), op0=ALU.min,
                                           op1=ALU.subtract).then_inc(step.up(), 1)
            dve.wait_ge(step.sem, step.n)
            nc.vector.tensor_copy(SM[0:H, 344:352], row(1, T, W)).then_inc(sig("sample_gates_ready").up(), 1)
            nc.vector.tensor_copy(SM[0:H, 352:360], row(0, T, W)).then_inc(sig("sample_gates_ready").up(), 1)
            for ub in range(4):
                dve.wait_ge(sig(f"xc{ub}_saved").sem, 32)
            for c in range(NCH):
                last = nc.vector.tensor_tensor_scan(row(3, c * CH, (c + 1) * CH), ones[0:H, :],
                                                    row(1, c * CH, (c + 1) * CH), 0.0, ALU.mult, ALU.add)
            last.then_inc(step.up(), 1)
            dve.wait_ge(step.sem, step.n)
            nc.vector.tensor_tensor(row(4, 0, T), row(0, 0, T), row(3, 0, T), ALU.subtract).then_inc(sig("a_rows_ready").up(), 1)
            dve.wait_ge(sig("a_rows_ready").sem, sig("a_rows_ready").n)
            for c in range(NCH):
                end = (c + 1) * CH
                nc.vector.tensor_tensor_scan(row(5, c * CH, end), ones[0:H, :], row(4, c * CH, end),
                                             MPV[:, c:c + 1], ALU.mult, ALU.max).then_inc(step.up(), 1)
                dve.wait_ge(step.sem, step.n)
                nc.vector.tensor_tensor(MPV[:, c + 1:c + 2], row(5, end - 1, end), row(3, end - 1, end),
                                        ALU.add).then_inc(step.up(), 1)
                dve.wait_ge(step.sem, step.n)
            m = row(5, 0, T).rearrange("h (c t) -> h c t", c=NCH)
            nc.vector.tensor_scalar(RR[:, :, 0, :], m, -1.0, None, ALU.mult).then_inc(step.up(), 1)
            dve.wait_ge(step.sem, step.n)
            mp = MPV[:, 0:NCH].unsqueeze(2).to_broadcast([H, NCH, CH])
            nc.vector.tensor_tensor(RR[:, :, 1, :], RR[:, :, 0, :], mp, ALU.add)
            nc.vector.tensor_tensor(
                RR[:, :, 2, :], RR[:, :, 0, :], row(3, 0, T).rearrange("h (c t) -> h c t", c=NCH), ALU.subtract).then_inc(sig("rows_ready").up(), 1)

        s_out = sig("outputs_stored")

        CT = WK[:, 0:3072].rearrange("p (h k n) -> p h k n", h=H, k=2)
        VA = WK[:, 3072:3840].rearrange("p (b n) -> p b n", b=2)
        KW = WK[:, 3840:4352].rearrange("p (b n) -> p b n", b=2)
        BS = WK[:, 4352:5376].rearrange("p (b n) -> p b n", b=2)
        DD = WK[:, 5376:5632].rearrange("p (b n) -> p b n", b=2)
        SCT = WK[:, 5632:5888].rearrange("p (b n) -> p b n", b=2)
        QD = WK[:, 5888:6400].rearrange("p (b k n) -> p b k n", b=2, k=2)
        DM = WK[:, 6400:6528]
        DN = WK[:, 6528:6656]
        NU = NCH * H

        def qk_view(h, x, c):
            at = (h * 6 + 2 * x) * W
            return BIG[:, at:at + 2 * W].rearrange("p (k n) -> p k n", k=2)[:, :, c * CH:(c + 1) * CH]

        def stage2_pe(pe):
            pe.wait_ge(*read_of("rows_s"))
            pe.wait_ge(sig("rows_exp").sem, 1)
            for n in range(NU + 1):
                if n < NU:
                    c, h = n // H, n % H
                    if n >= 2:
                        pe.wait_ge(sig("bs_ready").sem, n - 1)
                    nc.tensor.matmul(PS[:, n % 2, 0:384], CST[0:H, C_SEL + h * P:C_SEL + (h + 1) * P],
                                     RR[:, c].rearrange("h x t -> h (x t)"), start=True, stop=True)
                    q, k, v = (qk_view(h, x, c) for x in range(3))
                    for kt in range(2):
                        last = nc.tensor.matmul(PS[:, n % 2, 384:512], k[:, kt, :], q[:, kt, :],
                                                start=(kt == 0), stop=(kt == 1))
                    last.then_inc(sig("scores_done").up(), 1)
                    if n >= 2:
                        pe.wait_ge(sig("kw_ready").sem, n - 1)
                    for kt in range(2):
                        nc.tensor.transpose(PS[:, 2 + n % 2, kt * P:(kt + 1) * P], k[:, kt, :], ident)
                    for kt in range(2):
                        last = nc.tensor.transpose(PS[:, 2 + n % 2, 256 + kt * P:256 + (kt + 1) * P], v[:, kt, :],
                                                   ident)
                    last.then_inc(sig("kv_turned").up(), 1)
                if n >= 1:
                    u = n - 1
                    c, h, b = u // H, u % H, u % 2
                    pe.wait_ge(sig("sc_ready").sem, u + 1)
                    pe.wait_ge(sig("va_ready").sem, u + 1)
                    if u >= 2:
                        pe.wait_ge(sig("hs_done").sem, u - 1)
                    if c > 0:
                        pe.wait_ge(sig("ct_done").sem, u - 3)
                    for m in range(3):
                        out = PS[:, 4 + b, m * P:(m + 1) * P]
                        last = nc.tensor.matmul(out, VA[:, b, m * P:(m + 1) * P], SCT[:, b, :],
                                                start=True, stop=(c == 0))
                        if c > 0:
                            for kt in range(2):
                                last = nc.tensor.matmul(out, CT[:, h, kt, m * P:(m + 1) * P], QD[:, b, kt, :],
                                                        start=False, stop=(kt == 1))
                    last.then_inc(sig("num_done").up(), 1)
                    pe.wait_ge(sig("kw_ready").sem, u + 1)
                    if u >= 1:
                        pe.wait_ge(sig("ct_done").sem, u)
                    for kt in range(2):
                        last = nc.tensor.matmul(PS[:, 6 + kt, 0:384], KW[:, b, kt * P:(kt + 1) * P], VA[:, b, :],
                                                start=True, stop=True)
                    last.then_inc(sig("update_done").up(), 1)

        def stage2_act(act):
            for n in range(NU):
                b = n % 2
                act.wait_ge(sig("scores_done").sem, n + 1)
                if n >= 2:
                    act.wait_ge(sig("ct_done").sem, n - 1)
                if n == 0:
                    act.wait_ge(sig("conv_saved").sem, 32)
                nc.scalar.activation(BS[:, b, :], PS[:, b, :], ACT.Copy).then_inc(sig("bs_ready").up(), 1)
                act.wait_ge(sig("kv_turned").sem, n + 1)
                if n >= 2:
                    act.wait_ge(sig("update_done").sem, n - 1)
                nc.scalar.activation(VA[:, b, 0:256], PS[:, 2 + b, 256:512], ACT.Copy).then_inc(sig("va_ready").up(), 1)
                act.wait_ge(sig("d_args").sem, n + 1)
                nc.scalar.activation(DD[:, b, :], DD[:, b, :], ACT.Exp).then_inc(sig("d_ready").up(), 1)
                act.wait_ge(sig("d_ready").sem, sig("d_ready").n)
                nc.scalar.activation(KW[:, b, :], PS[:, 2 + b, 0:256], ACT.Copy,
                                     scale=DD[:, b, P - 1:P]).then_inc(sig("kw_ready").up(), 1)

        def stage2_dve(dve):
            dve.wait_ge(sig("rows_exp").sem, 1)
            for b in range(2):
                nc.vector.memset(VA[:, b, 256:384], 1.0).then_inc(step.up(), 1)
            dve.wait_ge(step.sem, step.n)
            for n in range(NU + 1):
                if n < NU:
                    c, h, b = n // H, n % H, n % 2
                    dve.wait_ge(sig("bs_ready").sem, n + 1)
                    if n >= 2:
                        dve.wait_ge(sig("kw_ready").sem, n - 1)
                    nc.vector.tensor_scalar(DD[:, b, :], BS[:, b, 0:CH], ACOL[:, c, h:h + 1], 0.0,
                                            ALU.add, ALU.min).then_inc(sig("d_args").up(), 1)
                    if n >= 2:
                        dve.wait_ge(sig("num_done").sem, n - 1)
                    nc.vector.tensor_tensor(QD[:, b], qk_view(h, 0, c),
                                            BS[:, b, CH:2 * CH].unsqueeze(1).to_broadcast([P, 2, CH]), ALU.mult)
                    dve.wait_ge(sig("d_ready").sem, n + 1)
                    nc.vector.tensor_tensor(DM, DD[:, b, :], causal, ALU.mult).then_inc(step.up(), 1)
                    dve.wait_ge(step.sem, step.n)
                    nc.vector.tensor_tensor(SCT[:, b, :], BS[:, b, 384:512], DM, ALU.mult).then_inc(sig("sc_ready").up(), 1)
                if n >= 1:
                    u = n - 1
                    c, h, b = u // H, u % H, u % 2
                    dve.wait_ge(sig("num_done").sem, u + 1)
                    dve.wait_ge(sig("hs_done").sem, sig("hs_done").n)
                    nc.vector.scalar_tensor_tensor(out=DN, in0=PS[:, 4 + b, 256:384], scalar=-1.0,
                                                   in1=BS[:, b, 256:384], op0=ALU.mult, op1=ALU.max).then_inc(step.up(), 1)
                    dve.wait_ge(step.sem, step.n)
                    nc.vector.tensor_tensor(DN, PS[:, 4 + b, 256:384], DN, ALU.max).then_inc(step.up(), 1)
                    dve.wait_ge(step.sem, step.n)
                    nc.vector.reciprocal(DN, DN).then_inc(step.up(), 1)
                    dve.wait_ge(step.sem, step.n)
                    nc.vector.tensor_tensor(
                        qk_view(h, 0, c), PS[:, 4 + b, 0:256].rearrange("p (k n) -> p k n", k=2),
                        DN.unsqueeze(1).to_broadcast([P, 2, CH]), ALU.mult).then_inc(sig("hs_done").up(), 1)
                    dve.wait_ge(sig("update_done").sem, u + 1)
                    for kt in range(2):
                        new = PS[:, 6 + kt, 0:384]
                        if c == 0:
                            last = nc.vector.tensor_copy(CT[:, h, kt, :], new)
                        else:
                            last = nc.vector.scalar_tensor_tensor(out=CT[:, h, kt, :], in0=CT[:, h, kt, :],
                                                                  scalar=BS[:, b, 255:256], in1=new,
                                                                  op0=ALU.mult, op1=ALU.add)
                    last.then_inc(sig("ct_done").up(), 1)

        CO = WK[:, 3072:4096 + 1024].rearrange("p (b n) -> p b n", b=2)

        def stage2_end_pe(pe):
            pe.wait_ge(sig("ct_done").sem, NU)
            for h in range(H):
                if h >= 2:
                    pe.wait_ge(sig("c_copied").sem, h - 1)
                for vt in range(2):
                    for kt in range(2):
                        last = nc.tensor.transpose(PS[:, 2 * (h % 2), vt * 256 + kt * P:vt * 256 + (kt + 1) * P],
                                                   CT[:, h, kt, vt * P:(vt + 1) * P], ident)
                last.then_inc(sig("c_turned").up(), 1)
            pe.wait_ge(sig("c_copied").sem, H)

        def stage2_end_act(act):
            own = sig("c_copied")
            for h in range(H):
                act.wait_ge(sig("c_turned").sem, h + 1)
                if h >= 2:
                    act.wait_ge(sig(f"c{h % 2}_saved").sem, 16)
                nc.scalar.activation(CO[:, h % 2, 0:512], PS[:, 2 * (h % 2), :], ACT.Copy).then_inc(own.up(), 1)
                act.wait_ge(own.sem, own.n)
                act.dma_start(o["C_p"][0, 0, h].rearrange("(v p) k -> p v k", p=P),
                              CO[:, h % 2, 0:512].rearrange("p (v k) -> p v k", v=2))\
                    .then_inc(sig(f"c{h % 2}_saved").sem, 16)

        def stage2_end_sp(sp):
            sp.wait_ge(sig("ct_done").sem, NU)
            for h in range(H):
                for kt in range(2):
                    sp.dma_start(o["n_p"][0, 0, h, kt * P:(kt + 1) * P].rearrange("(p a) -> p a", a=1),
                                 CT[:, h, kt, 256:257]).then_inc(sig("n_saved").sem, 16)
            sp.dma_start(o["m_p"].rearrange("a b h -> h (a b)"), MPV[:, NCH:NCH + 1]).then_inc(sig("n_saved").sem, 16)

        CTP, QWP, PRP = (WK[:, 4 * WT + at:4 * WT + at + 1024].rearrange("p (b n) -> p b n", b=2)
                         for at in (0, 1024, 2048))

        def hq(h):
            return BIG[:, h * 6 * W:(h * 6 + 2) * W]

        def gates_sp(sp):
            for name in ("o0_0", "o0_1", "zg0_0"):
                load_item(sp, name)
            sp.wait_ge(sig("sample_gates_ready").sem, 2)
            sp.dma_start(sg_d.rearrange("x h b -> h x b"), SM[0:H, 344:360].rearrange("h (x b) -> h x b", x=2))\
                .then_inc(sig("gates_saved").sem, 16)
            sp.wait_ge(sig("gates_saved").sem, 16)
            for x in range(2):
                sp.dma_start(SC32[:, 1 + x:2 + x], sg_d[x].rearrange("h (b a) -> (h b) a", a=1))\
                    .then_inc(sig("pair_inputs").sem, 16)
            for h in range(H):
                rows = slice(64 + h * NS, 64 + (h + 1) * NS)
                sp.dma_start(XTRA[rows, 768:1024], a["state_n"][0, :, h, :]).then_inc(sig("pair_inputs").sem, 16)
                sp.dma_start(XTRA[rows, 1792:1793], a["state_m"][0, :, h:h + 1],
                             allow_slow_non_contiguous=True).then_inc(sig("pair_inputs").sem, 16)

        def pair_scalars_dve(dve):
            def col(i, n=1):
                return SC32[:, i:i + n]

            def do(ins):
                ins.then_inc(step.up(), 1)
                dve.wait_ge(step.sem, step.n)

            dve.wait_ge(*read_of("rows_s"))
            dve.wait_ge(sig("pair_inputs").sem, 16 * 10)
            q, k = QKVN[:, 0:256], QKVN[:, 256:512]
            do(nc.vector.tensor_tensor(col(3), col(1), col(0), ALU.add))
            do(nc.vector.tensor_tensor(col(4), col(3), col(2), ALU.max))
            nc.vector.tensor_tensor(col(5), col(3), col(4), ALU.subtract)
            nc.vector.tensor_tensor(col(6), col(2), col(4), ALU.subtract)
            nc.vector.tensor_scalar(col(7), col(4), -1.0, None, ALU.mult).then_inc(sig("pair_exp_args").up(), 1)
            nc.vector.tensor_tensor_reduce(TMP32, q, k, 1.0, 0.0, ALU.mult, ALU.add, col(8))
            do(nc.vector.tensor_tensor_reduce(NN32, q, SN, 1.0, 0.0, ALU.mult, ALU.add, col(9)))
            dve.wait_ge(sig("pair_exp").sem, 1)
            do(nc.vector.tensor_tensor(col(10), col(8), col(6), ALU.mult))
            do(nc.vector.scalar_tensor_tensor(out=col(11), in0=col(9), scalar=col(5), in1=col(10), op0=ALU.mult,
                                              op1=ALU.add))
            do(nc.vector.scalar_tensor_tensor(out=col(12), in0=col(11), scalar=-1.0, in1=col(7), op0=ALU.mult,
                                              op1=ALU.max))
            do(nc.vector.tensor_tensor(col(12), col(11), col(12), ALU.max))
            do(nc.vector.reciprocal(col(12), col(12)))
            nc.vector.tensor_tensor(col(13), col(5), col(12), ALU.mult)
            nc.vector.tensor_tensor(col(14), col(10), col(12), ALU.mult)
            nc.vector.tensor_copy(col(15), col(5))
            do(nc.vector.tensor_scalar(WK32, k, col(6), None, ALU.mult))
            nc.vector.scalar_tensor_tensor(out=NN32, in0=SN, scalar=col(5), in1=WK32,
                                           op0=ALU.mult, op1=ALU.add).then_inc(sig("pair_scalars").up(), 1)

        def pair_scalars_act(act):
            act.wait_ge(sig("pair_exp_args").sem, 1)
            nc.scalar.activation(SC32[:, 5:8], SC32[:, 5:8], ACT.Exp).then_inc(sig("pair_exp").up(), 1)

        def pair_scalars_sp(sp):
            sp.wait_ge(sig("pair_scalars").sem, 1)
            back = sig("pair_saved").sem
            sp.dma_start(qw_d[:, 0:256], QKVN[:, 0:256]).then_inc(back, 16)
            sp.dma_start(qw_d[:, 256:512], WK32).then_inc(back, 16)
            sp.dma_start(cf_d, SC32[:, 13:16]).then_inc(back, 16)
            for h in range(H):
                rows = slice(64 + h * NS, 64 + (h + 1) * NS)
                sp.dma_start(o["n_s"][0, :, h, :], XTRA[rows, 1536:1792]).then_inc(sig("nm_saved").sem, 16)
                sp.dma_start(o["m_s"][0, :, h:h + 1], XTRA[rows, 1796:1797],
                             allow_slow_non_contiguous=True).then_inc(sig("nm_saved").sem, 16)
            sp.wait_ge(sig("pair_saved").sem, 48)
            sp.dma_start(COEF, cf_d.rearrange("i k -> (i k)").partition_broadcast(P)
                         .rearrange("p (i k) -> p i k", k=3)).then_inc(sig("coef_loaded").sem, 16)

        def pair_load(sp, i):
            h, b, buf = i // NS, i % NS, i % 2
            if i >= 2:
                sp.wait_ge(sig(f"cs{buf}_saved").sem, 16 * (i // 2))
            s = sig(f"pair{buf}_loaded").sem
            sp.dma_start(CTP[:, buf, :].rearrange("p (v k) -> p v k", v=2),
                         a["state_C"][0, b, h].rearrange("(v p) k -> p v k", p=P)).then_inc(s, 16)
            sp.dma_start(QWP[:, buf, :], qw_d[i].partition_broadcast(P)).then_inc(s, 16)

        def pair_store(sp, i):
            h, b, buf = i // NS, i % NS, i % 2
            sp.wait_ge(sig("pair_done").sem, i + 1)
            sp.dma_start(o["C_s"][0, b, h].rearrange("(v p) k -> p v k", p=P),
                         CTP[:, buf, :].rearrange("p (v k) -> p v k", v=2)).then_inc(sig(f"cs{buf}_saved").sem, 16)

        def pair_pool(pool, i):
            buf = i % 2
            pool.wait_ge(sig(f"pair{buf}_loaded").sem, 32 * (i // 2 + 1))
            if i >= 2:
                pool.wait_ge(sig("cq_done").sem, i - 1)
            v2 = lambda x: x[:, buf, :].rearrange("p (v k) -> p v k", v=2)
            nc.gpsimd.tensor_tensor(
                v2(PRP), v2(CTP), QWP[:, buf, 0:256].unsqueeze(1).to_broadcast([P, 2, 256]), ALU.mult).then_inc(sig("prod_done").up(), 1)

        def pair_act(act, i):
            act.wait_ge(sig("prod_done").sem, i + 1)
            nc.scalar.activation(CTP[:, i % 2, :], CTP[:, i % 2, :], ACT.Copy,
                                 scale=COEF[:, i, 2:3]).then_inc(sig("c_decayed").up(), 1)

        def pair_dve(dve, i):
            h, b, buf = i // NS, i % NS, i % 2
            dve.wait_ge(sig("prod_done").sem, i + 1)
            nc.vector.tensor_reduce(CQ[:, :, i:i + 1], PRP[:, buf, :].rearrange(
                "p (v k) -> p v k", v=2), AX.X, ALU.add).then_inc(sig("cq_done").up(), 1)
            dve.wait_ge(sig("c_decayed").sem, i + 1)
            for vt in range(2):
                c = CTP[:, buf, vt * 256:(vt + 1) * 256]
                at = (h * 6 + 4 + vt) * W + T + b
                last = nc.vector.scalar_tensor_tensor(out=c, in0=QWP[:, buf, 256:512], scalar=BIG[:, at:at + 1],
                                                      in1=c, op0=ALU.mult, op1=ALU.add)
            last.then_inc(sig("pair_done").up(), 1)

        def stage3_sp(sp):
            pair_scalars_sp(sp)
            for i in range(H * NS):
                h = i // NS
                if i == 0:
                    sp.wait_ge(sig("n_saved").sem, 16 * 9)
                    sp.wait_ge(sig("c0_saved").sem, 32)
                    sp.wait_ge(sig("c1_saved").sem, 32)
                if i >= 2:
                    pair_store(sp, i - 2)
                pair_load(sp, i)
                if i % NS == NS - 2:
                    if h >= 2:
                        sp.wait_ge(sig("y_ready").sem, h - 1)
                    for e in range(2):
                        sp.dma_start(wk(2 * (h % 2) + e), xc_d[2 * h + e]).then_inc(sig(f"xc_pair{h % 2}").up(16), 16)
            for i in (30, 31):
                pair_store(sp, i)

        def stage3_pool(pool):
            for i in range(H * NS):
                pair_pool(pool, i)

        def stage3_pe(pe):
            def mean(h):
                name = f"mean{h}"
                pe.wait_ge(*slot_free(name))
                pe.wait_ge(sig("gated").sem, h + 1)
                s = slot_of(name)
                for e in range(2):
                    for b in range(3):
                        last = nc.tensor.matmul(PS[:, s + b, 0:SEG], avg_h, big(h * 6 + e, b * SEG, (b + 1) * SEG),
                                                start=(e == 0), stop=(e == 1))
                last.then_inc(job_done.up(), 1)

            def var(h):
                name = f"var{h}"
                pe.wait_ge(*slot_free(name))
                pe.wait_ge(sig("squares").sem, h + 1)
                s = slot_of(name)
                for e in range(2):
                    for b in range(3):
                        last = nc.tensor.matmul(PS[:, s + b, 0:SEG], avg_h,
                                                big(h * 6 + 2 + e, b * SEG, (b + 1) * SEG),
                                                start=(e == 0), stop=(e == 1))
                last.then_inc(job_done.up(), 1)

            for h in range(H):
                for e in range(2):
                    pe_proj(pe, f"o{h}_{e}", ht)
                if h > 0:
                    var(h - 1)
                for e in range(2):
                    pe_proj(pe, f"zg{h}_{e}", ht)
                mean(h)
            var(3)

        def stage3_act(act):
            def root(h):
                act.wait_ge(job_done.sem, done(f"var{h}"))
                if h > 0:
                    act.wait_ge(sig("y_ready").sem, h)
                nc.scalar.activation(seg3(wk(7)), slot3(f"var{h}"), ACT.Sqrt, bias=EPSC).then_inc(job_read["act"].up(), 1)

            pair_scalars_act(act)
            for h in range(H):
                pairs = iter(range(h * NS + (4 if h > 0 else 0), (h + 1) * NS))
                for e in range(2):
                    act.wait_ge(job_done.sem, done(f"o{h}_{e}"))
                    nc.scalar.activation(seg3(big(h * 6 + 2 + e)), slot3(f"o{h}_{e}"),
                                         ACT.Sigmoid).then_inc(job_read["act"].up(), 1)
                    load_ahead(act, f"o{h}_{e}")
                    if h == 0 and e == 0:
                        act.wait_ge(sig("coef_loaded").sem, 16)
                    for _ in range(4 if h == 0 else 2):
                        pair_act(act, next(pairs))
                if h > 0:
                    root(h - 1)
                act.wait_ge(sig("hs_sample").sem, h + 1)
                for e in range(2):
                    act.wait_ge(job_done.sem, done(f"zg{h}_{e}"))
                    nc.scalar.activation(seg3(big(h * 6 + 4 + e)), slot3(f"zg{h}_{e}"),
                                         ACT.Silu).then_inc(job_read["act"].up(), 1)
                    load_ahead(act, f"zg{h}_{e}")
                if h < H - 1:
                    for i in range(4):
                        pair_act(act, (h + 1) * NS + i)
                act.wait_ge(*read_of(f"mean{h}"))
                nc.scalar.activation(BIG[:, (h * 6 + 2) * W:(h * 6 + 4) * W], hq(h),
                                     ACT.Square).then_inc(sig("squares").up(), 1)
            root(3)

        def stage3_dve(dve):
            def finish(h):
                dve.wait_ge(*read_of(f"var{h}"))
                nc.vector.reciprocal(wk(7), wk(7)).then_inc(step.up(), 1)
                dve.wait_ge(step.sem, step.n)
                dve.wait_ge(sig(f"xc_pair{h % 2}").sem, 32 * (h // 2 + 1))
                for e in range(2):
                    x, j = big(h * 6 + e), 2 * h + e
                    nc.vector.scalar_tensor_tensor(out=x, in0=x, scalar=vec(ROW_GHN, j), in1=wk(7),
                                                   op0=ALU.mult, op1=ALU.mult).then_inc(step.up(), 1)
                    dve.wait_ge(step.sem, step.n)
                    nc.vector.scalar_tensor_tensor(out=x, in0=wk(2 * (h % 2) + e),
                                                   scalar=vec(ROW_SKIP, j), in1=x,
                                                   op0=ALU.mult, op1=ALU.add).then_inc(step.up(), 1)
                    dve.wait_ge(step.sem, step.n)
                dve.wait_ge(*read_of(f"zg{h}_1"))
                nc.vector.tensor_tensor(hq(h), hq(h), BIG[:, (h * 6 + 4) * W:(h * 6 + 6) * W],
                                        ALU.mult).then_inc(sig("y_ready").up(), 1)

            pair_scalars_dve(dve)
            dve.wait_ge(sig("coef_loaded").sem, 16)
            for h in range(H):
                for i in range(h * NS + (4 if h > 0 else 0), (h + 1) * NS):
                    pair_dve(dve, i)
                pairs = slice(h * NS, (h + 1) * NS)
                c1, c2 = (COEF[:, pairs, x].unsqueeze(1).to_broadcast([P, 2, NS]) for x in range(2))
                v = BIG[:, (h * 6 + 4) * W:(h * 6 + 6) * W].rearrange("p (v w) -> p v w", v=2)[:, :, T:W]
                t0 = HSS[:, 0:16].rearrange("p (v b) -> p v b", v=2)
                t1 = HSS[:, 16:32].rearrange("p (v b) -> p v b", v=2)
                dve.wait_ge(sig("cq_done").sem, sig("cq_done").n)
                nc.vector.tensor_tensor(t0, CQ[:, :, pairs], c1, ALU.mult)
                nc.vector.tensor_tensor(t1, v, c2, ALU.mult).then_inc(step.up(), 1)
                dve.wait_ge(step.sem, step.n)
                nc.vector.tensor_tensor(
                    hq(h).rearrange("p (v w) -> p v w", v=2)[:, :, T:W], t0, t1, ALU.add).then_inc(sig("hs_sample").up(), 1)
                dve.wait_ge(sig("hs_sample").sem, sig("hs_sample").n)
                dve.wait_ge(*read_of(f"o{h}_1"))
                nc.vector.tensor_tensor(hq(h), hq(h), BIG[:, (h * 6 + 2) * W:(h * 6 + 4) * W],
                                        ALU.mult).then_inc(sig("gated").up(), 1)
                if h > 0:
                    finish(h - 1)
                for i in range(NS, NS + 4 if h < H - 1 else NS):
                    pair_dve(dve, h * NS + i)
                dve.wait_ge(job_done.sem, done(f"mean{h}"))
                dve.wait_ge(sig("gated").sem, sig("gated").n)
                for e in range(2):
                    last = nc.vector.tensor_tensor(seg3(big(h * 6 + e)), seg3(big(h * 6 + e)), slot3(f"mean{h}"),
                                                   ALU.subtract)
                last.then_inc(job_read["dve"].up(), 1)
            finish(3)

        ATT = {}

        def attention(name, base, q, k, nk, mask, v, out, p, pt, stat):
            ATT[name] = dict(base=base, q=q, k=k, nk=nk, mask=mask, v=v, out=out, p=p, pt=pt, stat=stat)

        def score_view(u, nk):
            b = 2 * (u % 2)
            return PS[:, b:b + 2, 0:2 * nk].rearrange("p b (x n) -> p b x n", x=2)

        def attend_pe(pe, name):
            c = ATT[name]
            for i in range(10):
                u = c["base"] + i
                if i < 8:
                    nk = c["nk"](i)
                    if i >= 2:
                        pe.wait_ge(sig("probs_ready").sem, u - 1)
                    for h in range(H):
                        bank = PS[:, 2 * (u % 2) + h // 2, :]
                        if c["mask"] and h % 2 == 0:
                            nc.tensor.matmul(bank[:, 0:2 * nk], BFC[:, M_ID:M_ID + P], c["mask"](i),
                                             start=True, stop=False, skip_group_check=True)
                        last = nc.tensor.matmul(bank[:, (h % 2) * nk:(h % 2 + 1) * nk], c["q"](h, i), c["k"](h, i),
                                                start=not c["mask"], stop=True, skip_group_check=True)
                    last.then_inc(sig("scores_ready").up(), 1)
                if i >= 2:
                    w, nk = u - 2, c["nk"](i - 2)
                    pe.wait_ge(sig("turned_copied").sem, w + 1)
                    if i >= 4:
                        pe.wait_ge(sig("out_read").sem, w - 1)
                    n = nk // P
                    for h in range(H):
                        for t in range(n):
                            at = h * nk + t * P
                            last = nc.tensor.matmul(PS[:, 6 + w % 2, h * P:(h + 1) * P], c["v"](h, t, i - 2),
                                                    c["pt"](w)[:, at:at + P], start=(t == 0), stop=(t == n - 1))
                    last.then_inc(sig("out_ready").up(), 1)
                if 1 <= i < 9:
                    w, nk = u - 1, c["nk"](i - 1)
                    pe.wait_ge(sig("probs_scaled").sem, w + 1)
                    if i >= 2:
                        pe.wait_ge(sig("turned_copied").sem, w)
                    n = nk // P
                    for h in range(H):
                        for t in range(n):
                            at = (h % 2) * nk + t * P
                            last = nc.tensor.transpose(PS[:, 4 + h // 2, at:at + P],
                                                       c["p"](w)[:, h * nk + t * P:h * nk + (t + 1) * P], ident)
                    last.then_inc(sig("probs_turned").up(), 1)
            pe.wait_ge(sig("out_read").sem, c["base"] + 8)

        def attend_act(act, name):
            c = ATT[name]
            negmax, total = c["stat"][0], c["stat"][1]
            for i in range(9):
                u = c["base"] + i
                if i < 8:
                    nk = c["nk"](i)
                    act.wait_ge(sig("max_ready").sem, 2 * (u + 1))
                    if i >= 2:
                        act.wait_ge(sig("probs_turned").sem, u - 1)
                    for h in range(H):
                        last = nc.scalar.activation(c["p"](u)[:, h * nk:(h + 1) * nk],
                                                    PS[:, 2 * (u % 2) + h // 2, (h % 2) * nk:(h % 2 + 1) * nk],
                                                    ACT.Exp, bias=negmax[:, 4 * i + h:4 * i + h + 1], scale=SCALE,
                                                    accum_out=total[:, 4 * i + h:4 * i + h + 1])
                    last.then_inc(sig("probs_ready").up(), 1)
                if i >= 1:
                    w, nk = u - 1, c["nk"](i - 1)
                    act.wait_ge(sig("probs_turned").sem, w + 1)
                    if i >= 3:
                        act.wait_ge(sig("out_ready").sem, w - 1)
                    nc.scalar.activation(
                        c["pt"](w)[:, 0:4 * nk].rearrange("p (b n) -> p b n", b=2), PS[:, 4:6, 0:2 * nk], ACT.Copy).then_inc(sig("turned_copied").up(), 1)

        def attend_dve(dve, name, between=lambda i: None):
            c = ATT[name]
            negmax, total, inv = c["stat"][0], c["stat"][1], c["stat"][2]
            for i in range(10):
                u = c["base"] + i
                if i < 8:
                    nk = c["nk"](i)
                    cols = slice(4 * i, 4 * i + 4)
                    dve.wait_ge(sig("scores_ready").sem, u + 1)
                    own = sig("max_ready")
                    nc.vector.tensor_reduce(negmax[:, cols].rearrange("p (b x) -> p b x", b=2),
                                            score_view(u, nk), AX.X, ALU.max, negate=True).then_inc(own.up(), 1)
                    dve.wait_ge(own.sem, own.n)
                    nc.vector.tensor_scalar(negmax[:, cols], negmax[:, cols], SCALE, None, ALU.mult).then_inc(own.up(), 1)
                if 1 <= i < 9:
                    w, nk = u - 1, c["nk"](i - 1)
                    cols = slice(4 * (i - 1), 4 * i)
                    dve.wait_ge(sig("probs_ready").sem, w + 1)
                    nc.vector.reciprocal(inv[:, cols], total[:, cols]).then_inc(step.up(), 1)
                    dve.wait_ge(step.sem, step.n)
                    for h in range(H):
                        x = c["p"](w)[:, h * nk:(h + 1) * nk]
                        at = 4 * (i - 1) + h
                        last = nc.vector.tensor_scalar(x, x, inv[:, at:at + 1], None, ALU.mult)
                    last.then_inc(sig("probs_scaled").up(), 1)
                if i >= 2:
                    w = u - 2
                    dve.wait_ge(sig("out_ready").sem, w + 1)
                    c["out"](i - 2, PS[:, 6 + w % 2, :].rearrange("p (h n) -> p h n", h=H)).then_inc(sig("out_read").up(), 1)
                if i < 8:
                    between(i)

        SMP = {}
        tile_loaded = [sig(f"tile{n}_loaded") for n in range(4)]
        query_loaded = [sig(f"query{n}_loaded") for n in range(2)]

        def samples(name, nt, base, key, value, query, tiles, queries, prods, misc, free, new=None):
            m = {}
            at = 0
            for what, size in (("scores", nt * HP), ("cols", 4), ("row", nt * P + nt), ("turned", 2 * nt * HP),
                               ("diag", nt * HP), ("qk", nt * HP)):
                m[what] = misc[:, at:at + size]
                at += size
            SMP[name] = dict(nt=nt, base=base, key=key, value=value, query=query, tiles=tiles, queries=queries,
                             prods=prods, m=m, free=free, new=new)

        def tile_count(c, n):
            g = c["first_load"] + n
            return tile_loaded[g % 4], 16 * (g // 4 + 1), g % 4

        def samples_sp(sp, name):
            c = SMP[name]
            n_u = c["nt"] * NS
            c["free"](sp)
            for n in range(2 * n_u):
                s, v, buf = tile_count(c, n)
                if n >= 4:
                    if n - 4 < n_u:
                        sp.wait_ge(sig("key_products").sem, c["base"] + n - 3)
                    else:
                        sp.wait_ge(sig("values_used").sem, c["base"] + n - 4 - n_u + 1)
                b, t = n % n_u // c["nt"], n % n_u % c["nt"]
                src = c["key"](b, t) if n < n_u else c["value"](b, t)
                sp.dma_start(c["tiles"][buf], src).then_inc(s.sem, 16)
                if n < n_u:
                    if n >= 2:
                        sp.wait_ge(sig("key_products").sem, c["base"] + n - 1)
                    u = c["base"] + n
                    sp.dma_start(c["queries"][u % 2].rearrange("p (h d) -> p h d", h=H),
                                 c["query"](b, t).partition_broadcast(P)).then_inc(query_loaded[u % 2].sem, 16)

        def samples_pool(pool, name, units):
            c = SMP[name]
            for n in units:
                s, v, buf = tile_count(c, n)
                u = c["base"] + n
                pool.wait_ge(s.sem, v)
                pool.wait_ge(query_loaded[u % 2].sem, 16 * (u // 2 + 1))
                if n >= 2:
                    pool.wait_ge(sig("key_sums").sem, u - 1)
                nc.gpsimd.tensor_tensor(c["prods"][u % 2], c["tiles"][buf],
                                        c["queries"][u % 2], ALU.mult).then_inc(sig("key_products").up(), 1)

        def samples_scores_dve(dve, name, units):
            c = SMP[name]
            sc = c["m"]["scores"].rearrange("p (t h b) -> p t h b", t=c["nt"], h=H)
            for n in units:
                b, t = n // c["nt"], n % c["nt"]
                u = c["base"] + n
                dve.wait_ge(sig("key_products").sem, u + 1)
                nc.vector.tensor_reduce(
                    sc[:, t, :, b:b + 1], c["prods"][u % 2].rearrange("p (h d) -> p h d", h=H), AX.X, ALU.add).then_inc(sig("key_sums").up(), 1)

        def samples_new_dve(dve, name):
            c = SMP[name]
            q, k, _ = c["new"]
            qk = c["m"]["qk"].rearrange("p (t n) -> p t n", t=c["nt"])
            for t in range(c["nt"]):
                last = nc.vector.tensor_tensor(qk[:, t, :].rearrange("p (h b) -> p h b", h=H), q(t),
                                               k(t).rearrange("p (h b) -> p h b", h=H), ALU.mult)
            last.then_inc(sig("new_products").up(), 1)

        def samples_dve(dve, name):
            c = SMP[name]
            m, nt = c["m"], c["nt"]
            nr = nt * P + (nt if c["new"] else 0)
            row, cols = m["row"][0:HP, 0:nr], m["cols"][0:HP, :]
            dve.wait_ge(*read_of(f"ss{name}"))
            nc.vector.tensor_reduce(cols[:, 0:1], row, AX.X, ALU.max, negate=True).then_inc(step.up(), 1)
            dve.wait_ge(step.sem, step.n)
            nc.vector.tensor_scalar(cols[:, 0:1], cols[:, 0:1], SCALE, None, ALU.mult).then_inc(sig("sample_max").up(), 1)
            dve.wait_ge(sig("sample_exp").sem, c["order"] + 1)
            nc.vector.reciprocal(cols[:, 2:3], cols[:, 1:2]).then_inc(step.up(), 1)
            dve.wait_ge(step.sem, step.n)
            ins = nc.vector.tensor_scalar(row, row, cols[:, 2:3], None, ALU.mult)
            if c["new"]:
                ins.then_inc(step.up(), 1)
                dve.wait_ge(step.sem, step.n)
                for t in range(nt):
                    ins = nc.vector.tensor_scalar(m["diag"][0:HP, t * HP:(t + 1) * HP], ident[0:HP, 0:HP],
                                                  row[:, nt * P + t:nt * P + t + 1], None, ALU.mult)
            ins.then_inc(sig("sample_probs").up(), 1)

        def sample_out_dve(dve, name, finish):
            dve.wait_ge(sig("sample_out_done").sem, SMP[name]["order"] + 1)
            finish(PS[:, 7, 0:HP])

        def samples_act(act, name):
            c = SMP[name]
            m, nt = c["m"], c["nt"]
            nr = nt * P + (nt if c["new"] else 0)
            row, cols = m["row"][0:HP, 0:nr], m["cols"][0:HP, :]
            act.wait_ge(job_done.sem, done(f"ss{name}"))
            nc.scalar.activation(row, PS[0:HP, slot_of(f"ss{name}"), 0:nr], ACT.Copy).then_inc(job_read["act"].up(), 1)
            act.wait_ge(sig("sample_max").sem, c["order"] + 1)
            nc.scalar.activation(row, row, ACT.Exp, bias=cols[:, 0:1], scale=SCALE,
                                 accum_out=cols[:, 1:2]).then_inc(sig("sample_exp").up(), 1)

        def samples_turned_act(act, name):
            c = SMP[name]
            m, nt = c["m"], c["nt"]
            act.wait_ge(job_done.sem, done(f"sp{name}"))
            n = nt * HP * (2 if c["new"] else 1)
            nc.scalar.activation(m["turned"][:, 0:n], PS[:, slot_of(f"sp{name}"), 0:n],
                                 ACT.Copy).then_inc(job_read["act"].up(), 1)

        def samples_pe(pe, name):
            c = SMP[name]
            m, nt = c["m"], c["nt"]
            pe.wait_ge(*slot_free(f"ss{name}"))
            s = slot_of(f"ss{name}")
            pe.wait_ge(sig("key_sums").sem, c["base"] + nt * NS)
            for t in range(nt):
                last = nc.tensor.transpose(PS[0:HP, s, t * P:(t + 1) * P], m["scores"][:, t * HP:(t + 1) * HP], ident)
            if c["new"]:
                pe.wait_ge(sig("new_products").sem, 1)
                for t in range(nt):
                    last = nc.tensor.matmul(PS[0:HP, s, nt * P + t:nt * P + t + 1],
                                            m["qk"][:, t * HP:(t + 1) * HP], ones[:, 0:1], start=True, stop=True)
            last.then_inc(job_done.up(), 1)

        def samples_turned_pe(pe, name):
            c = SMP[name]
            m, nt = c["m"], c["nt"]
            pe.wait_ge(*slot_free(f"sp{name}"))
            s = slot_of(f"sp{name}")
            pe.wait_ge(sig("sample_probs").sem, c["order"] + 1)
            for t in range(nt):
                last = nc.tensor.transpose(PS[:, s, t * HP:(t + 1) * HP], m["row"][0:HP, t * P:(t + 1) * P],
                                           ident[0:HP, 0:HP])
            if c["new"]:
                last = nc.tensor.matmul(PS[:, s, nt * HP:2 * nt * HP], ones[0:HP, :], m["diag"][0:HP, :],
                                        start=True, stop=True)
            last.then_inc(job_done.up(), 1)

        def sample_values_pe(pe, name, n):
            c = SMP[name]
            nt = c["nt"]
            n_u = nt * NS
            if n == 0:
                pe.wait_ge(*read_of(f"sp{name}"))
            b, t = n // nt, n % nt
            sem, v, buf = tile_count(c, n_u + n)
            pe.wait_ge(sem.sem, v)
            for h in range(H):
                at = t * HP + h * NS + b
                last = nc.tensor.matmul(PS[:, 7, h * NS + b:h * NS + b + 1], c["tiles"][buf][:, h * P:(h + 1) * P],
                                        c["m"]["turned"][:, at:at + 1], start=(n == 0 and h == 0), stop=True,
                                        skip_group_check=True)
            last.then_inc((sig("values_used") if n < n_u - 1 else sig("sample_out_done")).up(), 1)

        def query_rows_pe(pe, name, srcs):
            pe.wait_ge(*slot_free(name))
            s = slot_of(name)
            for i, src in enumerate(srcs):
                last = nc.tensor.transpose(PS[0:HP, s + i // 4, (i % 4) * P:(i % 4 + 1) * P], src, ident)
            last.then_inc(job_done.up(), 1)

        MKV = WK[:, 0:2048].rearrange("p (t n) -> p t n", t=2)
        MKT = WK[:, 2 * WT:2 * WT + D]
        STAT = WK[:, 7 * WT:7 * WT + 128]

        def cols4(tile0, stride, lo, hi):
            return BIG[:, :].rearrange("p (i w) -> p i w", w=W)[:, tile0:tile0 + 3 * stride + 1:stride, lo:hi]

        def memory_attention(name, base, q0, q_stride, z0, z_stride):
            def out(i, ps):
                c = slice(i * P, (i + 1) * P)
                return nc.vector.tensor_tensor(cols4(q0, q_stride, c.start, c.stop), ps,
                                               cols4(z0, z_stride, c.start, c.stop), ALU.mult)
            attention(name, base,
                      q=lambda h, i: big(q0 + h * q_stride, i * P, (i + 1) * P),
                      k=lambda h, i: MKT[:, h * NMEM:(h + 1) * NMEM],
                      nk=lambda i: NMEM, mask=None,
                      v=lambda h, t, i: MKV[:, t, 512 + h * P:512 + (h + 1) * P],
                      out=out, p=lambda u: wk(3 + u % 2, 0, D), pt=lambda u: wk(5 + u % 2, 0, D),
                      stat=(STAT[:, 0:32], STAT[:, 32:64], STAT[:, 64:96]))

        memory_attention("memA", 0, 2, 6, 3, 6)
        memory_attention("memB", 32, 16, 1, 20, 1)

        def memory_samples(name, l, base, order, first_load, tiles, other, q_row, free):
            kv = a["cache_mem_kv"][l].rearrange("b (t p) x h d -> b t p x (h d)", p=P)
            samples(name, 2, base, key=lambda b, t: kv[b, t, :, 0, :], value=lambda b, t: kv[b, t, :, 1, :],
                    query=lambda b, t: qs_d[q_row].rearrange("(h b) d -> b h d", b=NS)[b],
                    tiles=[BIG[:, tiles * W + 512 * n:tiles * W + 512 * (n + 1)] for n in range(4)],
                    queries=[BIG[:, other * W + 512 * n:other * W + 512 * (n + 1)] for n in range(2)],
                    prods=[BIG[:, other * W + 512 * (n + 2):other * W + 512 * (n + 3)] for n in range(2)],
                    misc=TRIG[:, 0:1024], free=free)
            SMP[name].update(order=order, first_load=first_load)

        QROWS = [TRIG[0:HP, 1100:1100 + P]] * 2

        def memory_jobs(x, l, q_tile, z_tile, w0):
            def pe_part(pe, after_qm=lambda h: None, before=lambda name: None):
                for h in range(H):
                    pe_proj(pe, f"qm{x}{h}", ht, before=before(f"qm{h}"))
                    after_qm(h)
                for h in range(H):
                    pe_proj(pe, f"zm{x}{h}", ht, before=before(f"zm{h}"))
                    if h == 0:
                        pe.wait_ge(sig("query_cols").sem, l + 1)
                        query_rows_pe(pe, f"qs{x}", [HSS])
                samples_pe(pe, x)
                pe.wait_ge(*slot_free(f"mk{x}"))
                s = slot_of(f"mk{x}")
                pe.wait_ge(sig("memory_loaded").sem, 16 * (l + 1))
                for h in range(H):
                    for t in range(2):
                        at = (h % 2) * NMEM + t * P
                        last = nc.tensor.transpose(PS[:, s + h // 2, at:at + P], MKV[:, t, h * P:(h + 1) * P], ident)
                last.then_inc(job_done.up(), 1)
                samples_turned_pe(pe, x)
                pe.wait_ge(*read_of(f"mk{x}"))
                pe.wait_ge(*read_of(f"sp{x}"))

            def act_part(act, after_qm=lambda h: None):
                for h in range(H):
                    act.wait_ge(job_done.sem, done(f"qm{x}{h}"))
                    nc.scalar.activation(seg3(big(q_tile(h))), slot3(f"qm{x}{h}"), ACT.Copy).then_inc(job_read["act"].up(), 1)
                    load_ahead(act, f"qm{x}{h}")
                    after_qm(h)
                act.wait_ge(*read_of(f"qm{x}3"))
                stride = q_tile(1) - q_tile(0)
                nc.scalar.activation(HSS.rearrange("p (h b) -> p h b", h=H),
                                     cols4(q_tile(0), stride, T, W), ACT.Copy).then_inc(sig("query_cols").up(), 1)
                for h in range(H):
                    act.wait_ge(job_done.sem, done(f"zm{x}{h}"))
                    nc.scalar.activation(seg3(big(z_tile(h))), slot3(f"zm{x}{h}"), ACT.Silu).then_inc(job_read["act"].up(), 1)
                    load_ahead(act, f"zm{x}{h}")
                    if h == 0:
                        act.wait_ge(job_done.sem, done(f"qs{x}"))
                        rows = QROWS[l]
                        nc.scalar.activation(rows, PS[0:HP, slot_of(f"qs{x}"), 0:P],
                                             ACT.Copy).then_inc(job_read["act"].up(), 1)
                        act.wait_ge(*read_of(f"qs{x}"))
                        act.dma_start(qs_d[l], rows).then_inc(sig("query_rows_saved").sem, 16)
                samples_act(act, x)
                act.wait_ge(job_done.sem, done(f"mk{x}"))
                s = slot_of(f"mk{x}")
                nc.scalar.activation(MKT.rearrange("p (b n) -> p b n", b=2), PS[:, s:s + 2, :],
                                     ACT.Copy).then_inc(job_read["act"].up(), 1)
                samples_turned_act(act, x)
            return pe_part, act_part

        def free_a(sp):
            sp.wait_ge(sig("query_rows_saved").sem, 16)
            sp.wait_ge(sig("y_ready").sem, 4)

        memory_samples("A", 0, 0, 0, 0, 4, 10, 0, free_a)
        memA_pe, memA_act = memory_jobs("A", 0, lambda h: h * 6 + 2, lambda h: h * 6 + 3, 0)

        def sample_memory_out(q_tile, z_tile, stride_q, stride_z, reader):
            def finish(ps):
                nc.vector.tensor_tensor(
                    cols4(q_tile, stride_q, T, W), ps.rearrange("p (h b) -> p h b", h=H),
                    cols4(z_tile, stride_z, T, W), ALU.mult).then_inc(sig("sample_out_read").up(), 1)
            return finish

        def load_memory_kv(sp, l):
            sp.dma_start(MKV, o["memkv_p"][l, 0].rearrange("(t p) x h d -> p t (x h d)", p=P))\
                .then_inc(sig("memory_loaded").sem, 16)

        def stage4_sp(sp):
            sp.wait_ge(sig("y_ready").sem, 4)
            sp.wait_ge(sig("memkv_saved").sem, 64)
            load_memory_kv(sp, 0)
            samples_sp(sp, "A")

        def stage4_pool(pool):
            samples_pool(pool, "A", range(2 * NS))

        def stage4_pe(pe):
            memA_pe(pe)
            attend_pe(pe, "memA")

        def stage4_act(act):
            act.wait_ge(job_done.sem, done("var3"))
            memA_act(act)
            attend_act(act, "memA")

        def stage4_dve(dve):
            samples_scores_dve(dve, "A", range(2 * NS))
            samples_dve(dve, "A")
            dve.wait_ge(*read_of("zmA3"))
            attend_dve(dve, "memA")
            sample_out_dve(dve, "A", sample_memory_out(2, 3, 6, 6, "A"))

        def xt5(kt, lo=0, hi=W):
            return big((kt // 2) * 6 + 4 + kt % 2, lo, hi)

        def out_products(pe, name, src, kt, kts):
            w, s = ring(name), slot_of(name)
            for b in range(3):
                last = nc.tensor.matmul(PS[:, s + b, 0:SEG], w[:, kt * P:(kt + 1) * P],
                                        src(kt, b * SEG, (b + 1) * SEG), start=(kt == 0), stop=(kt == kts - 1))
            return last

        def out_pe(pe, x, src, kts):
            early = kts - H
            units = iter(range(2 * NS))
            for n in range(2):
                pe.wait_ge(*slot_free(f"out{x}{n}"))
                pe.wait_ge(*weights_of(f"out{x}{n}"))
                for kt in range(early):
                    out_products(pe, f"out{x}{n}", src, kt, kts)
                    for _ in range(NS // early):
                        sample_values_pe(pe, x, next(units))
            pe.wait_ge(sig("sample_out_read").sem, SMP[x]["order"] + 1)
            for n in range(2):
                for kt in range(early, kts):
                    last = out_products(pe, f"out{x}{n}", src, kt, kts)
                last.then_inc(job_done.up(), 1)
            for n in range(2, KT):
                pe_proj(pe, f"out{x}{n}", src, kts=kts)
            name = f"post{x}"
            pe.wait_ge(*slot_free(name))
            pe.wait_ge(sig(f"squares_added_{x}").sem, KT - 1)
            for b in range(3):
                last = nc.tensor.matmul(PS[:, slot_of(name) + b, 0:SEG], avg_d, wk(7, b * SEG, (b + 1) * SEG),
                                        start=True, stop=True)
            last.then_inc(job_done.up(), 1)

        def square_tile(n):
            return wk(7) if n == 0 else wk(5 + n % 2)

        def out_act(act, x, l):
            for n in range(KT):
                act.wait_ge(job_done.sem, done(f"out{x}{n}"))
                if n >= 3:
                    act.wait_ge(sig(f"squares_added_{x}").sem, n - 2)
                nc.scalar.activation(seg3(square_tile(n)), slot3(f"out{x}{n}"),
                                     ACT.Square).then_inc(sig(f"squared_{x}").up(), 1)
                nc.scalar.activation(seg3(ht(n)), slot3(f"out{x}{n}"), ACT.Copy,
                                     scale=vec(ROW_GPOST + l, n)).then_inc(job_read["act"].up(), 1)
            root_act(act, f"post{x}")

        def add_squares(dve, x):
            own = sig(f"squares_added_{x}")
            for n in range(1, KT):
                dve.wait_ge(sig(f"squared_{x}").sem, n + 1)
                if n > 1:
                    dve.wait_ge(own.sem, n - 1)
                nc.vector.tensor_tensor(wk(7), wk(7), square_tile(n), ALU.add).then_inc(own.up(), 1)

        DVE_TILES, POOL_TILES = range(5), range(5, KT)

        def residual(eng, ops, x, order, tiles, xt, turned, done, parts=((0, W),)):
            eng.wait_ge(sig("inverse_root").sem, order)
            eng.wait_ge(sig(f"x{x}_reloaded").sem, 16 * KT)
            for lo, hi in parts:
                for kt in tiles:
                    ops.tensor_tensor(ht(kt, lo, hi), ht(kt, lo, hi), wk(7, lo, hi), ALU.mult).then_inc(turned.up(), 1)
                    eng.wait_ge(turned.sem, turned.n)
                    ops.tensor_tensor(xt(kt, lo, hi), ht(kt, lo, hi), xt(kt, lo, hi), ALU.add).then_inc(done.up(), 1)

        def ya_src(kt, lo, hi):
            return big((kt // 2) * 6 + kt % 2, lo, hi) if kt < KT else big((kt - KT) * 6 + 2, lo, hi)

        def stage5_sp(sp):
            for n in range(3, KT):
                load_item(sp, f"outA{n}")
            sp.wait_ge(sig("sample_out_done").sem, 1)
            for kt in range(KT):
                sp.dma_start(xt5(kt), xt_d[kt]).then_inc(sig("xA_reloaded").sem, 16)

        def stage5_pe(pe):
            out_pe(pe, "A", ya_src, 12)
            norm_pe(pe, "normB")

        def x1_ready(eng, kt):
            if kt in DVE_TILES:
                eng.wait_ge(sig("x1_ready").sem, kt + 1)
            else:
                eng.wait_ge(sig("x1_ready_pool").sem, kt - POOL_TILES[0] + 1)

        def hb_ready(eng, kt):
            if kt in DVE_TILES:
                eng.wait_ge(sig("hb_ready").sem, kt + 1)
            else:
                eng.wait_ge(sig("hb_ready_pool").sem, kt - POOL_TILES[0] + 1)

        def stage5_act(act):
            out_act(act, "A", 0)
            norm_act(act, "normB", xt5, order=(0, 5, 1, 2, 6, 3, 4, 7), src_ready=lambda kt: x1_ready(act, kt))
            for kt in range(KT):
                act.dma_start(xt_d[kt], xt5(kt)).then_inc(sig("x1_saved").up(16), 16)

        def stage5_pool(pool):
            residual(pool, nc.gpsimd, "A", 2, POOL_TILES, xt5, sig("pool_steps"), sig("x1_ready_pool"))
            for n in ("k00", "k01", "k02"):
                scale_item(pool, n)
            pool.wait_ge(sig("inverse_root").sem, 3)
            for kt in POOL_TILES:
                nc.gpsimd.tensor_tensor(ht(kt), xt5(kt), wk(7), ALU.mult).then_inc(sig("hb_ready_pool").up(), 1)

        def stage5_dve(dve):
            add_squares(dve, "A")
            residual(dve, nc.vector, "A", 2, DVE_TILES, xt5, step, sig("x1_ready"))
            dve.wait_ge(sig("inverse_root").sem, 3)
            for kt in DVE_TILES:
                nc.vector.tensor_tensor(ht(kt), xt5(kt), wk(7), ALU.mult).then_inc(sig("hb_ready").up(), 1)

        COS, SIN = TRIG[:, 0:W], TRIG[:, W:2 * W]
        VN = WK[:, 4096:8192].rearrange("p (i n) -> p i n", i=8)
        GSTAT = WK[:, 8192:8320]
        KN = [big(20, 0, 512), big(21, 0, 512)]
        OWN = [7], [1, 3, 5, 7], list(range(8))

        def perm(ap, d):
            return ap.rearrange("p (r j) -> p j r", r=d)

        def natural(ap, d):
            return ap.rearrange("p (j r) -> p j r", r=d)

        def k_tile(h):
            return 12 + h

        def v_tile(h):
            return 16 + h

        def group_attention(g):
            def nk(i):
                return 2 * P if (g == 0 and i > 0) or (g == 1 and i % 2 == 1) else P

            def mask(i):
                if g == 2:
                    return BFC[:, M_PAIR:M_PAIR + 2 * P]
                both = BFC[:, M_BAND:M_BAND + 4 * P]
                return both if nk(i) == 2 * P else both.rearrange("p (x n) -> p x n", x=2)[:, :, P:2 * P]

            def out(i, ps):
                at = g * 4
                dst = BIG[:, :].rearrange("p (i w) -> p i w", w=W)[:, at:at + 4, i * P:(i + 1) * P]
                return nc.vector.tensor_copy(dst, ps)

            attention(f"win{g}", 8 + 8 * g,
                      q=lambda h, i: big(4 * g + h, i * P, (i + 1) * P),
                      k=lambda h, i: big(k_tile(h), (i + 1) * P - nk(i), (i + 1) * P), nk=nk, mask=mask,
                      v=lambda h, t, i: VN[:, i + 1 - nk(i) // P + t, h * P:(h + 1) * P],
                      out=out, p=lambda u: WK[:, (u % 2) * D:(u % 2 + 1) * D],
                      pt=lambda u: WK[:, (2 + u % 2) * D:(3 + u % 2) * D],
                      stat=(GSTAT[:, 0:32], GSTAT[:, 32:64], GSTAT[:, 96:128]))

        for g in range(3):
            group_attention(g)

        def group_names(g):
            return [f"k{g}{h}" for h in range(H)] + [f"v{g}{h}" for h in range(H)] + [f"q{g}{h}" for h in range(H)]

        def kn_stored(g, kn):
            n = 0
            for gg in range(g + 1):
                parts = 2 if gg == 2 else 1
                n += sum(2 * parts for x in range(len(OWN[gg])) if x % 2 == kn % 2 and (gg < g or x <= kn))
            return sig(f"window_rows{kn % 2}_stored").sem, 16 * n

        def last_two(g):
            return range(max(0, len(OWN[g]) - 2), len(OWN[g]))

        def store_rows(sp, g):
            for kn, i in enumerate(OWN[g]):
                parts = 2 if g == 2 else 1
                n = P // parts
                sp.wait_ge(sig("rows_copied").sem, 8 * g + i + 1)
                for x, src in ((0, KN[kn % 2]), (1, VN[:, i, :])):
                    for part in range(parts):
                        sp.dma_start(window_rows(g, i, x, part), src[part * n:(part + 1) * n, :])\
                            .then_inc(sig(f"window_rows{kn % 2}_stored").sem, 16)

        def stage6_sp(sp):
            for n in group_names(0)[:3]:
                load_item(sp, n)
            sp.wait_ge(sig("nm_saved").sem, 16 * 8)
            sp.wait_ge(sig("sample_out_read").sem, 1)
            sp.dma_start(TRIG[:, :], a["c_trig"]).then_inc(sig("layer_b_constants").sem, 16)
            sp.dma_start(MASKF, a["c_masks"]).then_inc(sig("layer_b_constants").sem, 16)
            for g in range(3):
                nxt = group_names(g + 1) if g < 2 else [f"zgB{h}" for h in range(H)]
                for n in group_names(g)[3:] + nxt[:3]:
                    load_item(sp, n)
                store_rows(sp, g)

        def stage6_pool(pool):
            pool.wait_ge(sig("layer_b_constants").sem, 32)
            nc.gpsimd.tensor_copy(BFC, MASKF).then_inc(sig("masks_cast").up(), 1)
            pool.wait_ge(sig("x1_saved").sem, 16 * KT)
            for g, d in enumerate(STRIDES):
                nxt = group_names(g + 1) if g < 2 else [f"zgB{h}" for h in range(H)]
                ahead = group_names(g)[3:] + nxt[:3]
                for x in range(3):
                    for h in range(H):
                        move(pool, g, d, x, h)
                        scale_item(pool, ahead[x * H + h])

        def move(pool, g, d, x, h):
            n = g * 8 + (h if x == 0 else H + h)
            if x == 1:
                pool.wait_ge(*read_of(f"v{g}{h}"))
                dst, src = big(v_tile(h)), big(20 + h)
                nc.gpsimd.tensor_copy(KVS[:, g, 1, h * NS:(h + 1) * NS], src[:, T:W])
                nc.gpsimd.tensor_copy(perm(dst[:, 0:T], d), natural(src[:, 0:T], d)).then_inc(sig("values_moved").up(), 1)
                return
            tmp = 20 + 2 * (n % 2)
            pool.wait_ge(*read_of(f"{'kvq'[x]}{g}{h}"))
            dst = big(k_tile(h)) if x == 0 else big(4 * g + h)
            tail = KVS[:, g, 0, h * NS:(h + 1) * NS] if x == 0 else dst[:, T:W]
            nc.gpsimd.tensor_tensor(tail, big(tmp, T, W), big(tmp + 1, T, W), ALU.add)
            if x == 0 and g > 0:
                pool.wait_ge(sig("out_read").sem, 8 + 8 * g)
            nc.gpsimd.tensor_tensor(perm(dst[:, 0:T], d), natural(big(tmp, 0, T), d),
                                    natural(big(tmp + 1, 0, T), d), ALU.add).then_inc(sig("rotated").up(), 1)

        def rotate(dve, g, x, h):
            name = f"{'kvq'[x]}{g}{h}"
            n = g * 8 + (h if x == 0 else H + h)
            tmp = 20 + 2 * (n % 2)
            if n >= 2:
                dve.wait_ge(sig("rotated").sem, n - 1)
            if x == 2 and h < 2:
                dve.wait_ge(sig("values_moved").sem, g * 4 + 4)
            if x == 0 and h == 0 and g > 0:
                for kn in last_two(g - 1):
                    dve.wait_ge(*kn_stored(g - 1, kn))
                dve.wait_ge(sig("lse_saved").sem, 16 * g)
            dve.wait_ge(job_done.sem, done(name))
            s = slot_of(name)
            nc.vector.tensor_tensor(seg3(big(tmp)), slot3(name), seg3(COS), ALU.mult)
            last = None
            for lo, hi in ((0, 64), (64, 0)):
                last = nc.vector.tensor_tensor(seg3(big(tmp + 1))[hi:hi + 64], PS[lo:lo + 64, s:s + 3, 0:SEG],
                                               seg3(SIN)[lo:lo + 64], ALU.mult)
            last.then_inc(job_read["dve"].up(), 1)

        def stage6_dve(dve):
            dve.wait_ge(sig("layer_b_constants").sem, 32)
            dve.wait_ge(sig("x1_saved").sem, 16 * KT)
            for g in range(3):
                for x in (0, 2):
                    for h in range(H):
                        rotate(dve, g, x, h)
                attend_dve(dve, f"win{g}")
                dve.wait_ge(sig("log_sums").sem, g + 1)
                nc.vector.tensor_tensor(GSTAT[:, 64:96], GSTAT[:, 64:96], GSTAT[:, 0:32],
                                        ALU.subtract).then_inc(sig("lse_ready").up(), 1)

        def stage6_pe(pe):
            for g in range(3):
                for n in group_names(g):
                    pe_proj(pe, n, ht, before=(lambda kt: hb_ready(pe, kt)) if n == "k00" else None)
                pe.wait_ge(*read_of(f"q{g}3"))
                for i in range(8):
                    u = 8 * g + i
                    if i == 0:
                        pe.wait_ge(sig("values_moved").sem, 4 * g + 4)
                        pe.wait_ge(sig("rotated").sem, 8 * g + 4)
                    if i >= 2:
                        pe.wait_ge(sig("rows_copied").sem, u - 1)
                    b = 2 * (i % 2)
                    for h in range(H):
                        last = nc.tensor.transpose(PS[:, b, h * P:(h + 1) * P], big(v_tile(h), i * P, (i + 1) * P),
                                                   ident)
                    if i in OWN[g]:
                        for h in range(H):
                            last = nc.tensor.transpose(PS[:, b + 1, h * P:(h + 1) * P],
                                                       big(k_tile(h), i * P, (i + 1) * P), ident)
                    last.then_inc(sig("rows_turned").up(), 1)
                pe.wait_ge(sig("rows_copied").sem, 8 * g + 8)
                if g == 0:
                    pe.wait_ge(sig("masks_cast").sem, 1)
                pe.wait_ge(sig("rotated").sem, 8 * g + 8)
                attend_pe(pe, f"win{g}")
                pe.wait_ge(*slot_free(f"lse{g}"))
                pe.wait_ge(sig("lse_ready").sem, g + 1)
                nc.tensor.transpose(PS[0:HP, slot_of(f"lse{g}"), 0:P], GSTAT[:, 64:96], ident).then_inc(job_done.up(), 1)

        def window_rows(g, i, x, part):
            w = o[f"win{g}_p"][0].rearrange("(j r) x h d -> x r j (h d)", r=STRIDES[g])[x]
            if g == 0:
                return w[0]
            if g == 1:
                return w[i // 2]
            return w[2 * i + part]

        def stage6_act(act):
            def evac_v(g, h):
                act.wait_ge(job_done.sem, done(f"v{g}{h}"))
                if h == 0:
                    act.wait_ge(sig("rotated").sem, 8 * g + 4)
                nc.scalar.activation(seg3(big(20 + h)), slot3(f"v{g}{h}"), ACT.Copy).then_inc(job_read["act"].up(), 1)

            for g in range(3):
                for h in range(H):
                    evac_v(g, h)
                for i in range(8):
                    act.wait_ge(sig("rows_turned").sem, 8 * g + i + 1)
                    b = 2 * (i % 2)
                    ins = nc.scalar.activation(VN[:, i, :], PS[:, b, :], ACT.Copy)
                    if i in OWN[g]:
                        kn = OWN[g].index(i)
                        if kn == 0:
                            act.wait_ge(sig("rotated").sem, 8 * g + 8)
                        elif kn >= 2:
                            act.wait_ge(*kn_stored(g, kn - 2))
                        ins = nc.scalar.activation(KN[kn % 2], PS[:, b + 1, :], ACT.Copy)
                    ins.then_inc(sig("rows_copied").up(), 1)
                attend_act(act, f"win{g}")
                nc.scalar.activation(GSTAT[:, 64:96], GSTAT[:, 32:64], ACT.Ln).then_inc(sig("log_sums").up(), 1)
                rows = big(23, 0, P)[0:HP, :]
                act.wait_ge(job_done.sem, done(f"lse{g}"))
                nc.scalar.activation(rows, PS[0:HP, slot_of(f"lse{g}"), 0:P], ACT.Copy).then_inc(job_read["act"].up(), 1)
                act.wait_ge(*read_of(f"lse{g}"))
                act.dma_start(ls_d[g].rearrange("i h t -> (i h) t"), rows).then_inc(sig("lse_saved").sem, 16)
                for kn in last_two(g):
                    act.wait_ge(*kn_stored(g, kn))
                act.wait_ge(sig("lse_saved").sem, 16 * (g + 1))

        def lrow(i, lo=0, hi=T):
            return WK[0:H, i * WT + lo:i * WT + hi]

        SQB = XTRA[:, 1600:1696].rearrange("p (g n) -> p g n", g=3)
        RQ = WK[32:64, 0:9 * P]
        wins = [a[f"cache_win{g}"].rearrange("b (r d) x h e -> b r d x (h e)", d=STRIDES[g])[:, :, 0]
                for g in range(3)]

        def free_d(sp):
            sp.wait_ge(sig("query_rows_saved_d").sem, 48)
            sp.wait_ge(sig("rotated").sem, 24)

        samples("D", 3, 16, key=lambda b, t: wins[t][b, :, 0, :], value=lambda b, t: wins[t][b, :, 1, :],
                query=lambda b, t: qs_d[2 + t].rearrange("(h b) d -> b h d", b=NS)[b],
                tiles=[TRIG[:, 512 * n:512 * (n + 1)] for n in range(4)],
                queries=[WK[:, 6 * WT + 512 * n:6 * WT + 512 * (n + 1)] for n in range(2)],
                prods=[WK[:, 7 * WT + 512 * n:7 * WT + 512 * (n + 1)] for n in range(2)],
                misc=XTRA[:, 1696:3072], free=free_d,
                new=(lambda t: cols4(4 * t, 1, T, W), lambda t: KVS[:, t, 0, :], lambda t: KVS[:, t, 1, :]))
        SMP["D"].update(order=1, first_load=32)

        def free_b(sp):
            sp.wait_ge(sig("query_rows_saved").sem, 32)

        memory_samples("B", 1, 40, 2, 80, 4, 6, 1, free_b)
        memB_pe, memB_act = memory_jobs("B", 1, lambda h: 16 + h, lambda h: 20 + h, 0)

        HALVES = (0, 4 * P), (4 * P, W)

        def xt7(kt, lo=0, hi=W):
            return big(8 + kt, lo, hi)

        def stage7_sp(sp):
            for g in range(3):
                sp.wait_ge(sig("lse_saved").sem, 16 * 3)
                sp.dma_start(lrow(g).rearrange("h (i t) -> h i t", i=8), ls_d[g].rearrange("i h t -> h i t"))\
                    .then_inc(sig("lse_loaded").sem, 16)
            samples_sp(sp, "D")
            sp.wait_ge(*read_of("wb3_2"))
            load_memory_kv(sp, 1)
            samples_sp(sp, "B")
            for n in range(3, KT):
                load_item(sp, f"outB{n}")
            sp.wait_ge(sig("yd_ready").sem, 1)
            sp.wait_ge(sig("sample_out_done").sem, 3)
            for kt in range(KT):
                sp.dma_start(xt7(kt), xt_d[kt]).then_inc(sig("xB_reloaded").sem, 16)

        def stage7_pool(pool):
            for n, name in ((range(4), "zgB3"), (range(4, 8), "qmB0")):
                samples_pool(pool, "D", n)
                scale_item(pool, name)
            scale_item(pool, "qmB1")
            samples_pool(pool, "D", range(8, 3 * NS))
            for n in ("qmB2", "qmB3", "zmB0", "zmB1"):
                scale_item(pool, n)
            samples_pool(pool, "B", range(4))
            scale_item(pool, "zmB2")
            samples_pool(pool, "B", range(4, 9))
            scale_item(pool, "zmB3")
            samples_pool(pool, "B", range(9, 2 * NS))
            residual(pool, nc.gpsimd, "B", 4, POOL_TILES, xt7, sig("pool_steps"), sig("y_ready_pool"), HALVES)

        def stage7_pe(pe):
            pe.wait_ge(sig("pair_query_cols").sem, 1)
            query_rows_pe(pe, "qsD", [SQB[:, g, :] for g in range(3)] + [KVS[:, g, x, :] for g in range(3)
                                                                       for x in range(2)])
            for h in range(H):
                pe_proj(pe, f"zgB{h}", ht)
            for h in range(H):
                for g in range(3):
                    name = f"wb{h}_{g}"
                    pe.wait_ge(*slot_free(name))
                    if h == 0 and g == 0:
                        pe.wait_ge(sig("weights_ready").sem, 1)
                    s = slot_of(name)
                    for b in range(2):
                        last = nc.tensor.matmul(PS[:, s + b, :], CST[0:H, C_SEL + h * P:C_SEL + (h + 1) * P],
                                                lrow((0, 3, 4)[g], b * 512, (b + 1) * 512), start=True, stop=True)
                    last.then_inc(job_done.up(), 1)
            units = iter(range(3 * NS))

            def values_between(name):
                return (lambda kt: sample_values_pe(pe, "D", next(units))) if name in ("qm2", "qm3", "zm0") else None

            memB_pe(pe, lambda h: (samples_pe, samples_turned_pe)[h](pe, "D") if h < 2 else None, values_between)
            attend_pe(pe, "memB")
            pe.wait_ge(sig("yd_ready").sem, 1)
            out_pe(pe, "B", lambda kt, lo, hi: big(kt if kt < H else 12 + kt, lo, hi), KT)
            for t in range(9):
                name = f"yt{t}"
                pe.wait_ge(*slot_free(name))
                s = slot_of(name)
                if t in (0, 4):
                    pe.wait_ge(sig("y_ready_dve").sem, len(DVE_TILES) * (1 + t // 4))
                    pe.wait_ge(sig("y_ready_pool").sem, len(POOL_TILES) * (1 + t // 4))
                n = P if t < 8 else NS
                for kt in range(KT):
                    last = nc.tensor.transpose(PS[0:n, s + kt // 4, (kt % 4) * P:(kt % 4 + 1) * P],
                                               big(8 + kt, t * P, t * P + n), ident)
                last.then_inc(job_done.up(), 1)

        def stage7_act(act):
            nc.scalar.activation(
                SQB.rearrange("p g (h b) -> p (g h) b", h=H),
                BIG[:, :].rearrange("p (i w) -> p i w", w=W)[:, 0:12, T:W], ACT.Copy).then_inc(sig("pair_query_cols").up(), 1)
            act.wait_ge(job_done.sem, done("qsD"))
            s = slot_of("qsD")
            nc.scalar.activation(RQ[:, 0:8 * P].rearrange("p (b n) -> p b n", b=2), PS[0:HP, s:s + 2, :], ACT.Copy)
            nc.scalar.activation(RQ[:, 8 * P:9 * P], PS[0:HP, s + 2, 0:P], ACT.Copy).then_inc(job_read["act"].up(), 1)
            act.wait_ge(*read_of("qsD"))
            for g in range(3):
                act.dma_start(qs_d[2 + g], RQ[:, g * P:(g + 1) * P]).then_inc(sig("query_rows_saved_d").sem, 16)
            for g in range(3):
                for x in range(2):
                    at = (3 + 2 * g + x) * P
                    for h in range(H):
                        act.dma_start(o[f"win{g}_s"][:, 0, x, h, :], RQ[h * NS:(h + 1) * NS, at:at + P])\
                            .then_inc(sig("new_rows_saved").sem, 16)
            act.wait_ge(sig("lse_shifted").sem, 1)
            nc.scalar.activation(lrow(0), lrow(0), ACT.Exp).then_inc(sig("lse_exp").up(), 1)
            nc.scalar.activation(WK[0:H, 3 * WT:5 * WT].rearrange("h (i n) -> h i n", i=2)[:, :, 0:T],
                                 WK[0:H, 3 * WT:5 * WT].rearrange("h (i n) -> h i n", i=2)[:, :, 0:T],
                                 ACT.Exp).then_inc(sig("lse_exp").up(), 1)
            for h in range(H):
                act.wait_ge(job_done.sem, done(f"zgB{h}"))
                nc.scalar.activation(seg3(big(12 + h)), slot3(f"zgB{h}"), ACT.Silu).then_inc(job_read["act"].up(), 1)
                load_ahead(act, f"zgB{h}")
            memB_act(act, lambda h: (samples_act, samples_turned_act)[h](act, "D") if h < 2 else None)
            attend_act(act, "memB")
            out_act(act, "B", 1)
            yo = sig("y_rows_copied")
            for t in range(9):
                n = P if t < 8 else NS
                name = f"yt{t}"
                act.wait_ge(job_done.sem, done(name))
                if t >= 2:
                    act.wait_ge(sig(f"y{t % 2}_saved").sem, 16 * (t // 2))
                s = slot_of(name)
                row = WK[0:n, (t % 2) * WT:(t % 2) * WT + D]
                nc.scalar.activation(row.rearrange("p (b n) -> p b n", b=2),
                                     PS[0:n, s:s + 2, :], ACT.Copy).then_inc(job_read["act"].up(), 1)
                act.wait_ge(*read_of(name))
                dst = o["y_prompt"][0, t * P:(t + 1) * P, :] if t < 8 else o["y_sample"].rearrange("b t d -> (b t) d")
                act.dma_start(dst, row).then_inc(sig(f"y{t % 2}_saved").sem, 16)
            act.wait_ge(sig("y0_saved").sem, 16 * 5)
            act.wait_ge(sig("y1_saved").sem, 16 * 4)
            act.wait_ge(sig("new_rows_saved").sem, 16 * 24)
            for kn in last_two(2):
                act.wait_ge(*kn_stored(2, kn))

        def stage7_dve(dve):
            def do(ins):
                ins.then_inc(step.up(), 1)
                dve.wait_ge(step.sem, step.n)

            dve.wait_ge(sig("lse_loaded").sem, 16 * 3)
            dve.wait_ge(sig("new_rows_saved").sem, 16 * 24)
            dve.wait_ge(sig("query_rows_saved_d").sem, 48)
            l0 = lrow(0)

            def tok(i, d):
                return lrow(i).rearrange("h (r j) -> h j r", r=d)

            def nat(i, d):
                return lrow(i).rearrange("h (j r) -> h j r", r=d)

            mx = 5
            do(nc.vector.tensor_tensor(nat(mx, 4), nat(0, 4), tok(1, 4), ALU.max))
            do(nc.vector.tensor_tensor(nat(mx, 16), nat(mx, 16), tok(2, 16), ALU.max))
            nc.vector.tensor_tensor(lrow(0), lrow(0), lrow(mx), ALU.subtract)
            nc.vector.tensor_tensor(nat(3, 4), tok(1, 4), nat(mx, 4), ALU.subtract)
            nc.vector.tensor_tensor(nat(4, 16), tok(2, 16), nat(mx, 16), ALU.subtract).then_inc(sig("lse_shifted").up(), 1)
            dve.wait_ge(sig("lse_exp").sem, 2)
            do(nc.vector.tensor_tensor(lrow(1), lrow(0), lrow(3), ALU.add))
            do(nc.vector.tensor_tensor(lrow(1), lrow(1), lrow(4), ALU.add))
            do(nc.vector.reciprocal(lrow(1), lrow(1)))
            for i in (0, 3, 4):
                ins = nc.vector.tensor_tensor(lrow(i), lrow(i), lrow(1), ALU.mult)
            ins.then_inc(sig("weights_ready").up(), 1)
            samples_new_dve(dve, "D")
            samples_scores_dve(dve, "D", range(8))
            for h in range(H):
                for g, d in enumerate(STRIDES):
                    name = f"wb{h}_{g}"
                    dve.wait_ge(job_done.sem, done(name))
                    s = slot_of(name)
                    x = perm(big(4 * g + h, 0, T), d)
                    nc.vector.tensor_tensor(
                        x, x, natural(PS[:, s:s + 2, :].rearrange("p b n -> p (b n)"), d), ALU.mult).then_inc(job_read["dve"].up(), 1)
                dve.wait_ge(*read_of(f"wb{h}_2"))
                y = big(h, 0, T)
                for g, d in ((1, 4), (2, 16)):
                    do(nc.vector.tensor_tensor(natural(y, d), natural(y, d), perm(big(4 * g + h, 0, T), d), ALU.add))
                samples_scores_dve(dve, "D", range(8 + 4 * h, 12 + 4 * h))

            def windows_out(ps):
                m = SMP["D"]["m"]
                y = m["qk"][:, 0:HP]
                t = m["qk"][:, HP:2 * HP]
                nc.vector.tensor_copy(y, ps).then_inc(sig("sample_out_read").up(), 1)
                for g in range(3):
                    p_new = m["turned"][:, (3 + g) * HP:(4 + g) * HP]
                    if g == 0:
                        dve.wait_ge(sig("sample_out_read").sem, 2)
                    do(nc.vector.tensor_tensor(t, p_new, KVS[:, g, 1, :], ALU.mult))
                    do(nc.vector.tensor_tensor(y, y, t, ALU.add))
                do(nc.vector.tensor_copy(cols4(0, 1, T, W), y.rearrange("p (h b) -> p h b", h=H)))
                nc.vector.tensor_tensor(cols4(0, 1, T, W), cols4(0, 1, T, W), cols4(12, 1, T, W),
                                        ALU.mult).then_inc(sig("yd_ready").up(), 1)

            dve.wait_ge(*read_of("zgB3"))
            for h in range(H):
                nc.vector.tensor_tensor(big(h, 0, T), big(h, 0, T), big(12 + h, 0, T), ALU.mult)
            samples_dve(dve, "D")
            sample_out_dve(dve, "D", windows_out)
            samples_scores_dve(dve, "B", range(2 * NS))
            samples_dve(dve, "B")
            dve.wait_ge(*read_of("zmB3"))
            attend_dve(dve, "memB")
            sample_out_dve(dve, "B", sample_memory_out(16, 20, 1, 1, "B"))
            add_squares(dve, "B")
            residual(dve, nc.vector, "B", 4, DVE_TILES, xt7, step, sig("y_ready_dve"), HALVES)

        with nc.Block() as block:
            @block.sync
            def _(sp):
                stage0_sp(sp)
                stage1_sp(sp)
                gates_sp(sp)
                stage2_end_sp(sp)
                stage3_sp(sp)
                stage4_sp(sp)
                stage5_sp(sp)
                stage6_sp(sp)
                stage7_sp(sp)
                sp.wait_ge(sig("n_saved").sem, 16 * 9)
                sp.wait_ge(s_out.sem, 16)
                sp.wait_ge(sig("x1_saved").sem, 128)
                sp.wait_ge(sig("cs0_saved").sem, 256)
                sp.wait_ge(sig("cs1_saved").sem, 256)
                sp.wait_ge(sig("nm_saved").sem, 128)
                sp.wait_ge(sig("memkv_saved").sem, 64)
                sp.wait_ge(sig("conv_saved").sem, 32)

            @block.gpsimd
            def _(pool):
                stage0_pool(pool)
                stage3_pool(pool)
                stage4_pool(pool)
                stage5_pool(pool)
                stage6_pool(pool)
                stage7_pool(pool)

            @block.scalar
            def _(act):
                stage0_act(act)
                stage1_act(act)
                stage2_act(act)
                stage2_end_act(act)
                stage3_act(act)
                stage4_act(act)
                stage5_act(act)
                stage6_act(act)
                stage7_act(act)
                for b in range(2):
                    act.wait_ge(sig(f"c{b}_saved").sem, 32)

            @block.vector
            def _(dve):
                stage0_dve(dve)
                stage1_dve(dve)
                stage2_dve(dve)
                stage3_dve(dve)
                stage4_dve(dve)
                stage5_dve(dve)
                stage6_dve(dve)
                stage7_dve(dve)

            @block.tensor
            def _(pe):
                stage0_pe(pe)
                stage1_pe(pe)
                stage2_pe(pe)
                stage2_end_pe(pe)
                stage3_pe(pe)
                stage4_pe(pe)
                stage5_pe(pe)
                stage6_pe(pe)
                stage7_pe(pe)


_INS = ['x_prompt', 'x_sample', 'mem_prompt', 'state_conv', 'state_C', 'state_n', 'state_m', 'cache_win0',
        'cache_win1', 'cache_win2', 'cache_mem_kv', 'g_pre', 'g_post', 'w_in_a', 'conv_w_a', 'conv_b_a', 'w_q_a',
        'w_k_a', 'w_v_a', 'w_if_a', 'b_if_a', 'g_hn_a', 'skip_a', 'w_out_a', 'g_kv', 'w_kv_b', 'w_in_b',
        'w_out_b', 'w_mkv']
_OUTS = {'y_prompt': (1, 1024, 1024), 'y_sample': (8, 1, 1024), 'conv_p': (1, 1, 3, 1024),
         'C_p': (1, 1, 4, 256, 256), 'n_p': (1, 1, 4, 256), 'm_p': (1, 1, 4), 'win0_p': (1, 128, 2, 4, 128),
         'win1_p': (1, 512, 2, 4, 128), 'win2_p': (1, 1024, 2, 4, 128), 'memkv_p': (2, 1, 256, 2, 4, 128),
         'conv_s': (1, 8, 3, 1024), 'C_s': (1, 8, 4, 256, 256), 'n_s': (1, 8, 4, 256), 'm_s': (1, 8, 4),
         'win0_s': (8, 1, 2, 4, 128), 'win1_s': (8, 1, 2, 4, 128), 'win2_s': (8, 1, 2, 4, 128)}


def constants():
    import numpy as np
    c = np.zeros((P, C_END), np.float32)
    i, j = np.arange(P)[:, None], np.arange(P)[None, :]
    c[:, C_ID:C_ID + P] = i == j
    c[:, C_ONE:C_ONE + P] = 1.0
    c[:, C_AVG_D:C_AVG_D + P] = 1.0 / D
    c[:, C_AVG_H:C_AVG_H + P] = 1.0 / 256
    c[:, C_CAUSAL:C_CAUSAL + P] = i <= j
    prev = np.where(j >= i, 0.0, NEG)
    own = np.where(j <= i, 0.0, NEG)
    pair = np.where((j <= i) & (i // 64 == j // 64), 0.0, NEG)
    masks = np.concatenate([i == j, prev, own, prev, own, pair, pair], 1).astype(np.float32)
    for h in range(H):
        c[h, C_SEL + h * P:C_SEL + (h + 1) * P] = 1.0
    half = P // 2
    inv = (10000.0 ** (-np.arange(half) / half)).astype(np.float32)
    pos = np.concatenate([np.arange(T, dtype=np.float32), np.full(NS, 2048, np.float32)])
    ang = (inv[:, None] * pos[None, :]).astype(np.float32)
    cos, sin = np.cos(ang).astype(np.float32), np.sin(ang).astype(np.float32)
    trig = np.concatenate([np.concatenate([cos, cos], 0), np.concatenate([sin, -sin], 0)], 1)
    return {'c_block': c, 'c_masks': masks, 'c_trig': trig}


def kernel(**inputs):
    import numpy as _np
    import concourse.bacc as _bacc
    from concourse.bass_utils import run_bass_kernel_spmd as _run

    nc = _bacc.Bacc("TRN2", target_bir_lowering=False, num_devices=1)
    arrays, a, o = {}, {}, {}
    for name, value in [(n, _np.ascontiguousarray(inputs[n])) for n in _INS] + list(constants().items()):
        arrays[f"in_{name}"] = value
        a[name] = nc.dram_tensor(f"in_{name}", value.shape, mybir.dt.from_np(value.dtype), kind="ExternalInput").ap()
    for name, shape in _OUTS.items():
        o[name] = nc.dram_tensor(f"out_{name}", shape, F32, kind="ExternalOutput").ap()
    build(nc, a, o)
    r = _run(nc, [arrays], core_ids=[0])
    return tuple(r.results[0][f"out_{name}"] for name in _OUTS)
```
